# Optimizing a Trainium2 kernel written in Bass

```python
import jax, jax.numpy as jnp
from jax import lax
import numpy as np

D_MODEL = 1024
BATCH = 1
SEQ = 1024
DEPTH = 1
DEC_BATCH = 8
DEC_SEQ = 1
PAST_LEN = 256
PAGE_SIZE = 128

RET_HEADS = 4
RET_DK = 128
RET_DV = 256
RET_CHUNK = 128
RET_QK = RET_HEADS * RET_DK
RET_V = RET_HEADS * RET_DV
ATT_GROUPS = ((128, 1), (512, 4), (2048, 16))
N_GROUPS = 3
HEADS_PER_GROUP = 4
ATT_HEADS = N_GROUPS * HEADS_PER_GROUP
HEAD_DIM = 64
ATT_BLOCK = 128
ATT_W = ATT_HEADS * HEAD_DIM
ATT_OUT = HEADS_PER_GROUP * HEAD_DIM
D_FF = -(-8 * D_MODEL // (3 * 256)) * 256
COL_SIZES = (RET_QK, RET_QK, RET_V, RET_V, ATT_W, ATT_W, ATT_W, D_MODEL, D_MODEL)
D_IN = 2 * RET_QK + 2 * RET_V + 3 * ATT_W + 2 * D_MODEL
RMS_EPS = 1e-6
GN_EPS = 1e-5

kernel_name = 'retention_dilated_attn_hybrid_step'

def _rms_norm(x, g):
    x32 = x.astype(jnp.float32)
    y = x32 * lax.rsqrt(jnp.mean(x32 * x32, axis=-1, keepdims=True) + RMS_EPS)
    return (y * g.astype(jnp.float32)).astype(x.dtype)

def _log_gamma():
    return jnp.log1p(-jnp.exp2(-5.0 - jnp.arange(RET_HEADS, dtype=jnp.float32)))

def _alibi_slopes():
    return jnp.exp2(-8.0 * (jnp.arange(ATT_HEADS, dtype=jnp.float32) + 1.0) / ATT_HEADS)

def _retention_chunk(q, k, v, s0, log_gamma):
    c = q.shape[1]
    idx = jnp.arange(c, dtype=jnp.float32)
    diff = idx[:, None] - idx[None, :]
    decay = jnp.where(diff >= 0, jnp.exp(jnp.maximum(diff, 0.0)[None] * log_gamma[:, None, None]), 0.0)
    scores = jnp.einsum('nihd,njhd->nhij', q, k) * decay[None]
    intra = jnp.einsum('nhij,njhv->nihv', scores, v)
    inner = jnp.exp((idx + 1.0)[:, None] * log_gamma[None, :])
    cross = jnp.einsum('nihd,nhdv->nihv', q, s0) * inner[None, :, :, None]
    tail = jnp.exp((c - 1.0 - idx)[:, None] * log_gamma[None, :])
    s1 = s0 * jnp.exp(c * log_gamma)[None, :, None, None] + jnp.einsum(
        'njhd,njhv->nhdv', k * tail[None, :, :, None], v)
    return intra + cross, s1

def _retention(q, k, v, s0):
    n, t = q.shape[:2]
    chunk = RET_CHUNK if t % RET_CHUNK == 0 else t
    nc = t // chunk
    log_gamma = _log_gamma()

    def split(a):
        return a.reshape(n, nc, chunk, *a.shape[2:]).swapaxes(0, 1)

    def step(s, inp):
        o, s = _retention_chunk(inp[0], inp[1], inp[2], s, log_gamma)
        return s, o

    s_final, o = lax.scan(step, s0, (split(q), split(k), split(v)))
    o = o.swapaxes(0, 1).reshape(n, t, RET_HEADS, RET_DV)
    return o, s_final

def _dilated_group_prompt(q, k, v, slopes, window, dilation):
    b, t, h, dh = q.shape
    span = dilation * ATT_BLOCK
    tp = -(-t // span) * span
    lres = tp // dilation
    nb = lres // ATT_BLOCK

    def arrange(a):
        a = jnp.pad(a, ((0, 0), (0, tp - t), (0, 0), (0, 0)))
        a = a.reshape(b, lres, dilation, h, dh).swapaxes(1, 2)
        return a.reshape(b, dilation, nb, ATT_BLOCK, h, dh)

    def with_prev(a):
        prev = jnp.pad(a, ((0, 0), (0, 0), (1, 0), (0, 0), (0, 0), (0, 0)))[:, :, :-1]
        return jnp.concatenate([prev, a], axis=3)

    qb = arrange(q)
    kk = with_prev(arrange(k))
    vv = with_prev(arrange(v))
    steps = window // dilation
    qi = jnp.arange(ATT_BLOCK)[:, None]
    kj = jnp.arange(2 * ATT_BLOCK)[None, :]
    dist = qi + ATT_BLOCK - kj
    blk = jnp.arange(nb)[:, None, None]
    valid = ((dist >= 0) & (dist <= steps))[None] & ((blk > 0) | (kj >= ATT_BLOCK)[None])
    s = jnp.einsum('brnihd,brnjhd->brnhij', qb, kk) * (HEAD_DIM ** -0.5)
    s = s - slopes[:, None, None] * (dist * dilation).astype(jnp.float32)[None]
    s = jnp.where(valid[None, None, :, None], s, -jnp.inf)
    m = jnp.max(s, axis=-1, keepdims=True)
    p = jnp.exp(s - m)
    l = jnp.sum(p, axis=-1, keepdims=True)
    o = jnp.einsum('brnhij,brnjhd->brnihd', p / l, vv)
    lse = (m + jnp.log(l))[..., 0].swapaxes(3, 4)
    o = o.reshape(b, dilation, lres, h, dh).swapaxes(1, 2).reshape(b, tp, h, dh)[:, :t]
    lse = lse.reshape(b, dilation, lres, h).swapaxes(1, 2).reshape(b, tp, h)[:, :t]
    return o, lse

def _dilated_group_sample(q, k_new, v_new, kv_buf, slopes, window, dilation):
    wlen = kv_buf.shape[1]
    s_new = q.shape[1]
    buf = kv_buf.astype(jnp.float32)
    keys = jnp.concatenate([buf[:, :, 0], k_new], axis=1)
    vals = jnp.concatenate([buf[:, :, 1], v_new], axis=1)
    steps = window // dilation
    j = jnp.arange(steps + 1)
    idx = wlen + jnp.arange(s_new)[:, None] - dilation * j[None, :]
    valid = idx >= 0
    idx = jnp.clip(idx, 0)
    kg = jnp.take(keys, idx, axis=1)
    vg = jnp.take(vals, idx, axis=1)
    s = jnp.einsum('nshd,nsjhd->nshj', q, kg) * (HEAD_DIM ** -0.5)
    s = s - slopes[:, None] * (dilation * j).astype(jnp.float32)[None, :]
    s = jnp.where(valid[None, :, None, :], s, -jnp.inf)
    lse = jax.nn.logsumexp(s, axis=-1)
    p = jnp.exp(s - lse[..., None])
    o = jnp.einsum('nshj,nsjhd->nshd', p, vg)
    return o, lse

def _token_mix(hn, w_in, w_ret_branch, w_att_branch, w_out, ret_s0, kv_bufs):
    f32 = jnp.float32
    n, t = hn.shape[:2]
    proj = hn @ w_in
    rq, rk, rv, rg, aq, ak, av, gr, ga = jnp.split(proj, np.cumsum(COL_SIZES)[:-1].tolist(), axis=-1)
    rq = rq.reshape(n, t, RET_HEADS, RET_DK).astype(f32) * (RET_DK ** -0.5)
    rk = rk.reshape(n, t, RET_HEADS, RET_DK).astype(f32)
    rv = rv.reshape(n, t, RET_HEADS, RET_DV).astype(f32)
    ro, ret_s1 = _retention(rq, rk, rv, ret_s0)
    mu = jnp.mean(ro, axis=-1, keepdims=True)
    var = jnp.mean(jnp.square(ro - mu), axis=-1, keepdims=True)
    ro = (ro - mu) * lax.rsqrt(var + GN_EPS)
    ro = (ro.reshape(n, t, RET_V) * jax.nn.silu(rg.astype(f32))).astype(hn.dtype)
    r_branch = ro @ w_ret_branch
    aq = aq.reshape(n, t, N_GROUPS, HEADS_PER_GROUP, HEAD_DIM)
    ak = ak.reshape(n, t, N_GROUPS, HEADS_PER_GROUP, HEAD_DIM)
    av = av.reshape(n, t, N_GROUPS, HEADS_PER_GROUP, HEAD_DIM)
    slopes = _alibi_slopes().reshape(N_GROUPS, HEADS_PER_GROUP)
    outs, lses, new_kv = [], [], []
    for g, (win, dil) in enumerate(ATT_GROUPS):
        qg = aq[:, :, g].astype(f32)
        kg = ak[:, :, g].astype(f32)
        vg = av[:, :, g].astype(f32)
        if kv_bufs is None:
            o, lse = _dilated_group_prompt(qg, kg, vg, slopes[g], win, dil)
            keep = min(win, t)
            new_kv.append(jnp.stack([ak[:, t - keep:, g], av[:, t - keep:, g]], axis=2))
        else:
            o, lse = _dilated_group_sample(qg, kg, vg, kv_bufs[g], slopes[g], win, dil)
            new_kv.append(jnp.stack([ak[:, :, g], av[:, :, g]], axis=2))
        outs.append(o)
        lses.append(lse)
    wgt = jax.nn.softmax(jnp.stack(lses, axis=0), axis=0)
    ao = jnp.einsum('gnth,gnthd->nthd', wgt, jnp.stack(outs, axis=0))
    a_branch = ao.reshape(n, t, ATT_OUT).astype(hn.dtype) @ w_att_branch
    merged = jax.nn.sigmoid(gr) * r_branch + jax.nn.sigmoid(ga) * a_branch
    return merged @ w_out, ret_s1, new_kv

def _trunk(x, ret_states, kv_caches, norm_mix, w_in, w_ret_branch, w_att_branch, w_out,
           norm_ffn, w_gate_up, w_down, norm_final):
    n = x.shape[0]
    rets, kvs = [], []
    for l in range(DEPTH):
        if ret_states is None:
            s0 = jnp.zeros((n, RET_HEADS, RET_DK, RET_DV), jnp.float32)
            bufs = None
        else:
            s0 = ret_states[l].astype(jnp.float32)
            bufs = [c[l] for c in kv_caches]
        hn = _rms_norm(x, norm_mix[l])
        y, s1, kv = _token_mix(hn, w_in[l], w_ret_branch[l], w_att_branch[l], w_out[l], s0, bufs)
        x = x + y
        hn = _rms_norm(x, norm_ffn[l])
        gate, up = jnp.split(hn @ w_gate_up[l], 2, axis=-1)
        x = x + (jax.nn.silu(gate) * up) @ w_down[l]
        rets.append(s1.astype(x.dtype))
        kvs.append(kv)
    y = _rms_norm(x, norm_final)
    ret_out = jnp.stack(rets, axis=0)
    kv_out = [jnp.stack([kvs[l][g] for l in range(DEPTH)], axis=0) for g in range(N_GROUPS)]
    return y, ret_out, kv_out

def setup_inputs(seed: int = 0) -> dict:
    key = jax.random.key(seed)
    ks = jax.random.split(key, 16)
    f32 = jnp.float32
    nrm = jax.random.normal
    wl = [min(w, PAST_LEN) for (w, _) in ATT_GROUPS]
    return {
        'x_prompt': nrm(ks[0], (BATCH, SEQ, D_MODEL), f32),
        'x_sample': nrm(ks[1], (DEC_BATCH, DEC_SEQ, D_MODEL), f32),
        'state_ret': nrm(ks[2], (DEPTH, DEC_BATCH, RET_HEADS, RET_DK, RET_DV), f32),
        'cache_kv_w128': nrm(ks[3], (DEPTH, DEC_BATCH, wl[0], 2, HEADS_PER_GROUP, HEAD_DIM), f32),
        'cache_kv_w512': nrm(ks[4], (DEPTH, DEC_BATCH, wl[1], 2, HEADS_PER_GROUP, HEAD_DIM), f32),
        'cache_kv_w2048': nrm(ks[5], (DEPTH, DEC_BATCH, wl[2], 2, HEADS_PER_GROUP, HEAD_DIM), f32),
        'norm_mix': 1.0 + 0.01 * nrm(ks[6], (DEPTH, D_MODEL), f32),
        'w_in': nrm(ks[7], (DEPTH, D_MODEL, D_IN), f32) * D_MODEL ** -0.5,
        'w_ret_branch': nrm(ks[8], (DEPTH, RET_V, D_MODEL), f32) * RET_V ** -0.5,
        'w_att_branch': nrm(ks[9], (DEPTH, ATT_OUT, D_MODEL), f32) * ATT_OUT ** -0.5,
        'w_out': nrm(ks[10], (DEPTH, D_MODEL, D_MODEL), f32) * D_MODEL ** -0.5,
        'norm_ffn': 1.0 + 0.01 * nrm(ks[11], (DEPTH, D_MODEL), f32),
        'w_gate_up': nrm(ks[12], (DEPTH, D_MODEL, 2 * D_FF), f32) * D_MODEL ** -0.5,
        'w_down': nrm(ks[13], (DEPTH, D_FF, D_MODEL), f32) * D_FF ** -0.5,
        'norm_final': 1.0 + 0.01 * nrm(ks[14], (D_MODEL,), f32),
    }

def reference(x_prompt, x_sample, state_ret, cache_kv_w128, cache_kv_w512, cache_kv_w2048,
              norm_mix, w_in, w_ret_branch, w_att_branch, w_out, norm_ffn, w_gate_up, w_down,
              norm_final):
    y_prompt, p_ret, p_kv = _trunk(x_prompt, None, None, norm_mix, w_in, w_ret_branch,
                                   w_att_branch, w_out, norm_ffn, w_gate_up, w_down, norm_final)
    y_sample, s_ret, s_kv = _trunk(x_sample, state_ret, (cache_kv_w128, cache_kv_w512, cache_kv_w2048),
                                   norm_mix, w_in, w_ret_branch, w_att_branch, w_out, norm_ffn,
                                   w_gate_up, w_down, norm_final)
    return (y_prompt, y_sample, p_ret, p_kv[0], p_kv[1], p_kv[2], s_ret, s_kv[0], s_kv[1], s_kv[2])


_drawn_inputs = setup_inputs


def setup_inputs(seed=0):
    import zlib

    import numpy as np

    out = dict(_drawn_inputs(seed))
    spreads = {}
    factors = {'norm_mix': 3.446, 'norm_ffn': 7.862, 'norm_final': 5.747}
    for name, (base, spread) in spreads.items():
        noise = np.random.default_rng([zlib.crc32(name.encode()), seed]).standard_normal(out[name].shape)
        drawn = base * np.exp(spread * noise) if base else spread * noise
        out[name] = __import__('jax').numpy.asarray(drawn.astype(out[name].dtype))
    for name, factor in factors.items():
        out[name] = (out[name] * factor).astype(out[name].dtype)
    return out
```

```python
from contextlib import ExitStack

import numpy as np
import concourse.bass as bass
from concourse import mybir

F32 = mybir.dt.float32
F32R = mybir.dt.float32r
ALU = mybir.AluOpType
ACT = mybir.ActivationFunctionType
AX_X = mybir.AxisListType.X
ds = bass.ds

P = 128
D = 1024
SEQ = 1024
SAMPLES = 8
TOKENS = SEQ + SAMPLES
PIECES = 3
PIECE = TOKENS // PIECES
KT = D // P
HEADS, DK, DV = 4, 128, 256
CHUNKS = SEQ // P
GROUPS = 3
DILATION = (1, 4, 16)
KEPT = (128, 512, 1024)
AH, HD = 4, 64
PAST = (128, 256, 256)
D_FF = 2816
D_IN = 7424
COL_RQ, COL_RK, COL_RV, COL_RG = 0, 512, 1024, 2048
COL_ATT, COL_GATE_R, COL_GATE_A = 3072, 5376, 6400
KIND = 768
RMS_EPS, GN_EPS = 1e-6, 1e-5
MASKED = -1e30
ROWS_B1, ROWS_B2 = 64, 16
ROWS_B = ROWS_B1 + ROWS_B2 + GROUPS
OUT_ROW = AH * (HD + 2)

U_HEAD0 = 0
U_HEADS = 4
U_GROUP0 = U_HEADS + 6 * (HEADS - 1)
U_GATE3 = U_GROUP0 + 6
U_GROUPS = U_GATE3 + 2
U_GATES = U_GROUPS + 12
U_BRANCH = U_GATES + 16
U_OUT = U_BRANCH + 16
U_FFN = U_OUT + 8
FF_CHUNKS = (8, 7, 7)
T_NORM1 = 18
T_RET = T_NORM1 + 4
RET_TASKS = 28
T_ATT = T_RET + HEADS * RET_TASKS
PREP = (6, 6, 8)
TILE_TASKS = 6
T_PREP0 = T_ATT
T_TILE0 = T_PREP0 + PREP[0]
T_TILES0 = T_TILE0 + TILE_TASKS
T_PREP1 = T_TILES0 + 7 * TILE_TASKS
T_FREE1 = T_PREP1 + PREP[1]
T_PREV1 = T_FREE1 + 2 * TILE_TASKS
T_PREP2 = T_PREV1 + 4 * TILE_TASKS
T_FREE2 = T_PREP2 + PREP[2]
T_SAMPLE = T_FREE2 + 4 * TILE_TASKS
T_MERGE = T_SAMPLE + 10
T_NORM2 = T_MERGE + 4
T_END = T_NORM2 + 4
U_FFN_CHUNK = [U_FFN + sum(2 * n + 8 for n in FF_CHUNKS[:c]) for c in range(len(FF_CHUNKS) + 1)]
U_FINAL = U_FFN_CHUNK[-1]

VT, VS, KT_, KS, SC, UP, OUT_, OUTER, OS, TURN, TS = 0, 4, 5, 7, 8, 10, 14, 18, 22, 23, 27
RET_AT = {(0, 2 + j): j for j in range(6)}
RET_AT.update({(1, 0): 6, (1, 1): 7, (1, 2): 8, (1, 3): 9, (1, 5): 10, (1, 6): 11, (1, 7): 12, (2, 0): 13})
RET_AT.update({(2, 1 + j): 14 + j for j in range(7)})
RET_AT.update({(3, 0): 21, (3, 3): 22, (4, 0): 23, (4, 1): 24, (4, 2): 25, (4, 3): 26, (4, 4): 27})
TILE_AT = (1, 2, 5, 6, 7, 8)
STEPS_HEAD, STEPS_BRANCH, STEPS_OUT, STEPS_FFN = 25, 4, 2, 2
K_STORES = ((0, 0), (0, 1), (1, 2), (3, 4))

CONSTS = {}
_at = 0
for _name, _n in (("ident", P), ("ones", P), ("eye8", 64), ("tail", HEADS), ("gamma_c", HEADS),
                  ("gamma", HEADS), ("eps", 2), ("bias_sa", P), ("bias_sb", ROWS_B)):
    CONSTS[_name] = (_at, _n)
    _at += _n
N_CONST = _at


def tables():
    f = np.float32
    log_gamma = np.log1p(-np.exp2(f(-5.0) - np.arange(HEADS, dtype=f))).astype(f)
    idx = np.arange(P, dtype=f)
    diff = idx[None, :] - idx[:, None]
    decay = np.where(diff[:, None, :] >= 0,
                     np.exp(np.maximum(diff, 0)[:, None, :] * log_gamma[None, :, None]), 0).astype(f)
    inner = np.exp((idx + 1)[None, :] * log_gamma[:, None]).astype(f)
    inner = np.broadcast_to(inner[None], (P, HEADS, P))
    slopes = np.exp2(f(-8.0) * (np.arange(GROUPS * AH, dtype=f) + 1) / f(GROUPS * AH)).astype(f)
    slopes = slopes.reshape(GROUPS, AH)
    parts = {
        "ident": np.eye(P), "ones": np.ones((P, P)),
        "eye8": np.broadcast_to(np.eye(8).reshape(1, 64), (P, 64)),
        "tail": np.exp((P - 1 - idx)[:, None] * log_gamma[None]),
        "gamma_c": np.broadcast_to(np.exp(P * log_gamma)[None], (P, HEADS)),
        "gamma": np.broadcast_to(np.exp(log_gamma)[None], (P, HEADS)),
        "eps": np.broadcast_to(np.array([[RMS_EPS, GN_EPS]]), (P, 2)),
    }
    sa, sb = np.zeros((P, P)), np.zeros((P, ROWS_B))
    for n in range(SAMPLES):
        for h in range(AH):
            row = n * AH + h
            sa[row] = -slopes[0, h] * (P - np.arange(P))
            sb[row, :ROWS_B1] = -slopes[1, h] * (PAST[1] - 4 * np.arange(ROWS_B1))
            sb[row, ROWS_B1:ROWS_B1 + ROWS_B2] = -slopes[2, h] * (PAST[2] - 16 * np.arange(ROWS_B2))
    parts["bias_sa"], parts["bias_sb"] = sa, sb
    small = np.zeros((P, N_CONST), f)
    for name, (at, n) in CONSTS.items():
        small[:, at:at + n] = parts[name]
    qi, kj = np.arange(P)[:, None], np.arange(2 * P)[None]
    dist = qi + P - kj
    near = [np.where((dist >= 0) & (dist <= P), -slopes[g][:, None, None] * (dist * DILATION[g]), MASKED)
            for g in (0, 1)]
    a, b = np.arange(P) // 2, np.arange(P) % 2
    d2 = a[:, None] - a[None]
    near.append(np.where((d2 >= 0) & (b[:, None] == b[None]), -slopes[2][:, None, None] * (d2 * 16), MASKED))
    bias = [x.reshape(2, 2, P, -1).transpose(2, 1, 0, 3).astype(f) for x in near]
    return {"c_small": small, "c_decay": decay.reshape(P, -1), "c_inner": np.ascontiguousarray(inner).reshape(P, -1),
            "c_bias0": bias[0].reshape(P, -1), "c_bias1": bias[1].reshape(P, -1), "c_bias2": bias[2].reshape(P, -1)}


class Place:

    def __init__(self, first, per=0, turn=None):
        assert first % 2 == 0 and per % 2 == 0
        self.first, self.per, self.turn = first, per, turn

    def n(self, j):
        at = self.first + j
        return at if self.turn is None else self.turn * self.per + at

    def half(self, j):
        at = (self.first + j) // 2
        return at if self.turn is None else self.turn * (self.per // 2) + at


class Steps:

    def __init__(self, eng, sem):
        self.eng, self.sem, self.count, self.shift = eng, sem, 0, None

    def __call__(self, instruction):
        instruction.then_inc(self.sem, 1)
        self.count += 1

    def settle(self):
        self.eng.wait_ge(self.sem, self.count if self.shift is None else self.shift + self.count)

    def enter(self, turn, per):
        self.saved = (self.count, self.shift, per)
        self.shift = turn * per if self.shift is None else self.shift + turn * per

    def leave(self, turns):
        count, self.shift, per = self.saved
        assert self.count - count == per, (self.count - count, per)
        self.count = count + per * turns


def wait(eng, sem, value):
    if not isinstance(value, int) or value > 0:
        eng.wait_ge(sem, value)


def build(nc, a, out):
    ctx = ExitStack()
    with ctx:
        def sb(name, shape, dt=F32, stack=ctx):
            return stack.enter_context(nc.sbuf_tensor(name, shape, dt))

        def scratch(name, shape):
            return nc.dram_tensor(name, shape, F32, kind="Internal").ap()

        def sem(name):
            return ctx.enter_context(nc.semaphore(name))

        a_hi = sb("a_hi", [P, KT, TOKENS], F32R)
        a_lo = sb("a_lo", [P, KT, TOKENS], F32R)
        wide = sb("wide", [P, KT, TOKENS])
        w_raw = sb("w_raw", [P, 2, KT, P])
        w_part = sb("w_part", [P, 2, 2, KT, P], F32R)
        rstd = sb("rstd", [P, TOKENS])
        consts = sb("consts", [P, N_CONST])
        gains = sb("gains", [P, 2, KT])

        def const(name, rows=P):
            at, n = CONSTS[name]
            return consts[0:rows, at:at + n]

        with ExitStack() as s:
            x_row = sb("x_row", [P, 2, D], stack=s)
            square = sb("square", [P, 2, TOKENS], stack=s)
            square_sum = sb("square_sum", [P, TOKENS], stack=s)
        with ExitStack() as s:
            decay = sb("decay", [P, HEADS, P], stack=s)
            inner = sb("inner", [P, HEADS, P], stack=s)
            stage = sb("stage", [P, 2, TOKENS], stack=s)
            with ExitStack() as r:
                q_t = sb("q_t", [P, TOKENS], stack=r)
                k_t = sb("k_t", [P, TOKENS], stack=r)
                v_t = sb("v_t", [P, 2, TOKENS], stack=r)
                k_tok = sb("k_tok", [P, CHUNKS, DK], stack=r)
                v_tok = sb("v_tok", [P, CHUNKS, DV], stack=r)
                scores_t = sb("scores_t", [P, CHUNKS, P], stack=r)
                states = sb("states", [P, CHUNKS, DV], stack=r)
                o_tok = sb("o_tok", [P, CHUNKS, DV], stack=r)
                stats = sb("stats", [P, CHUNKS + 1, 6], stack=r)
                moments = sb("moments", [P, CHUNKS + 1, 2], stack=r)
                spread = sb("spread", [P, CHUNKS + 1], stack=r)
                s_state = sb("s_state", [P, SAMPLES, DV], stack=r)
                s_kmask = sb("s_kmask", [SAMPLES, SAMPLES, DK], stack=r)
                s_ktok = sb("s_ktok", [SAMPLES, DK], stack=r)
                s_vtok = sb("s_vtok", [SAMPLES, DV], stack=r)
                s_qmask = sb("s_qmask", [P, SAMPLES, SAMPLES], stack=r)
                s_otok = sb("s_otok", [SAMPLES, DV], stack=r)
            with ExitStack() as r:
                att_in = sb("att_in", [P, 3, 2, SEQ], stack=r)
                att_v = sb("att_v", [P, CHUNKS, 4 * HD], stack=r)
                att_kout = sb("att_kout", [P, 2, 2, 4 * HD], stack=r)
                bias = sb("bias", [P, 1024], stack=r)
                q_win = sb("q_win", [P, 2, 2, 2, P], stack=r)
                k_win = sb("k_win", [P, 2, 2, 2 * P], stack=r)
                probs = sb("probs", [P, 2, 2, 4 * P], stack=r)
                probs_t = sb("probs_t", [P, 2, 2, 4, P], stack=r)
                o_ext = sb("o_ext", [P, 2, 2, AH, HD + 2], stack=r)
        with ExitStack() as s:
            ao_hi = sb("ao_hi", [P, 2, TOKENS], F32R, stack=s)
            ao_lo = sb("ao_lo", [P, 2, TOKENS], F32R, stack=s)
            with ExitStack() as r:
                s_qkv_t = sb("s_qkv_t", [P, 18, SAMPLES], stack=r)
                s_qkv = sb("s_qkv", [SAMPLES, 3, KIND], stack=r)
                kv_a = sb("kv_a", [P, SAMPLES, 2, 4 * HD], stack=r)
                kv_b = sb("kv_b", [ROWS_B, SAMPLES, 2, 4 * HD], stack=r)
                q_a = sb("q_a", [P, SAMPLES, 4 * HD], stack=r)
                q_b = sb("q_b", [ROWS_B, SAMPLES, 4 * HD], stack=r)
                s_score = sb("s_score", [P, 2, 32], stack=r)
                s_prob = sb("s_prob", [32, P + ROWS_B], stack=r)
                s_ptok = sb("s_ptok", [P, 2, 32], stack=r)
                s_small = sb("s_small", [32, 4], stack=r)
            with ExitStack() as r:
                parts = sb("parts", [P, GROUPS, CHUNKS * AH, HD + 2], stack=r)
                ao_tok = sb("ao_tok", [P, CHUNKS, 4 * HD], stack=r)
                prod = sb("prod", [P, CHUNKS * AH, HD], stack=r)
                mrg = sb("mrg", [P, 8, CHUNKS * AH], stack=r)
            with ExitStack() as r:
                b_hi = sb("b_hi", [P, KT, TOKENS], F32R, stack=r)
                b_lo = sb("b_lo", [P, KT, TOKENS], F32R, stack=r)
        with ExitStack() as s:
            temp = sb("temp", [P, 4, TOKENS], stack=s)
            y_row = sb("y_row", [P, 2, D], stack=s)
            gain_row = sb("gain_row", [P, D], stack=s)
            fin = sb("fin", [P, 2, 2], stack=s)
            y_square = sb("y_square", [P, D], stack=s)

        unit_ps = [ctx.enter_context(nc.psum_tensor(f"unit_ps{g}", [P, PIECES, 512], F32)) for g in range(2)]
        task_ps = [ctx.enter_context(nc.psum_tensor(f"task_ps{b}", [P, 512], F32)) for b in range(2)]

        x_spill = scratch("x_spill", [KT, P, TOKENS])
        att_spill = scratch("att_spill", [18, P, TOKENS])
        gate_spill = scratch("gate_spill", [2 * KT, P, TOKENS])
        att_rows = scratch("att_rows", [GROUPS, SEQ, OUT_ROW])
        sample_rows = scratch("sample_rows", [3, SAMPLES, KIND])

        const_loaded = sem("const_loaded")
        table_loaded = sem("table_loaded")
        x_loaded = [sem(f"x_loaded{i}") for i in range(2)]
        x_spilled = sem("x_spilled")
        squared = sem("squared")
        summed = sem("summed")
        root = sem("root")
        rstd_ready = sem("rstd_ready")
        w_loaded = [sem(f"w_loaded{i}") for i in range(2)]
        w_high = sem("w_high")
        w_split = sem("w_split")
        unit_done = sem("unit_done")
        unit_free = [sem(f"unit_free{g}") for g in range(2)]
        task_done = [sem(f"task_done{b}") for b in range(2)]
        task_free = [sem(f"task_free{b}") for b in range(2)]
        a_ready = sem("a_ready")
        b_ready = sem("b_ready")
        dve_step = sem("dve_step")
        act_step = sem("act_step")
        silu_done = sem("silu_done")
        q_ready = sem("q_ready")
        masked_ready = sem("masked_ready")
        normed = sem("normed")
        s_loaded = sem("s_loaded")
        s_stored = sem("s_stored")
        p_stored = sem("p_stored")
        spilled = [sem(f"spilled{i}") for i in range(2)]
        att_loaded = sem("att_loaded")
        window = sem("window")
        peak = sem("peak")
        exps = sem("exps")
        rows_stored = [sem(f"rows_stored{i}") for i in range(2)]
        v_stored = sem("v_stored")
        k_stored = [sem(f"k_stored{i}") for i in range(2)]
        qkv_loaded = sem("qkv_loaded")
        cache_loaded = sem("cache_loaded")
        rows_written = sem("rows_written")
        smp_out = sem("smp_out")
        smp_dve = sem("smp_dve")
        smp_act = sem("smp_act")
        parts_loaded = sem("parts_loaded")
        mrg_dve = sem("mrg_dve")
        mrg_act = sem("mrg_act")
        gate_loaded = [sem(f"gate_loaded{i}") for i in range(2)]
        x_back = [sem(f"x_back{i}") for i in range(2)]
        gain_loaded = sem("gain_loaded")
        y_stored = [sem(f"y_stored{i}") for i in range(2)]

        w_in, w_ret, w_att, w_out, w_gu, w_down = (
            a[name][0].rearrange("(k p) n -> p k n", p=P)
            for name in ("w_in", "w_ret_branch", "w_att_branch", "w_out", "w_gate_up", "w_down"))
        p_kv = (out["p_kv_w128"], out["p_kv_w512"], out["p_kv_w2048"])
        s_kv = (out["s_kv_w128"], out["s_kv_w512"], out["s_kv_w2048"])

        def flat(ap):
            return ap.rearrange("p a b -> p (a b)")

        def pieces(ap):
            return ap.rearrange("p (n t) -> p n t", n=PIECES)

        def unit_out(g):
            return unit_ps[g][:, :, 0:PIECE]

        def columns(ap, g, t, tokens=P):
            if g == 0:
                return ap[:, ds(t * P, tokens)]
            if g == 1:
                start = (t // 4) * 512 + t % 4 if isinstance(t, int) else t
                return ap[:, ds(start, tokens, 4)]
            return ap[:, ds(t, tokens, 8)]

        block = ctx.enter_context(nc.Block())

        @block.sync
        def _(sp):
            sp.dma_start(consts[:], a["c_small"]).then_inc(const_loaded, 16)
            for t in range(2):
                sp.dma_start(x_row[:, t, :], a["x_prompt"][0, t * P:(t + 1) * P, :]).then_inc(x_loaded[t], 16)
            sp.dma_start(gains[:], a["norm_gains"]).then_inc(const_loaded, 16)

            def load(pl, j, kt, src):
                wait(sp, w_split, pl.n(j) - 1)
                sp.dma_start(w_raw[:, j % 2, 0:kt, :], src).then_inc(w_loaded[j % 2], 16)

            cols = (COL_RV, COL_RV + P, COL_RK, COL_RQ)
            for j in range(2):
                load(Place(0), j, KT, w_in[:, :, cols[j]:cols[j] + P])
            for t in range(2, CHUNKS + 1):
                sp.wait_ge(task_done[1], t - 1)
                if t < CHUNKS:
                    sp.dma_start(x_row[:, t % 2, :], a["x_prompt"][0, t * P:(t + 1) * P, :]).then_inc(x_loaded[t % 2], 16)
                else:
                    sp.dma_start(x_row[0:SAMPLES, 0, :], a["x_sample"][:, 0, :]).then_inc(x_loaded[0], 16)
            for j in range(2, 4):
                load(Place(0), j, KT, w_in[:, :, cols[j]:cols[j] + P])
            for b in range(2):
                sp.wait_ge(task_free[b], CHUNKS + 1)
            sp.dma_start(x_spill.rearrange("k p t -> p k t"), wide[:]).then_inc(x_spilled, 16)
            sp.wait_ge(rstd_ready, 1)
            sp.dma_start(flat(decay[:]), a["c_decay"]).then_inc(table_loaded, 16)
            sp.dma_start(flat(inner[:]), a["c_inner"]).then_inc(table_loaded, 16)
            with sp.Fori(0, HEADS - 1) as h:
                for j, (c, by) in enumerate(((COL_RV + DV, DV), (COL_RV + DV + P, DV), (COL_RK + DK, DK),
                                             (COL_RQ + DK, DK), (COL_RG, DV), (COL_RG + P, DV))):
                    load(Place(U_HEADS, 6, h), j, KT, w_in[:, :, ds(h * by + c, P)])
            for j in range(6):
                c = COL_ATT + KIND * (j // 2) + P * (j % 2)
                load(Place(U_GROUP0), j, KT, w_in[:, :, c:c + P])
            for j in range(2):
                c = COL_RG + 3 * DV + P * j
                load(Place(U_GATE3), j, KT, w_in[:, :, c:c + P])
            for g in (1, 2):
                with sp.Fori(0, 3) as kind:
                    for j in range(2):
                        load(Place(U_GROUPS + 6 * (g - 1), 2, kind), j, KT,
                             w_in[:, :, ds(kind * KIND + (COL_ATT + 256 * g + P * j), P)])
            with sp.Fori(0, KT) as m:
                for j, c in enumerate((COL_GATE_R, COL_GATE_A)):
                    load(Place(U_GATES, 2, m), j, KT, w_in[:, :, ds(m * P + c, P)])

            def branch_loads(pl, m, x):
                sp.dma_start(wide[:, 2 * x:2 * x + 2, :], gate_spill[ds(m * 2, 2)].rearrange("a p t -> p a t"))\
                  .then_inc(gate_loaded[x], 16)
                load(pl, 0, KT, w_ret[:, :, ds(m * P, P)])
                load(pl, 1, 2, w_att[:, :, ds(m * P, P)])

            sp.wait_ge(a_ready, 2 * KT)
            for x in range(2):
                sp.wait_ge(spilled[x], 16 * 17)
            for m in range(2):
                branch_loads(Place(U_BRANCH + 2 * m), m, m)
            with sp.Fori(0, KT // 2 - 1) as i:
                for x in range(2):
                    sp.wait_ge(unit_free[1], i * 2 + (U_BRANCH // 2 + x + 1))
                    branch_loads(Place(U_BRANCH + 4 + 2 * x, 4, i), i * 2 + (2 + x), x)

            def out_loads(pl, j, m):
                sp.dma_start(temp[:, j, :], x_spill[ds(m, 1)].rearrange("a p t -> p (a t)")).then_inc(x_back[j], 16)
                load(pl, j, KT, w_out[:, :, ds(m * P, P)])

            sp.wait_ge(x_spilled, 16)
            sp.wait_ge(unit_done, U_OUT)
            for j in range(2):
                out_loads(Place(U_OUT), j, j)
            with sp.Fori(0, KT // 2 - 1) as i:
                for j in range(2):
                    sp.wait_ge(unit_free[j], i + (U_OUT // 2 + 1))
                    out_loads(Place(U_OUT + 2, 2, i), j, i * 2 + (2 + j))
            for c, nf in enumerate(FF_CHUNKS):
                f0 = sum(FF_CHUNKS[:c])
                with sp.Fori(0, nf) as f:
                    for j in range(2):
                        load(Place(U_FFN_CHUNK[c], 2, f), j, KT, w_gu[:, :, ds(f * P + (j * D_FF + f0 * P), P)])
                with sp.Fori(0, KT // 2) as i:
                    for j in range(2):
                        load(Place(U_FFN_CHUNK[c] + 2 * nf, 2, i), j, nf,
                             w_down[:, f0:f0 + nf, ds(i * 2 * P + j * P, P)])
            sp.wait_ge(unit_done, U_FINAL)
            sp.dma_start(gain_row[:], a["norm_final"].partition_broadcast(P)).then_inc(gain_loaded, 16)
            for t in range(CHUNKS + 1):
                sp.wait_ge(unit_free[t % 2], Place(U_FINAL).half(t) + 1)
                if t < CHUNKS:
                    sp.dma_start(out["y_prompt"][0, t * P:(t + 1) * P, :], y_row[:, t % 2, :]).then_inc(y_stored[t % 2], 16)
                else:
                    sp.dma_start(out["y_sample"][:, 0, :], y_row[0:SAMPLES, 0, :]).then_inc(y_stored[0], 16)
            sp.wait_ge(y_stored[0], 16 * 5)
            sp.wait_ge(y_stored[1], 16 * 4)
            sp.wait_ge(s_stored, 16 * HEADS)
            sp.wait_ge(p_stored, 16 * HEADS)
            sp.wait_ge(v_stored, 16 * GROUPS)
            for x in range(2):
                sp.wait_ge(k_stored[x], 16 * K_STORES[GROUPS][x])
            sp.wait_ge(smp_out, 16 * GROUPS)

        @block.gpsimd
        def _(pool):
            def split(pl, j, kt):
                s = j % 2
                pool.wait_ge(w_loaded[s], pl.half(j) * 16 + 16)
                wait(pool, unit_done, pl.n(j) - 1)
                raw, part = w_raw[:, s, 0:kt, :], w_part[:, s, :, 0:kt, :]
                one = const("ones").unsqueeze(1).to_broadcast([P, kt, P])
                pool.tensor_tensor(part[:, 0], raw, one, ALU.mult).then_inc(w_high, 1)
                pool.wait_ge(w_high, pl.n(j) + 1)
                pool.tensor_tensor(part[:, 1], raw, part[:, 0].bitcast(F32), ALU.subtract).then_inc(w_split, 1)

            pool.wait_ge(const_loaded, 16 * 2)
            for j in range(2):
                split(Place(0), j, KT)
            for k in range(KT):
                pool.wait_ge(squared, k + 1)
                if k == 0:
                    pool.tensor_copy(square_sum[:], square[:, 0, :]).then_inc(summed, 1)
                else:
                    pool.wait_ge(summed, k)
                    pool.tensor_tensor(square_sum[:], square_sum[:], square[:, k % 2, :], ALU.add).then_inc(summed, 1)
            for j in range(2, 4):
                split(Place(0), j, KT)
            with pool.Fori(0, (U_BRANCH - U_HEADS) // 2) as i:
                for j in range(2):
                    split(Place(U_HEADS, 2, i), j, KT)
            with pool.Fori(0, KT) as m:
                for j, kt in enumerate((KT, 2)):
                    split(Place(U_BRANCH, 2, m), j, kt)
            with pool.Fori(0, KT // 2) as i:
                for j in range(2):
                    split(Place(U_OUT, 2, i), j, KT)
            for c, nf in enumerate(FF_CHUNKS):
                with pool.Fori(0, nf) as f:
                    for j in range(2):
                        split(Place(U_FFN_CHUNK[c], 2, f), j, KT)
                with pool.Fori(0, KT // 2) as i:
                    for j in range(2):
                        split(Place(U_FFN_CHUNK[c] + 2 * nf, 2, i), j, nf)

        @block.tensor
        def _(pe):
            ident = const("ident")

            def unit(pl, j, kt, hi, lo, ready=None, between=None):
                s = j % 2
                pe.wait_ge(w_split, pl.n(j) + 1)
                wait(pe, unit_free[s], pl.half(j))
                for k in range(kt):
                    if between:
                        between(k)
                    if ready:
                        pe.wait_ge(ready[0], ready[1] + k + 1)
                    for part, (w, x) in enumerate(((0, hi), (0, lo), (1, hi))):
                        for n in range(PIECES):
                            mm = pe.matmul(unit_ps[s][:, n, 0:PIECE], w_part[:, s, w, k, :],
                                           x[:, k, n * PIECE:(n + 1) * PIECE],
                                           start=(k == 0 and part == 0), stop=(k == kt - 1 and part == 2))
                mm.then_inc(unit_done, 1)
                if between:
                    between(kt)

            def begin(pl, j):
                wait(pe, task_free[j % 2], pl.half(j))
                return task_ps[j % 2]

            def end(mm, j):
                mm.then_inc(task_done[j % 2], 1)

            def taken(pl, j):
                pe.wait_ge(task_free[j % 2], pl.half(j) + 1)

            def norm_sum(pl, tiles, source):
                pe.wait_ge(summed, tiles)
                for j in range(4):
                    ps = begin(pl, j)
                    n = TOKENS // 4
                    end(pe.matmul(ps[:, 0:n], const("ones"), source[:, j * n:(j + 1) * n], start=True, stop=True), j)

            pe.wait_ge(const_loaded, 16 * 2)
            for t in range(CHUNKS + 1):
                rows = P if t < CHUNKS else SAMPLES
                pe.wait_ge(x_loaded[t % 2], 16 * (t // 2 + 1))
                for b in range(2):
                    ps = begin(Place(0), 2 * t + b)
                    for q in range(4):
                        c = (4 * b + q) * P
                        mm = pe.transpose(ps[:, q * P:q * P + rows], x_row[0:rows, t % 2, c:c + P], ident[0:rows, 0:rows])
                    end(mm, b)
            unit(Place(0), 0, KT, a_hi, a_lo, ready=(a_ready, 0))
            norm_sum(Place(T_NORM1), KT, square_sum)
            for j in range(1, 4):
                unit(Place(0), j, KT, a_hi, a_lo)

            def ret_task(pl, up, heads, j):
                ps = begin(pl, j)
                if j == 0:
                    pe.wait_ge(unit_free[0], up.half(0))
                    pe.wait_ge(unit_free[1], up.half(0))
                if j < VS:
                    for q in range(2):
                        n = 2 * j + q
                        for v in range(2):
                            mm = pe.transpose(ps[:, (2 * q + v) * P:(2 * q + v + 1) * P], v_t[:, v, n * P:(n + 1) * P], ident)
                elif j == VS:
                    for v in range(2):
                        mm = pe.transpose(ps[0:SAMPLES, v * P:(v + 1) * P], v_t[:, v, SEQ:TOKENS], ident)
                elif j < KS:
                    for q in range(4):
                        n = 4 * (j - KT_) + q
                        mm = pe.transpose(ps[:, q * P:(q + 1) * P], k_t[:, n * P:(n + 1) * P], ident)
                elif j == KS:
                    mm = pe.transpose(ps[0:SAMPLES, 0:P], k_t[:, SEQ:TOKENS], ident)
                elif j < UP:
                    for q in range(4):
                        c = slice((4 * (j - SC) + q) * P, (4 * (j - SC) + q + 1) * P)
                        mm = pe.matmul(ps[:, q * P:(q + 1) * P], k_t[:, c], q_t[:, c], start=True, stop=True)
                elif j < OUT_:
                    for q in range(2):
                        n = 2 * (j - UP) + q
                        mm = pe.matmul(ps[:, q * DV:(q + 1) * DV], k_tok[:, n, :], v_tok[:, n, :], start=True, stop=True)
                elif j < OUTER:
                    if j == OUT_:
                        pe.wait_ge(q_ready, heads + 1)
                    for q in range(2):
                        n = 2 * (j - OUT_) + q
                        mm = pe.matmul(ps[:, q * DV:(q + 1) * DV], scores_t[:, n, :], v_tok[:, n, :], start=True, stop=n == 0)
                        if n:
                            mm = pe.matmul(ps[:, q * DV:(q + 1) * DV], q_t[:, n * P:(n + 1) * P], states[:, n - 1, :],
                                           start=False, stop=True)
                elif j < OS:
                    if j == OUTER:
                        pe.wait_ge(masked_ready, heads + 1)
                    for q in range(2):
                        mm = pe.matmul(ps[:, q * DV:(q + 1) * DV], s_kmask[:, 2 * (j - OUTER) + q, :], s_vtok[:],
                                       start=True, stop=True)
                elif j == OS:
                    taken(pl, OUTER + 3)
                    for n in range(SAMPLES):
                        mm = pe.matmul(ps[0:SAMPLES, 0:DV], s_qmask[:, n, :], s_state[:, n, :],
                                       start=(n == 0), stop=(n == SAMPLES - 1))
                elif j < TS:
                    if j == TURN:
                        pe.wait_ge(normed, heads * 2 + 2)
                    for v in range(2):
                        for q in range(2):
                            mm = pe.transpose(ps[:, (2 * v + q) * P:(2 * v + q + 1) * P],
                                              o_tok[:, 2 * (j - TURN) + q, v * P:(v + 1) * P], ident)
                else:
                    for v in range(2):
                        mm = pe.matmul(ps[:, v * SAMPLES:(v + 1) * SAMPLES], s_otok[:, v * P:(v + 1) * P],
                                       ident[0:SAMPLES, 0:SAMPLES], start=True, stop=True)
                end(mm, j)

            def ret_stage(pl, up, heads):
                for j in range(6):
                    unit(up, j, KT, a_hi, a_lo,
                         between=lambda k: ret_task(pl, up, heads, RET_AT[j, k]) if (j, k) in RET_AT else None)

            with pe.Fori(0, HEADS - 1) as h:
                ret_stage(Place(T_RET, RET_TASKS, h), Place(U_HEADS, 6, h), h)
            ret_stage(Place(T_RET + RET_TASKS * (HEADS - 1)), Place(U_GROUP0), HEADS - 1)

            def prep_task(pl, g, j):
                if j == 0:
                    pe.wait_ge(att_loaded, 16 * 2 * (g + 1))
                ps = begin(pl, j)
                kind, t0 = (2, 2 * j) if j < 4 else (1, 2 * (j - 4) + (0 if g == 2 else 4))
                for q in range(2):
                    for pair in range(2):
                        mm = pe.transpose(ps[:, (2 * q + pair) * P:(2 * q + pair + 1) * P],
                                          columns(att_in[:, kind, pair, :], g, t0 + q), ident)
                end(mm, j)

            def tile_scores(pl, e, nth, buf, prev, tiles):
                ps = begin(pl, e)
                pe.wait_ge(window, nth + 1)
                keys = 2 * P if prev else P
                half = slice(64 * e, 64 * e + 64)
                for t in range(tiles):
                    for pair in range(2):
                        at = (2 * t + pair) * keys
                        mm = pe.matmul(ps[:, at:at + keys], q_win[half, buf, pair, t, :],
                                       k_win[half, buf, pair, t * P:t * P + keys], start=True, stop=True)
                end(mm, e)

            def tile_turn(pl, e, nth, buf, prev, tiles):
                ps = begin(pl, 2 + e)
                pe.wait_ge(exps, nth * 2 + (e + 1))
                for x in range(2 * tiles * (2 if prev else 1)):
                    mm = pe.transpose(ps[:, x * P:(x + 1) * P], probs[:, buf, e, x * P:(x + 1) * P], ident)
                end(mm, 2 + e)

            def tile_values(pl, e, buf, prev, tiles, v_tiles):
                ps = begin(pl, 4 + e)
                for t in range(tiles):
                    for pair in range(2):
                        at, col = (2 * t + pair) * HD, (2 * pair + e) * HD
                        blocks = ((2 * pair, v_tiles[0]), (2 * pair + 1, v_tiles[1])) if prev else ((2 * t + pair, v_tiles[t]),)
                        for x, (blk, tile) in enumerate(blocks):
                            v = flat(att_v[:, ds(tile, 1), col:col + HD])
                            mm = pe.matmul(ps[:, at:at + HD], probs_t[:, buf, e, blk, :], v,
                                           start=(x == 0), stop=(x == len(blocks) - 1))
                end(mm, 4 + e)

            def tile_task(j, pl, nth, buf, prev, tiles, v_tiles):
                if j < 2:
                    tile_scores(pl, j, nth, buf, prev, tiles)
                elif j < 4:
                    tile_turn(pl, j - 2, nth, buf, prev, tiles)
                else:
                    tile_values(pl, j - 4, buf, prev, tiles, v_tiles)

            def beside(at, *args):
                def between(k):
                    for j in range(TILE_TASKS):
                        if at[j] == k:
                            tile_task(j, *args)
                return between

            unit(Place(U_GATE3), 0, KT, a_hi, a_lo)
            unit(Place(U_GATE3), 1, KT, a_hi, a_lo,
                 between=lambda k: prep_task(Place(T_PREP0), 0, k - 1) if 1 <= k < 7 else None)
            for j in range(TILE_TASKS):
                tile_task(j, Place(T_TILE0), 0, 0, False, 1, (0,))
            with pe.Fori(0, 3) as i:
                for x in range(2):
                    up = Place(U_GROUPS + 2 * x, 4, i)
                    unit(up, 0, KT, a_hi, a_lo,
                         between=beside(TILE_AT, Place(T_TILES0 + 6 * x, 12, i), i * 2 + (1 + x), (1 + x) % 2, True, 1,
                                        (i * 2 + x, i * 2 + (x + 1))))
                    unit(up, 1, KT, a_hi, a_lo)
            for j in range(TILE_TASKS):
                tile_task(j, Place(T_TILES0 + 36), 7, 1, True, 1, (6, 7))
            for j in range(PREP[1]):
                prep_task(Place(T_PREP1), 1, j)
            with pe.Fori(0, 1) as i:
                for x in range(2):
                    up = Place(U_GATES + 2 * x, 4, i)
                    unit(up, 0, KT, a_hi, a_lo,
                         between=beside(TILE_AT, Place(T_FREE1 + 6 * x, 12, i), i + (8 + x), x, False, 2,
                                        (i + 2 * x, i + (2 * x + 1))))
                    unit(up, 1, KT, a_hi, a_lo)
            with pe.Fori(0, 2) as i:
                for x in range(2):
                    unit(Place(U_GATES + 4, 2, i), x, KT, a_hi, a_lo,
                         between=beside(TILE_AT, Place(T_PREV1 + 6 * x, 12, i), i * 2 + (10 + x), x, True, 1,
                                        (i * 2 + x, i * 2 + (4 + x))))
            for j in range(PREP[2]):
                prep_task(Place(T_PREP2), 2, j)
            with pe.Fori(0, 2) as i:
                for x in range(2):
                    up = Place(U_GATES + 8 + 2 * x, 4, i)
                    unit(up, 0, KT, a_hi, a_lo,
                         between=beside(TILE_AT, Place(T_FREE2 + 6 * x, 12, i), i * 2 + (14 + x), x, False, 2,
                                        (i * 4 + 2 * x, i * 4 + (2 * x + 1))))
                    unit(up, 1, KT, a_hi, a_lo)

            pl = Place(T_SAMPLE)
            pe.wait_ge(qkv_loaded, 16)
            for j in range(6):
                ps = begin(pl, j)
                for q in range(4 - 2 * (j % 2)):
                    f = 4 * (j % 2) + q
                    mm = pe.transpose(ps[0:SAMPLES, q * P:(q + 1) * P], s_qkv_t[:, 6 * (f // 2) + 2 * (j // 2) + f % 2, :], ident)
                end(mm, j)
            ps = begin(pl, 6)
            pe.wait_ge(smp_dve, 1)
            pe.transpose(ps[0:32, 0:P], s_score[:, 0, :], ident)
            end(pe.transpose(ps[0:32, P:P + ROWS_B], s_score[0:ROWS_B, 1, :], ident[0:ROWS_B, 0:ROWS_B]), 6)
            ps = begin(pl, 7)
            pe.wait_ge(smp_dve, 2)
            pe.transpose(ps[:, 0:32], s_prob[:, 0:P], ident[0:32, 0:32])
            end(pe.transpose(ps[0:ROWS_B, 32:64], s_prob[:, P:P + ROWS_B], ident[0:32, 0:32]), 7)
            taken(pl, 7)
            for pair in range(2):
                ps = begin(pl, 8 + pair)
                for n in range(SAMPLES):
                    c, f = 4 * n + 2 * pair, slice(pair * P, (pair + 1) * P)
                    pe.matmul(ps[:, 2 * n:2 * n + 2], kv_a[:, n, 1, f], s_ptok[:, 0, c:c + 2], start=True, stop=False)
                    mm = pe.matmul(ps[:, 2 * n:2 * n + 2], kv_b[:, n, 1, f], s_ptok[0:ROWS_B, 1, c:c + 2], start=False, stop=True)
                end(mm, 8 + pair)

            pe.wait_ge(mrg_dve, 2)
            for j in range(4):
                ps = begin(Place(T_MERGE), j)
                for pair in range(2):
                    for q in range(2):
                        mm = pe.transpose(ps[:, (2 * pair + q) * P:(2 * pair + q + 1) * P],
                                          ao_tok[:, 2 * j + q, pair * P:(pair + 1) * P], ident)
                end(mm, j)

            with pe.Fori(0, KT) as m:
                unit(Place(U_BRANCH, 2, m), 0, KT, a_hi, a_lo, ready=(a_ready, KT))
                for b in range(2):
                    pe.wait_ge(task_free[b], T_NORM2 // 2)
                unit(Place(U_BRANCH, 2, m), 1, 2, ao_hi, ao_lo)
            with pe.Fori(0, KT // 2) as i:
                for j in range(2):
                    unit(Place(U_OUT, 2, i), j, KT, b_hi, b_lo, ready=(b_ready, 0))
            norm_sum(Place(T_NORM2), 2 * KT, temp[:, 3])
            for c, nf in enumerate(FF_CHUNKS):
                with pe.Fori(0, nf) as f:
                    for j in range(2):
                        unit(Place(U_FFN_CHUNK[c], 2, f), j, KT, a_hi, a_lo, ready=(a_ready, 2 * KT))
                with pe.Fori(0, KT // 2) as i:
                    for j in range(2):
                        unit(Place(U_FFN_CHUNK[c] + 2 * nf, 2, i), j, nf, b_hi, b_lo,
                             ready=(b_ready, KT + sum(FF_CHUNKS[:c])))
            for g in range(2):
                pe.wait_ge(unit_free[g], U_FINAL // 2)
            for t in range(CHUNKS + 1):
                n, g = P if t < CHUNKS else SAMPLES, t % 2
                pe.wait_ge(unit_free[g], Place(U_FINAL).half(t))
                for k in range(KT):
                    mm = pe.transpose(unit_ps[g][0:n, k // 4, (k % 4) * P:(k % 4 + 1) * P], wide[:, k, t * P:t * P + n], ident)
                mm.then_inc(unit_done, 1)

        @block.scalar
        def _(act):
            def full(pl, j):
                act.wait_ge(task_done[j % 2], pl.half(j) + 1)
                return task_ps[j % 2]

            def empty(ins, j):
                ins.then_inc(task_free[j % 2], 1)

            def norm_root(pl):
                n = TOKENS // 4
                for j in range(4):
                    ps = full(pl, j)
                    empty(act.activation(rstd[:, j * n:(j + 1) * n], ps[:, 0:n], ACT.Sqrt, scale=1.0 / D,
                                         bias=const("eps")[:, 0:1]), j)

            for t in range(CHUNKS + 1):
                n = P if t < CHUNKS else SAMPLES
                for b in range(2):
                    ps = full(Place(0), 2 * t + b)
                    empty(act.activation(wide[:, 4 * b:4 * b + 4, t * P:t * P + n],
                                         ps[:].rearrange("p (q t) -> p q t", q=4)[:, :, 0:n], ACT.Copy), b)
            for b in range(2):
                act.wait_ge(task_free[b], CHUNKS + 1)
            for k in range(KT):
                if k >= 2:
                    act.wait_ge(summed, k - 1)
                act.activation(square[:, k % 2, :], wide[:, k, :], ACT.Square).then_inc(squared, 1)
            norm_root(Place(T_NORM1))

            def load_states(h):
                act.dma_start(s_state[:], a["state_ret"][0][:, ds(h, 1)].rearrange("n a d v -> d (n a) v")).then_inc(s_loaded, 16)

            act.wait_ge(rstd_ready, 1)
            load_states(0)

            def ret_slot(pl, h, j):
                for x in {0: range(VT, KT_), 1: (KS,), 2: range(OUT_, OUTER), 3: (OS,)}.get(j, ()):
                    ps = full(pl, x)
                    if x < VS:
                        ins = act.activation(v_tok[:, 2 * x:2 * x + 2, :], ps[:].rearrange("p (q d) -> p q d", q=2), ACT.Copy)
                    elif x == VS:
                        ins = act.activation(s_vtok[:], ps[0:SAMPLES, 0:DV], ACT.Copy)
                    elif x == KS:
                        ins = act.activation(s_ktok[:], ps[0:SAMPLES, 0:DK], ACT.Copy)
                    elif x < OUTER:
                        n = 2 * (x - OUT_)
                        ins = act.activation(o_tok[:, n:n + 2, :], ps[:].rearrange("p (q d) -> p q d", q=2), ACT.Copy)
                    else:
                        ins = act.activation(s_otok[:], ps[0:SAMPLES, 0:DV], ACT.Copy)
                    empty(ins, x)
                if j == 2:
                    act.wait_ge(task_free[1], pl.half(UP + 3) + 1)
                    act.dma_start(out["p_ret"][0, 0][ds(h, 1)].rearrange("a d v -> d (a v)"), states[:, CHUNKS - 1, :])\
                       .then_inc(p_stored, 16)
                if j == 3:
                    act.wait_ge(task_free[0], pl.half(OUTER + 2) + 1)
                    act.wait_ge(task_free[1], pl.half(OUTER + 3) + 1)
                    act.dma_start(out["s_ret"][0][:, ds(h, 1)].rearrange("n a d v -> d (n a) v"), s_state[:]).then_inc(s_stored, 16)
                    act.wait_ge(normed, h * 2 + 1)
                    act.activation(spread[:, 0:CHUNKS], flat(moments[:, 0:CHUNKS, 1:2]), ACT.Sqrt, bias=const("eps")[:, 1:2])
                    act.activation(spread[0:SAMPLES, CHUNKS:CHUNKS + 1], moments[0:SAMPLES, CHUNKS, 1:2], ACT.Sqrt,
                                   bias=const("eps", SAMPLES)[:, 1:2]).then_inc(root, 1)

            def in_place(pl, j, func):
                act.wait_ge(unit_free[j % 2], pl.half(j) + 1)
                act.activation(stage[:, j % 2, :], stage[:, j % 2, :], func).then_inc(silu_done, 1)

            with act.Fori(0, HEADS - 1) as h:
                pl = Place(T_RET, RET_TASKS, h)
                up = Place(U_HEADS, 6, h)
                for j in range(6):
                    ret_slot(pl, h, j)
                    if j >= 4:
                        in_place(up, j, ACT.Silu)
                act.wait_ge(s_stored, h * 16 + 16)
                load_states(h + 1)

            def spill(pl, j, dst):
                act.wait_ge(unit_free[j % 2], pl.half(j) + 1)
                act.dma_start(dst, stage[:, j % 2, :]).then_inc(spilled[j % 2], 16)

            for j in range(6):
                ret_slot(Place(T_RET + RET_TASKS * (HEADS - 1)), HEADS - 1, j)
                spill(Place(U_GROUP0), j, att_spill[j])

            def load_group(g):
                for x in range(2):
                    act.wait_ge(spilled[x], 16 * 3 * (g + 1))
                act.dma_start(att_in[:].rearrange("p a b t -> p (a b) t"),
                              att_spill[6 * g:6 * g + 6, :, 0:SEQ].rearrange("a p t -> p a t")).then_inc(att_loaded, 16)
                n = 1024 if g < 2 else 512
                act.dma_start(bias[:, 0:n], a[f"c_bias{g}"]).then_inc(att_loaded, 16)

            for b in range(2):
                act.wait_ge(task_free[b], T_ATT // 2)
            act.wait_ge(s_stored, 16 * HEADS)
            act.wait_ge(p_stored, 16 * HEADS)
            load_group(0)

            def kv_store(g, kind, t0, n, src, stored):
                rows = p_kv[g][0, 0][:, kind - 1].rearrange("r h d -> r (h d)")
                if g == 0:
                    dst, src = rows, src[:, n - 1, :]
                elif g == 1:
                    dst = rows.rearrange("(p t) d -> p t d", t=4)[:, t0 - 4:t0 - 4 + n, :]
                else:
                    dst = rows.rearrange("(p t) d -> p t d", t=8)[:, t0:t0 + n, :]
                act.dma_start(dst, src).then_inc(stored, 16)

            def prep(pl, g):
                wait(act, v_stored, 16 * g)
                for j in range(PREP[g]):
                    ps = full(pl, j)[:].rearrange("p (q d) -> p q d", q=2)
                    if j < 4:
                        empty(act.activation(att_v[:, 2 * j:2 * j + 2, :], ps, ACT.Copy), j)
                        continue
                    wait(act, k_stored[j % 2], 16 * (K_STORES[g][j % 2] + (j - 4) // 2))
                    empty(act.activation(att_kout[:, j % 2], ps, ACT.Copy), j)
                    if j == 4:
                        for b in range(2):
                            act.wait_ge(task_free[b], pl.half(2 + b) + 1)
                        t0 = (7, 4, 0)[g]
                        kv_store(g, 2, t0, 8 - t0, att_v[:, t0:8, :], v_stored)
                    if g or j == 5:
                        act.wait_ge(task_free[j % 2], pl.half(j) + 1)
                        kv_store(g, 1, 2 * (j - 4) + (0 if g == 2 else 4), 2, att_kout[:, j % 2], k_stored[j % 2])

            def tile(pl, g, t, nth, buf, prev, tiles, dst):
                for pair in range(2):
                    if prev:
                        act.activation(k_win[:, buf, pair, :],
                                       columns(att_in[:, 1, pair, :], g, t - 1 if g == 0 else t, 2 * P), ACT.Copy)
                        start = t if g == 0 else t + 512
                        ins = act.activation(q_win[:, buf, pair, 0, :], columns(att_in[:, 0, pair, :], g, start), ACT.Copy,
                                             scale=HD ** -0.5)
                    else:
                        for x in range(tiles):
                            k = k_win[:, buf, pair, x * P:(x + 1) * P]
                            q = q_win[:, buf, pair, x, :]
                            act.activation(k, columns(att_in[:, 1, pair, :], g, t + x), ACT.Copy)
                            ins = act.activation(q, columns(att_in[:, 0, pair, :], g, t + x), ACT.Copy, scale=HD ** -0.5)
                ins.then_inc(window, 1)
                keys = 2 * P if prev else P
                for e in range(2):
                    act.wait_ge(peak, nth * 2 + (e + 1))
                    for x in range(tiles):
                        for pair in range(2):
                            s = probs[:, buf, e, (2 * x + pair) * keys:(2 * x + pair + 1) * keys]
                            o = o_ext[:, buf, x, 2 * pair + e, :]
                            ins = act.activation(s, s, ACT.Exp, bias=o[:, HD + 1:HD + 2], accum_out=o[:, HD:HD + 1])
                    ins.then_inc(exps, 1)
                for e in range(2):
                    ps = full(pl, 4 + e)[:, 0:tiles * 2 * HD].rearrange("p (x d) -> p x d", d=HD)
                    o = o_ext[:, buf, 0:tiles].rearrange("p x h d -> p (x h) d")[:, e::2, 0:HD]
                    empty(act.activation(o, ps, ACT.Copy), 4 + e)
                for e in range(2):
                    act.wait_ge(task_free[e], pl.half(4 + e) + 1)
                act.wait_ge(exps, nth * 2 + 2)
                act.dma_start(dst, o_ext[:, buf, 0:tiles].rearrange("p x h d -> p x (h d)")).then_inc(rows_stored[buf], 16)

            def rows0(t):
                return att_rows[0].rearrange("(t p) d -> p t d", p=P)[:, ds(t, 1)]

            def rows1(half, t, n):
                return att_rows[1].rearrange("(f p t) d -> p f t d", f=2, t=4)[:, half, ds(t, n)]

            def rows2(t):
                return att_rows[2].rearrange("(p t) d -> p t d", t=8)[:, ds(t, 2)]

            for j in range(2):
                if j:
                    prep(Place(T_PREP0), 0)
                in_place(Place(U_GATE3), j, ACT.Silu)
            tile(Place(T_TILE0), 0, 0, 0, 0, False, 1, rows0(0))
            with act.Fori(0, 3) as i:
                for x in range(2):
                    tile(Place(T_TILES0 + 6 * x, 12, i), 0, i * 2 + (1 + x), i * 2 + (1 + x), (1 + x) % 2, True, 1,
                         rows0(i * 2 + (1 + x)))
                    for j in range(2):
                        spill(Place(U_GROUPS + 2 * x, 4, i), j,
                              att_spill[ds(i * 4 + (6 + 2 * x + j), 1)].rearrange("a p t -> p (a t)"))
            tile(Place(T_TILES0 + 36), 0, 7, 7, 1, True, 1, rows0(7))

            def next_group(g, nth):
                act.wait_ge(window, nth)
                act.wait_ge(peak, 2 * nth)
                load_group(g)

            def gate(pl, j, m):
                in_place(pl, j, ACT.Sigmoid)
                act.wait_ge(silu_done, m * 2 + (2 * HEADS + j + 1))
                act.dma_start(gate_spill[ds(m * 2 + j, 1)].rearrange("a p t -> p (a t)"), stage[:, j, :]).then_inc(spilled[j], 16)

            next_group(1, 8)
            prep(Place(T_PREP1), 1)
            with act.Fori(0, 1) as i:
                for x in range(2):
                    tile(Place(T_FREE1 + 6 * x, 12, i), 1, 2 * x, i + (8 + x), x, False, 2, rows1(0, 2 * x, 2))
                    for j in range(2):
                        gate(Place(U_GATES + 2 * x, 4, i), j, i * 2 + x)
            with act.Fori(0, 2) as i:
                for x in range(2):
                    tile(Place(T_PREV1 + 6 * x, 12, i), 1, i * 2 + x, i * 2 + (10 + x), x, True, 1, rows1(1, i * 2 + x, 1))
                    gate(Place(U_GATES + 4, 2, i), x, i + 2)
            next_group(2, 14)
            prep(Place(T_PREP2), 2)
            with act.Fori(0, 2) as i:
                for x in range(2):
                    tile(Place(T_FREE2 + 6 * x, 12, i), 2, i * 4 + 2 * x, i * 2 + (14 + x), x, False, 2, rows2(i * 4 + 2 * x))
                    for j in range(2):
                        gate(Place(U_GATES + 8 + 2 * x, 4, i), j, i * 2 + (4 + x))

            act.wait_ge(v_stored, 16 * GROUPS)
            for x in range(2):
                act.wait_ge(k_stored[x], 16 * K_STORES[GROUPS][x])
            for x in range(2):
                act.wait_ge(spilled[x], 16 * 17)
                act.wait_ge(rows_stored[x], 16 * 9)
            act.dma_start(s_qkv_t[:], att_spill[:, :, SEQ:TOKENS].rearrange("a p t -> p a t")).then_inc(qkv_loaded, 16)
            act.dma_start(kv_a[:], a["cache_kv_w128"][0].rearrange("n r c h d -> r n c (h d)")).then_inc(cache_loaded, 16)
            for name, by, r0, r1 in (("cache_kv_w512", 4, 0, ROWS_B1), ("cache_kv_w2048", 16, ROWS_B1, ROWS_B1 + ROWS_B2)):
                act.dma_start(kv_b[r0:r1], a[name][0].rearrange("n (r s) c h d -> r s n c (h d)", s=by)[:, 0]).then_inc(cache_loaded, 16)
            pl = Place(T_SAMPLE)
            for j in range(6):
                ps = full(pl, j)
                c, n = (0, 512) if j % 2 == 0 else (512, 256)
                empty(act.activation(s_qkv[:, j // 2, c:c + n], ps[0:SAMPLES, 0:n], ACT.Copy), j)
            for b in range(2):
                act.wait_ge(task_free[b], pl.half(4 + b) + 1)
            act.dma_start(sample_rows.rearrange("a n c -> n a c"), s_qkv[:]).then_inc(rows_written, 16)
            for g in range(GROUPS):
                act.dma_start(s_kv[g][0, :, 0].rearrange("n c h d -> n c (h d)"),
                              s_qkv[:, 1:3, g * 256:(g + 1) * 256]).then_inc(smp_out, 16)
            act.wait_ge(rows_written, 16)
            r2 = ROWS_B1 + ROWS_B2
            act.dma_start(q_a[:], sample_rows[0, :, 0:256].partition_broadcast(P)).then_inc(cache_loaded, 16)
            act.dma_start(q_b[0:ROWS_B1], sample_rows[0, :, 256:512].partition_broadcast(ROWS_B1)).then_inc(cache_loaded, 16)
            act.dma_start(q_b[ROWS_B1:r2], sample_rows[0, :, 512:768].partition_broadcast(ROWS_B2)).then_inc(cache_loaded, 16)
            by_group = sample_rows.rearrange("a n (g c) -> a g n c", g=GROUPS)
            act.dma_start(q_b[r2:ROWS_B], by_group[0]).then_inc(cache_loaded, 16)
            for c in range(2):
                act.dma_start(kv_b[r2:ROWS_B, :, c, :], by_group[1 + c]).then_inc(cache_loaded, 16)
            act.wait_ge(smp_act, 1)
            act.activation(s_prob[:], s_prob[:], ACT.Exp, bias=s_small[:, 0:1], accum_out=s_small[:, 1:2]).then_inc(root, 1)

            for b in range(2):
                act.wait_ge(task_free[b], T_MERGE // 2)
            act.wait_ge(smp_out, 16 * GROUPS)
            for g in range(GROUPS):
                act.dma_start(parts[:, g].rearrange("p (t h) d -> p t (h d)", h=AH),
                              att_rows[g].rearrange("(t p) d -> p t d", p=P)).then_inc(parts_loaded, 16)
            act.wait_ge(mrg_dve, 1)
            act.activation(mrg[:, 0:3, :], mrg[:, 0:3, :], ACT.Exp).then_inc(mrg_act, 1)

            for m in range(KT):
                act.wait_ge(unit_free[m % 2], Place(U_OUT).half(m) + 1)
                act.wait_ge(summed, m + KT)
                act.activation(temp[:, 2, :], wide[:, m, :], ACT.Square).then_inc(squared, 1)
            norm_root(Place(T_NORM2))
            for c, nf in enumerate(FF_CHUNKS):
                with act.Fori(0, nf) as f:
                    act.wait_ge(unit_free[0], Place(U_FFN_CHUNK[c], 2, f).half(0) + 1)
                    act.activation(temp[:, 0, :], temp[:, 0, :], ACT.Silu).then_inc(silu_done, 1)
            for t in range(CHUNKS + 1):
                n, g = P if t < CHUNKS else SAMPLES, t % 2
                act.wait_ge(unit_done, U_FINAL + t + 1)
                if t:
                    act.wait_ge(act_step, 2 * t)
                act.activation(y_square[0:n, :].rearrange("p (a b) -> p a b", a=2), unit_ps[g][0:n, 0:2, :], ACT.Square,
                               accum_out=fin[0:n, g, 0:1]).then_inc(act_step, 1)
                act.wait_ge(act_step, 2 * t + 1)
                act.activation(fin[0:n, g, 0:1], fin[0:n, g, 0:1], ACT.Sqrt, scale=1.0 / D, bias=const("eps", n)[:, 0:1])\
                   .then_inc(act_step, 1)

        @block.vector
        def _(dve):
            step = Steps(dve, dve_step)

            def full(pl, j):
                dve.wait_ge(task_done[j % 2], pl.half(j) + 1)
                return task_ps[j % 2]

            def empty(ins, j):
                ins.then_inc(task_free[j % 2], 1)

            def take(pl, j):
                dve.wait_ge(unit_done, pl.n(j) + 1)
                return unit_out(j % 2)

            def scaled(pl, j, dst, by=None):
                ps = take(pl, j)
                if by is None:
                    ins = dve.tensor_tensor(pieces(dst), ps, pieces(rstd[:]), ALU.mult)
                else:
                    ins = dve.scalar_tensor_tensor(out=pieces(dst), in0=ps, scalar=by, in1=pieces(rstd[:]),
                                                   op0=ALU.mult, op1=ALU.mult)
                ins.then_inc(unit_free[j % 2], 1)

            def norm_factor(tasks):
                for b in range(2):
                    dve.wait_ge(task_free[b], tasks // 2)
                dve.reciprocal(rstd[:], rstd[:]).then_inc(rstd_ready, 1)

            dve.wait_ge(const_loaded, 16 * 2)
            for b in range(2):
                dve.wait_ge(task_free[b], CHUNKS + 1)
            for k in range(KT):
                step(dve.tensor_scalar(a_hi[:, k, :], wide[:, k, :], gains[:, 0, k:k + 1], None, ALU.mult))
                step.settle()
                dve.scalar_tensor_tensor(out=a_lo[:, k, :], in0=wide[:, k, :], scalar=gains[:, 0, k:k + 1],
                                         in1=a_hi[:, k, :].bitcast(F32), op0=ALU.mult, op1=ALU.subtract).then_inc(a_ready, 1)
            norm_factor(T_RET)
            dve.wait_ge(rstd_ready, 1)
            scaled(Place(0), 0, v_t[:, 0, :])
            scaled(Place(0), 1, v_t[:, 1, :])
            scaled(Place(0), 2, k_t[:])
            scaled(Place(0), 3, q_t[:], DK ** -0.5)
            dve.wait_ge(table_loaded, 16 * 2)
            dve.wait_ge(x_spilled, 16)

            def ret_slot(pl, h, j):
                if j < 2:
                    empty(dve.tensor_scalar(k_tok[:, 4 * j:4 * j + 4, :],
                                            full(pl, KT_ + j)[:].rearrange("p (q d) -> p q d", q=4),
                                            const("tail")[:, ds(h, 1)], None, ALU.mult), KT_ + j)
                if j == 1:
                    dve.wait_ge(task_free[KS % 2], pl.half(KS) + 1)
                    eye = const("eye8").rearrange("p (a b) -> p a b", a=SAMPLES)
                    dve.tensor_tensor(s_kmask[:], s_ktok[:].unsqueeze(1).to_broadcast([SAMPLES, SAMPLES, DK]),
                                      masks8().to_broadcast([SAMPLES, SAMPLES, DK]), ALU.mult)
                    dve.tensor_tensor(s_qmask[:], q_t[:, SEQ:TOKENS].unsqueeze(2).to_broadcast([P, SAMPLES, SAMPLES]),
                                      eye, ALU.mult).then_inc(masked_ready, 1)
                    for x in range(2):
                        ps = full(pl, SC + x)[:].rearrange("p (q t) -> p q t", q=4)
                        empty(dve.tensor_tensor(scores_t[:, 4 * x:4 * x + 4, :], ps,
                                                decay[:, ds(h, 1), :].to_broadcast([P, 4, P]), ALU.mult), SC + x)
                    q = q_t[:, 0:SEQ].rearrange("p (n t) -> p n t", t=P)
                    dve.tensor_tensor(q, q, inner[:, ds(h, 1), :].to_broadcast([P, CHUNKS, P]), ALU.mult).then_inc(q_ready, 1)
                if j in (1, 2):
                    for x in (range(UP, UP + 3) if j == 1 else (UP + 3,)):
                        ps = full(pl, x)
                        if x == UP:
                            wait(dve, p_stored, h * 16)
                        for q in range(2):
                            n = 2 * (x - UP) + q
                            u = ps[:, q * DV:(q + 1) * DV]
                            if n == 0:
                                ins = dve.tensor_copy(states[:, 0, :], u)
                            else:
                                ins = dve.scalar_tensor_tensor(out=states[:, n, :], in0=states[:, n - 1, :],
                                                               scalar=const("gamma_c")[:, ds(h, 1)], in1=u,
                                                               op0=ALU.mult, op1=ALU.add)
                            if q == 0:
                                step(ins)
                                step.settle()
                            else:
                                empty(ins, x)
                                dve.wait_ge(task_free[x % 2], pl.half(x) + 1)
                if j in (2, 3):
                    for x in (range(OUTER, OUTER + 3) if j == 2 else (OUTER + 3,)):
                        if x == OUTER:
                            dve.wait_ge(s_loaded, h * 16 + 16)
                        s = s_state[:, 2 * (x - OUTER):2 * (x - OUTER) + 2, :]
                        ps = full(pl, x)[:].rearrange("p (q d) -> p q d", q=2)
                        empty(dve.scalar_tensor_tensor(out=s, in0=s, scalar=const("gamma")[:, ds(h, 1)], in1=ps,
                                                       op0=ALU.mult, op1=ALU.add), x)
                if j == 3:
                    for x in (OUT_ + 2, OUT_ + 3, OS):
                        dve.wait_ge(task_free[x % 2], pl.half(x) + 1)
                    rows = [(o_tok[:, n, :], P) for n in range(CHUNKS)] + [(s_otok[:], SAMPLES)]
                    for n, (o, r) in enumerate(rows):
                        step(dve.bn_stats(stats[0:r, n, :], o))
                    step.settle()
                    dve.memset(spread[:], 1.0)
                    for n, (o, r) in enumerate(rows):
                        ins = dve.bn_aggr(moments[0:r, n, :], stats[0:r, n, :])
                        if n < CHUNKS:
                            step(ins)
                    ins.then_inc(normed, 1)
                    dve.wait_ge(root, h + 1)
                    step(dve.reciprocal(spread[:, 0:CHUNKS], spread[:, 0:CHUNKS]))
                    step(dve.reciprocal(spread[0:SAMPLES, CHUNKS:CHUNKS + 1], spread[0:SAMPLES, CHUNKS:CHUNKS + 1]))
                    step.settle()
                    dve.wait_ge(normed, h * 2 + 1)
                    for n, (o, r) in enumerate(rows):
                        ins = dve.tensor_scalar(o, o, moments[0:r, n, 0:1], spread[0:r, n:n + 1], ALU.subtract, ALU.mult)
                    ins.then_inc(normed, 1)
                if j == 4:
                    for x in range(4):
                        ps = full(pl, TURN + x)[:].rearrange("p (v t) -> p v t", v=2)
                        empty(dve.tensor_copy(wide[:, ds(h * 2, 2), 2 * P * x:2 * P * (x + 1)], ps), TURN + x)
                    ps = full(pl, TS)[:, 0:2 * SAMPLES].rearrange("p (v t) -> p v t", v=2)
                    empty(dve.tensor_copy(wide[:, ds(h * 2, 2), SEQ:TOKENS], ps), TS)

            def masks8():
                return const("ident", SAMPLES)[:, 0:SAMPLES].unsqueeze(2)

            def gated(pl, j, h, v, done):
                scaled(pl, j, stage[:, j % 2, :])
                dve.wait_ge(silu_done, done)
                for b in range(2):
                    dve.wait_ge(task_free[b], h * (RET_TASKS // 2) + (T_RET + RET_TASKS) // 2)
                t = flat(wide[:, ds(h * 2 + v, 1), :])
                step(dve.tensor_tensor(t, t, stage[:, j % 2, :], ALU.mult))

            with dve.Fori(0, HEADS - 1) as h:
                step.enter(h, STEPS_HEAD)
                up = Place(U_HEADS, 6, h)
                for j in range(6):
                    ret_slot(Place(T_RET, RET_TASKS, h), h, j)
                    if j < 2:
                        scaled(up, j, v_t[:, j, :])
                    elif j == 2:
                        scaled(up, j, k_t[:])
                    elif j == 3:
                        scaled(up, j, q_t[:], DK ** -0.5)
                    else:
                        gated(up, j, h, j - 4, h * 2 + (j - 3))
                step.leave(HEADS - 1)

            def staged(pl, j, before):
                wait(dve, spilled[j % 2], before)
                scaled(pl, j, stage[:, j % 2, :])

            for j in range(6):
                ret_slot(Place(T_RET + RET_TASKS * (HEADS - 1)), HEADS - 1, j)
                staged(Place(U_GROUP0), j, 16 * (j // 2))
            for j in range(2):
                dve.wait_ge(spilled[j], 16 * 3)
                gated(Place(U_GATE3), j, HEADS - 1, j, 2 * (HEADS - 1) + j + 1)

            def tile(pl, g, nth, buf, prev, tiles, stored):
                wait(dve, rows_stored[buf], stored)
                keys = 2 * P if prev else P
                n = 2 * tiles
                for e in range(2):
                    ps = full(pl, e)[:, 0:n * keys]
                    s = probs[:, buf, e, 0:n * keys]
                    o = o_ext[:, buf, 0:tiles].rearrange("p x h d -> p (x h) d")[:, e::2, HD + 1:HD + 2]
                    if g == 2:
                        b = bias[:, 0:512].rearrange("p (e a k) -> p e a k", e=2, a=2)[:, e]
                    else:
                        b = bias[:].rearrange("p (e a k) -> p e a k", e=2, a=2)[:, e, :, 2 * P - keys:2 * P]
                    if tiles == 2:
                        b = b.unsqueeze(1).to_broadcast([P, 2, 2, P])
                        ps, sx = (y.rearrange("p (t a k) -> p t a k", t=2, a=2) for y in (ps, s))
                    else:
                        ps, sx = (y.rearrange("p (a k) -> p a k", a=2) for y in (ps, s))
                    empty(dve.tensor_tensor(sx, ps, b, ALU.add), e)
                    dve.wait_ge(task_free[e], pl.half(e) + 1)
                    dve.tensor_reduce(o, s.rearrange("p (x k) -> p x k", k=keys), AX_X, ALU.max, negate=True).then_inc(peak, 1)
                for e in range(2):
                    ps = full(pl, 2 + e)[:, 0:n * keys]
                    empty(dve.tensor_copy(probs_t[:, buf, e].rearrange("p x t -> p (x t)")[:, 0:n * keys], ps), 2 + e)

            dve.wait_ge(att_loaded, 16 * 2)
            tile(Place(T_TILE0), 0, 0, 0, False, 1, 0)
            with dve.Fori(0, 3) as i:
                for x in range(2):
                    tile(Place(T_TILES0 + 6 * x, 12, i), 0, None, (1 + x) % 2, True, 1, i * 16 + 16 * x)
                    for j in range(2):
                        staged(Place(U_GROUPS + 2 * x, 4, i), j, i * 32 + 16 * (3 + x))
            tile(Place(T_TILES0 + 36), 0, 7, 1, True, 1, 16 * 3)
            dve.wait_ge(att_loaded, 16 * 4)
            with dve.Fori(0, 1) as i:
                for x in range(2):
                    tile(Place(T_FREE1 + 6 * x, 12, i), 1, None, x, False, 2, i + 16 * 4)
                    for j in range(2):
                        staged(Place(U_GATES + 2 * x, 4, i), j, i + 16 * (9 + x))
            with dve.Fori(0, 2) as i:
                for x in range(2):
                    tile(Place(T_PREV1 + 6 * x, 12, i), 1, None, x, True, 1, i * 16 + 16 * 5)
                    staged(Place(U_GATES + 4, 2, i), x, i * 16 + 16 * 11)
            dve.wait_ge(att_loaded, 16 * 6)
            with dve.Fori(0, 2) as i:
                for x in range(2):
                    tile(Place(T_FREE2 + 6 * x, 12, i), 2, None, x, False, 2, i * 16 + 16 * 7)
                    for j in range(2):
                        staged(Place(U_GATES + 8 + 2 * x, 4, i), j, i * 32 + 16 * (13 + x))

            dve.wait_ge(unit_done, U_BRANCH)
            step.settle()
            for k in range(KT):
                step(dve.tensor_copy(a_hi[:, k, :], wide[:, k, :]))
                step.settle()
                dve.tensor_tensor(a_lo[:, k, :], wide[:, k, :], a_hi[:, k, :].bitcast(F32), ALU.subtract).then_inc(a_ready, 1)

            pl = Place(T_SAMPLE)
            dve.wait_ge(cache_loaded, 16 * 9)
            for x, (q, kv, r) in enumerate(((q_a, kv_a, P), (q_b, kv_b, ROWS_B))):
                step(dve.tensor_tensor(q[:], q[:], kv[:, :, 0, :], ALU.mult))
                step.settle()
                ins = dve.tensor_reduce(s_score[0:r, x, :], q[:].rearrange("p n (h d) -> p (n h) d", d=HD), AX_X, ALU.add)
                if x == 0:
                    step(ins)
            ins.then_inc(smp_dve, 1)
            ps = full(pl, 6)
            step(dve.scalar_tensor_tensor(out=s_prob[:, 0:P], in0=ps[0:32, 0:P], scalar=HD ** -0.5, in1=const("bias_sa", 32),
                                          op0=ALU.mult, op1=ALU.add))
            empty(dve.scalar_tensor_tensor(out=s_prob[:, P:P + ROWS_B], in0=ps[0:32, P:P + ROWS_B], scalar=HD ** -0.5,
                                           in1=const("bias_sb", 32), op0=ALU.mult, op1=ALU.add), 6)
            dve.wait_ge(task_free[0], pl.half(6) + 1)
            dve.tensor_reduce(s_small[:, 0:1], s_prob[:], AX_X, ALU.max, negate=True).then_inc(smp_act, 1)
            dve.wait_ge(root, HEADS + 1)
            step(dve.reciprocal(s_small[:, 2:3], s_small[:, 1:2]))
            step.settle()
            dve.tensor_scalar(s_prob[:], s_prob[:], s_small[:, 2:3], None, ALU.mult).then_inc(smp_dve, 1)
            ps = full(pl, 7)
            step(dve.tensor_copy(s_ptok[:, 0, :], ps[:, 0:32]))
            empty(dve.tensor_copy(s_ptok[0:ROWS_B, 1, :], ps[0:ROWS_B, 32:64]), 7)
            for pair in range(2):
                ps = full(pl, 8 + pair)[:, 0:2 * SAMPLES].rearrange("p (n e) -> p e n", e=2)
                for e in range(2):
                    half = slice(64 * e, 64 * e + 64)
                    step(dve.tensor_copy(ao_hi[half, pair, SEQ:TOKENS], ps[half, e, :]))
                step.settle()
                for e in range(2):
                    half = slice(64 * e, 64 * e + 64)
                    ins = dve.tensor_tensor(ao_lo[half, pair, SEQ:TOKENS], ps[half, e, :],
                                            ao_hi[half, pair, SEQ:TOKENS].bitcast(F32), ALU.subtract)
                    if e == 0:
                        step(ins)
                empty(ins, 8 + pair)

            dve.wait_ge(parts_loaded, 16 * GROUPS)
            low = mrg[:, 6, :].unsqueeze(2)
            minus = [parts[:, g, :, HD + 1:HD + 2] for g in range(GROUPS)]
            total = [parts[:, g, :, HD:HD + 1] for g in range(GROUPS)]
            step(dve.tensor_tensor(low, minus[0], minus[1], ALU.min))
            step.settle()
            step(dve.tensor_tensor(low, low, minus[2], ALU.min))
            step.settle()
            for g in range(GROUPS):
                ins = dve.tensor_tensor(mrg[:, g, :].unsqueeze(2), low, minus[g], ALU.subtract)
                if g < GROUPS - 1:
                    step(ins)
            ins.then_inc(mrg_dve, 1)
            dve.wait_ge(mrg_act, 1)
            for g in range(GROUPS):
                step(dve.tensor_tensor(mrg[:, 3 + g, :].unsqueeze(2), mrg[:, g, :].unsqueeze(2), total[g], ALU.mult))
            step.settle()
            for g in (1, 2):
                step(dve.tensor_tensor(mrg[:, 3, :], mrg[:, 3, :], mrg[:, 3 + g, :], ALU.add))
                step.settle()
            step(dve.reciprocal(mrg[:, 7, :], mrg[:, 3, :]))
            step.settle()
            for g in range(GROUPS):
                step(dve.tensor_tensor(mrg[:, g, :], mrg[:, g, :], mrg[:, 7, :], ALU.mult))
            step.settle()
            ao = ao_tok[:].rearrange("p t (h d) -> p (t h) d", d=HD)
            for g in range(GROUPS):
                by = mrg[:, g, :].unsqueeze(2).to_broadcast([P, CHUNKS * AH, HD])
                step(dve.tensor_tensor(prod[:] if g else ao, parts[:, g, :, 0:HD], by, ALU.mult))
                step.settle()
                if g:
                    ins = dve.tensor_tensor(ao, ao, prod[:], ALU.add)
                    if g == 1:
                        step(ins)
                        step.settle()
            ins.then_inc(mrg_dve, 1)
            for j in range(4):
                ps = full(Place(T_MERGE), j)[:].rearrange("p (a t) -> p a t", a=2)
                c = slice(2 * P * j, 2 * P * (j + 1))
                step(dve.tensor_copy(ao_hi[:, :, c], ps))
                step.settle()
                empty(dve.tensor_tensor(ao_lo[:, :, c], ps, ao_hi[:, :, c].bitcast(F32), ALU.subtract), j)

            with dve.Fori(0, KT // 2) as i:
                step.enter(i, STEPS_BRANCH)
                for x in range(2):
                    pl = Place(U_BRANCH + 2 * x, 4, i)
                    m = i * 2 + x
                    dve.wait_ge(gate_loaded[x], i * 16 + 16)
                    for j in range(2):
                        ps = take(pl, j)
                        dve.tensor_tensor(pieces(wide[:, 4 + j, :]), ps, pieces(wide[:, 2 * x + j, :]), ALU.mult)\
                           .then_inc(unit_free[j], 1)
                    for j in range(2):
                        dve.wait_ge(unit_free[j], pl.half(j) + 1)
                    step(dve.tensor_tensor(wide[:, 4, :], wide[:, 4, :], wide[:, 5, :], ALU.add))
                    step.settle()
                    hi, lo = flat(b_hi[:, ds(m, 1), :]), flat(b_lo[:, ds(m, 1), :])
                    step(dve.tensor_copy(hi, wide[:, 4, :]))
                    step.settle()
                    dve.tensor_tensor(lo, wide[:, 4, :], hi.bitcast(F32), ALU.subtract).then_inc(b_ready, 1)
                    dve.wait_ge(b_ready, m + 1)
                step.leave(KT // 2)

            dve.wait_ge(unit_done, U_OUT)
            step(dve.memset(temp[:, 3, :], 0.0))
            step.settle()
            with dve.Fori(0, KT // 2) as i:
                step.enter(i, STEPS_OUT)
                for j in range(2):
                    m = i * 2 + j
                    ps = take(Place(U_OUT, 2, i), j)
                    dve.wait_ge(x_back[j], i * 16 + 16)
                    x2 = flat(wide[:, ds(m, 1), :])
                    hi, lo = flat(a_hi[:, ds(m, 1), :]), flat(a_lo[:, ds(m, 1), :])
                    g = gains[:, 1, ds(m, 1)]
                    dve.tensor_tensor(pieces(x2), ps, pieces(temp[:, j, :]), ALU.add).then_inc(unit_free[j], 1)
                    dve.wait_ge(unit_free[j], Place(U_OUT, 2, i).half(j) + 1)
                    step(dve.tensor_scalar(hi, x2, g, None, ALU.mult))
                    step.settle()
                    dve.scalar_tensor_tensor(out=lo, in0=x2, scalar=g, in1=hi.bitcast(F32), op0=ALU.mult, op1=ALU.subtract)\
                       .then_inc(a_ready, 1)
                    dve.wait_ge(squared, m + (KT + 1))
                    dve.wait_ge(summed, m + KT)
                    dve.tensor_tensor(temp[:, 3, :], temp[:, 3, :], temp[:, 2, :], ALU.add).then_inc(summed, 1)
                step.leave(KT // 2)
            norm_factor(T_END)
            dve.wait_ge(rstd_ready, 2)

            for c, nf in enumerate(FF_CHUNKS):
                f0 = sum(FF_CHUNKS[:c])
                with dve.Fori(0, nf) as f:
                    step.enter(f, STEPS_FFN)
                    pl = Place(U_FFN_CHUNK[c], 2, f)
                    for j in range(2):
                        scaled(pl, j, temp[:, j, :])
                    dve.wait_ge(unit_free[1], pl.half(1) + 1)
                    dve.wait_ge(silu_done, f + (2 * HEADS + 2 * KT + f0 + 1))
                    step(dve.tensor_tensor(temp[:, 2, :], temp[:, 0, :], temp[:, 1, :], ALU.mult))
                    step.settle()
                    hi, lo = flat(b_hi[:, ds(f, 1), :]), flat(b_lo[:, ds(f, 1), :])
                    step(dve.tensor_copy(hi, temp[:, 2, :]))
                    step.settle()
                    dve.tensor_tensor(lo, temp[:, 2, :], hi.bitcast(F32), ALU.subtract).then_inc(b_ready, 1)
                    step.leave(nf)
                with dve.Fori(0, KT // 2) as i:
                    for j in range(2):
                        ps = take(Place(U_FFN_CHUNK[c] + 2 * nf, 2, i), j)
                        x = pieces(flat(wide[:, ds(i * 2 + j, 1), :]))
                        dve.tensor_tensor(x, ps, x, ALU.add).then_inc(unit_free[j], 1)

            dve.wait_ge(gain_loaded, 16)
            for t in range(CHUNKS + 1):
                n, g = P if t < CHUNKS else SAMPLES, t % 2
                dve.wait_ge(act_step, 2 * t + 2)
                wait(dve, y_stored[g], 16 * (t // 2))
                step(dve.reciprocal(fin[0:n, g, 1:2], fin[0:n, g, 0:1]))
                step.settle()
                ps = unit_ps[g][0:n, 0:2, :]
                dve.scalar_tensor_tensor(out=y_row[0:n, g, :].rearrange("p (a b) -> p a b", a=2), in0=ps,
                                         scalar=fin[0:n, g, 1:2], in1=gain_row[0:n, :].rearrange("p (a b) -> p a b", a=2),
                                         op0=ALU.mult, op1=ALU.mult).then_inc(unit_free[g], 1)


_INS = ["x_prompt", "x_sample", "state_ret", "cache_kv_w128", "cache_kv_w512", "cache_kv_w2048", "w_in",
        "w_ret_branch", "w_att_branch", "w_out", "w_gate_up", "w_down", "norm_final"]
_OUTS = [("y_prompt", (1, SEQ, D)), ("y_sample", (SAMPLES, 1, D)), ("p_ret", (1, 1, HEADS, DK, DV)),
         ("p_kv_w128", (1, 1, KEPT[0], 2, AH, HD)), ("p_kv_w512", (1, 1, KEPT[1], 2, AH, HD)),
         ("p_kv_w2048", (1, 1, KEPT[2], 2, AH, HD)), ("s_ret", (1, SAMPLES, HEADS, DK, DV)),
         ("s_kv_w128", (1, SAMPLES, 1, 2, AH, HD)), ("s_kv_w512", (1, SAMPLES, 1, 2, AH, HD)),
         ("s_kv_w2048", (1, SAMPLES, 1, 2, AH, HD))]


def kernel(**inputs):
    import concourse.bacc as bacc
    from concourse.bass_utils import run_bass_kernel_spmd

    nc = bacc.Bacc("TRN2", target_bir_lowering=False, num_devices=1)
    arrays, ins = {}, {}
    for name in _INS:
        arrays[f"in_{name}"] = np.ascontiguousarray(inputs[name])
    arrays["in_norm_gains"] = np.ascontiguousarray(
        np.stack([np.asarray(inputs[n])[0].reshape(KT, P).T for n in ("norm_mix", "norm_ffn")], 1))
    for name, table in tables().items():
        arrays[f"in_{name}"] = table
    for key, x in arrays.items():
        ins[key[3:]] = nc.dram_tensor(key, x.shape, F32, kind="ExternalInput").ap()
    outs = {name: nc.dram_tensor(f"out_{name}", shape, F32, kind="ExternalOutput").ap() for name, shape in _OUTS}
    build(nc, ins, outs)
    r = run_bass_kernel_spmd(nc, [arrays], core_ids=[0])
    return tuple(r.results[0][f"out_{name}"] for name, _ in _OUTS)
```

```python
from contextlib import ExitStack

import numpy as np
import concourse.bass as bass
from concourse import mybir

F32 = mybir.dt.float32
F32R = mybir.dt.float32r
ALU = mybir.AluOpType
ACT = mybir.ActivationFunctionType
AX_X = mybir.AxisListType.X
ds = bass.ds

P = 128
D = 1024
SEQ = 1024
SAMPLES = 8
TOKENS = SEQ + SAMPLES
PIECES = 3
PIECE = TOKENS // PIECES
KT = D // P
HEADS, DK, DV = 4, 128, 256
CHUNKS = SEQ // P
GROUPS = 3
DILATION = (1, 4, 16)
KEPT = (128, 512, 1024)
AH, HD = 4, 64
PAST = (128, 256, 256)
D_FF = 2816
D_IN = 7424
COL_RQ, COL_RK, COL_RV, COL_RG = 0, 512, 1024, 2048
COL_ATT, COL_GATE_R, COL_GATE_A = 3072, 5376, 6400
KIND = 768
RMS_EPS, GN_EPS = 1e-6, 1e-5
MASKED = -1e30
ROWS_B1, ROWS_B2 = 64, 16
ROWS_B = ROWS_B1 + ROWS_B2 + GROUPS
OUT_ROW = AH * (HD + 2)

U_HEAD0 = 0
U_HEADS = 4
U_GROUP0 = U_HEADS + 6 * (HEADS - 1)
U_GATE3 = U_GROUP0 + 6
U_GATE0 = U_GATE3 + 2
U_GROUPS = U_GATE0 + 2
U_GATES = U_GROUPS + 12
U_BRANCH = U_GATES + 14
U_ATT = U_BRANCH + 8
U_OUT = U_ATT + 8
U_FFN = U_OUT + 8
FF_CHUNKS = (8, 7, 7)
T_NORM1 = 18
T_RET = T_NORM1 + 4
RET_TASKS = 28
T_ATT = T_RET + HEADS * RET_TASKS
PREP = (6, 6, 8)
TILE_TASKS = 6
T_PREP0 = T_ATT
T_TILE0 = T_PREP0 + PREP[0]
T_TILES0 = T_TILE0 + TILE_TASKS
T_PREP1 = T_TILES0 + 7 * TILE_TASKS
T_FREE1 = T_PREP1 + PREP[1]
T_PREV1 = T_FREE1 + 2 * TILE_TASKS
T_PREP2 = T_PREV1 + 4 * TILE_TASKS
T_FREE2 = T_PREP2 + PREP[2]
T_SAMPLE = T_FREE2 + 4 * TILE_TASKS
T_MERGE = T_SAMPLE + 10
T_NORM2 = T_MERGE + 4
T_END = T_NORM2 + 4
U_FFN_CHUNK = [U_FFN + sum(2 * n + 8 for n in FF_CHUNKS[:c]) for c in range(len(FF_CHUNKS) + 1)]
U_FINAL = U_FFN_CHUNK[-1]

VT, VS, KT_, KS, SC, UP, OUT_, OUTER, OS, TURN, TS = 0, 4, 5, 7, 8, 10, 14, 18, 22, 23, 27
RET_AT = {(0, 2 + j): j for j in range(6)}
RET_AT.update({(1, 0): 6, (1, 1): 7, (1, 2): 8, (1, 3): 9, (1, 5): 10, (1, 6): 11, (1, 7): 12, (2, 0): 13})
RET_AT.update({(2, 1 + j): 14 + j for j in range(7)})
RET_AT.update({(3, 0): 21, (3, 3): 22, (4, 0): 23, (4, 1): 24, (4, 2): 25, (4, 3): 26, (4, 4): 27})
TILE_AT = (1, 2, 5, 6, 7, 8)
STEPS_HEAD, STEPS_OUT, STEPS_FFN = 25, 2, 2
X_NORM = ((0, 1, 2), (3, 4, 5), (6, 7), (8,))
LATE_AT = ((0, 3), (0, 4), (0, 5), (0, 6), (0, 7), (0, 8), (3, 4), (3, 7), (4, 1), (4, 2), (7, 5), (7, 6), (7, 7), (7, 8))
K_STORES = ((0, 0), (0, 1), (1, 2), (3, 4))

CONSTS = {}
_at = 0
for _name, _n in (("ident", P), ("ones", P), ("eye8", 64), ("tail", HEADS), ("gamma_c", HEADS),
                  ("gamma", HEADS), ("eps", 2), ("bias_sa", P), ("bias_sb", ROWS_B)):
    CONSTS[_name] = (_at, _n)
    _at += _n
N_CONST = _at


def tables():
    f = np.float32
    log_gamma = np.log1p(-np.exp2(f(-5.0) - np.arange(HEADS, dtype=f))).astype(f)
    idx = np.arange(P, dtype=f)
    diff = idx[None, :] - idx[:, None]
    decay = np.where(diff[:, None, :] >= 0,
                     np.exp(np.maximum(diff, 0)[:, None, :] * log_gamma[None, :, None]), 0).astype(f)
    inner = np.exp((idx + 1)[None, :] * log_gamma[:, None]).astype(f)
    inner = np.broadcast_to(inner[None], (P, HEADS, P))
    slopes = np.exp2(f(-8.0) * (np.arange(GROUPS * AH, dtype=f) + 1) / f(GROUPS * AH)).astype(f)
    slopes = slopes.reshape(GROUPS, AH)
    parts = {
        "ident": np.eye(P), "ones": np.ones((P, P)),
        "eye8": np.broadcast_to(np.eye(8).reshape(1, 64), (P, 64)),
        "tail": np.exp((P - 1 - idx)[:, None] * log_gamma[None]),
        "gamma_c": np.broadcast_to(np.exp(P * log_gamma)[None], (P, HEADS)),
        "gamma": np.broadcast_to(np.exp(log_gamma)[None], (P, HEADS)),
        "eps": np.broadcast_to(np.array([[RMS_EPS, GN_EPS]]), (P, 2)),
    }
    sa, sb = np.zeros((P, P)), np.zeros((P, ROWS_B))
    for n in range(SAMPLES):
        for h in range(AH):
            row = n * AH + h
            sa[row] = -slopes[0, h] * (P - np.arange(P))
            sb[row, :ROWS_B1] = -slopes[1, h] * (PAST[1] - 4 * np.arange(ROWS_B1))
            sb[row, ROWS_B1:ROWS_B1 + ROWS_B2] = -slopes[2, h] * (PAST[2] - 16 * np.arange(ROWS_B2))
    parts["bias_sa"], parts["bias_sb"] = sa, sb
    small = np.zeros((P, N_CONST), f)
    for name, (at, n) in CONSTS.items():
        small[:, at:at + n] = parts[name]
    qi, kj = np.arange(P)[:, None], np.arange(2 * P)[None]
    dist = qi + P - kj
    near = [np.where((dist >= 0) & (dist <= P), -slopes[g][:, None, None] * (dist * DILATION[g]), MASKED)
            for g in (0, 1)]
    a, b = np.arange(P) // 2, np.arange(P) % 2
    d2 = a[:, None] - a[None]
    near.append(np.where((d2 >= 0) & (b[:, None] == b[None]), -slopes[2][:, None, None] * (d2 * 16), MASKED))
    bias = [x.reshape(2, 2, P, -1).transpose(2, 1, 0, 3).astype(f) for x in near]
    return {"c_small": small, "c_decay": decay.reshape(P, -1), "c_inner": np.ascontiguousarray(inner).reshape(P, -1),
            "c_bias0": bias[0].reshape(P, -1), "c_bias1": bias[1].reshape(P, -1), "c_bias2": bias[2].reshape(P, -1)}


class Place:

    def __init__(self, first, per=0, turn=None):
        assert first % 2 == 0 and per % 2 == 0
        self.first, self.per, self.turn = first, per, turn

    def n(self, j):
        at = self.first + j
        return at if self.turn is None else self.turn * self.per + at

    def half(self, j):
        at = (self.first + j) // 2
        return at if self.turn is None else self.turn * (self.per // 2) + at


class Steps:

    def __init__(self, eng, sem):
        self.eng, self.sem, self.count, self.shift = eng, sem, 0, None

    def __call__(self, instruction):
        instruction.then_inc(self.sem, 1)
        self.count += 1

    def settle(self):
        self.eng.wait_ge(self.sem, self.count if self.shift is None else self.shift + self.count)

    def enter(self, turn, per):
        self.saved = (self.count, self.shift, per)
        self.shift = turn * per if self.shift is None else self.shift + turn * per

    def leave(self, turns):
        count, self.shift, per = self.saved
        assert self.count - count == per, (self.count - count, per)
        self.count = count + per * turns


def wait(eng, sem, value):
    if not isinstance(value, int) or value > 0:
        eng.wait_ge(sem, value)


def build(nc, a, out):
    ctx = ExitStack()
    with ctx:
        def sb(name, shape, dt=F32, stack=ctx):
            return stack.enter_context(nc.sbuf_tensor(name, shape, dt))

        def scratch(name, shape):
            return nc.dram_tensor(name, shape, F32, kind="Internal").ap()

        def sem(name):
            return ctx.enter_context(nc.semaphore(name))

        a_hi = sb("a_hi", [P, KT, TOKENS], F32R)
        with ExitStack() as s:
            gate_a = sb("gate_a", [P, 2, TOKENS], stack=s)
        a_lo = sb("a_lo", [P, KT, TOKENS], F32R)
        wide = sb("wide", [P, KT, TOKENS])
        w_raw = sb("w_raw", [P, 2, KT, P])
        w_part = sb("w_part", [P, 2, 2, KT, P], F32R)
        rstd = sb("rstd", [P, TOKENS])
        consts = sb("consts", [P, N_CONST])
        gains = sb("gains", [P, 2, KT])

        def const(name, rows=P):
            at, n = CONSTS[name]
            return consts[0:rows, at:at + n]

        with ExitStack() as s:
            x_row = sb("x_row", [P, 2, D], stack=s)
            x_square = sb("x_square", [P, D], stack=s)
            x_factor = sb("x_factor", [P, CHUNKS + 1], stack=s)
            diag = sb("diag", [P, CHUNKS + 1, P], stack=s)
        with ExitStack() as s:
            decay = sb("decay", [P, HEADS, P], stack=s)
            inner = sb("inner", [P, HEADS, P], stack=s)
            stage = sb("stage", [P, 2, TOKENS], stack=s)
            with ExitStack() as r:
                q_t = sb("q_t", [P, TOKENS], stack=r)
                k_t = sb("k_t", [P, TOKENS], stack=r)
                v_t = sb("v_t", [P, 2, TOKENS], stack=r)
                k_tok = sb("k_tok", [P, CHUNKS, DK], stack=r)
                v_tok = sb("v_tok", [P, CHUNKS, DV], stack=r)
                scores_t = sb("scores_t", [P, CHUNKS, P], stack=r)
                states = sb("states", [P, CHUNKS, DV], stack=r)
                o_tok = sb("o_tok", [P, CHUNKS, DV], stack=r)
                stats = sb("stats", [P, CHUNKS + 1, 6], stack=r)
                moments = sb("moments", [P, CHUNKS + 1, 2], stack=r)
                spread = sb("spread", [P, CHUNKS + 1], stack=r)
                s_state = sb("s_state", [P, SAMPLES, DV], stack=r)
                s_kmask = sb("s_kmask", [SAMPLES, SAMPLES, DK], stack=r)
                s_ktok = sb("s_ktok", [SAMPLES, DK], stack=r)
                s_vtok = sb("s_vtok", [SAMPLES, DV], stack=r)
                s_qmask = sb("s_qmask", [P, SAMPLES, SAMPLES], stack=r)
                s_otok = sb("s_otok", [SAMPLES, DV], stack=r)
            with ExitStack() as r:
                att_in = sb("att_in", [P, 3, 2, SEQ], stack=r)
                att_v = sb("att_v", [P, CHUNKS, 4 * HD], stack=r)
                att_kout = sb("att_kout", [P, 2, 2, 4 * HD], stack=r)
                bias = sb("bias", [P, 1024], stack=r)
                q_win = sb("q_win", [P, 2, 2, 2, P], stack=r)
                k_win = sb("k_win", [P, 2, 2, 2 * P], stack=r)
                probs = sb("probs", [P, 2, 2, 4 * P], stack=r)
                probs_t = sb("probs_t", [P, 2, 2, 4, P], stack=r)
                o_ext = sb("o_ext", [P, 2, 2, AH, HD + 2], stack=r)
        with ExitStack() as s:
            ao_hi = sb("ao_hi", [P, 2, TOKENS], F32R, stack=s)
            ao_lo = sb("ao_lo", [P, 2, TOKENS], F32R, stack=s)
            with ExitStack() as r:
                gate_r = sb("gate_r", [P, 2, TOKENS], stack=r)
                with ExitStack() as q:
                    s_qkv_t = sb("s_qkv_t", [P, 18, SAMPLES], stack=q)
                    with ExitStack() as z:
                        s_qkv = sb("s_qkv", [SAMPLES, 3, KIND], stack=z)
                    with ExitStack() as z:
                        q_a = sb("q_a", [P, SAMPLES, 4 * HD], stack=z)
                        q_b = sb("q_b", [ROWS_B, SAMPLES, 4 * HD], stack=z)
                        kv_a = sb("kv_a", [P, SAMPLES, 2, 4 * HD], stack=z)
                        kv_b = sb("kv_b", [ROWS_B, SAMPLES, 2, 4 * HD], stack=z)
                        s_score = sb("s_score", [P, 2, 32], stack=z)
                        s_prob = sb("s_prob", [32, P + ROWS_B], stack=z)
                        s_ptok = sb("s_ptok", [P, 2, 32], stack=z)
                        s_small = sb("s_small", [32, 4], stack=z)
                with ExitStack() as q:
                    parts = sb("parts", [P, GROUPS, CHUNKS * AH, HD + 2], stack=q)
                    ao_tok = sb("ao_tok", [P, CHUNKS, 4 * HD], stack=q)
                    prod = sb("prod", [P, CHUNKS * AH, HD], stack=q)
                    mrg = sb("mrg", [P, 8, CHUNKS * AH], stack=q)
            with ExitStack() as r:
                b_hi = sb("b_hi", [P, KT, TOKENS], F32R, stack=r)
                b_lo = sb("b_lo", [P, KT, TOKENS], F32R, stack=r)
        with ExitStack() as s:
            temp = sb("temp", [P, 4, TOKENS], stack=s)
            y_row = sb("y_row", [P, 2, D], stack=s)
            gain_row = sb("gain_row", [P, D], stack=s)
            fin = sb("fin", [P, 2, 2], stack=s)
            y_square = sb("y_square", [P, D], stack=s)

        unit_ps = [ctx.enter_context(nc.psum_tensor(f"unit_ps{g}", [P, PIECES, 512], F32)) for g in range(2)]
        task_ps = [ctx.enter_context(nc.psum_tensor(f"task_ps{b}", [P, 512], F32)) for b in range(2)]

        x_spill = scratch("x_spill", [KT, P, TOKENS])
        att_spill = scratch("att_spill", [18, P, TOKENS])
        gate_spill = scratch("gate_spill", [2 * KT, P, TOKENS])
        att_rows = scratch("att_rows", [GROUPS, SEQ, OUT_ROW])
        sample_rows = scratch("sample_rows", [3, SAMPLES, KIND])

        const_loaded = sem("const_loaded")
        table_loaded = sem("table_loaded")
        x_loaded = [sem(f"x_loaded{i}") for i in range(2)]
        x_spilled = sem("x_spilled")
        squared = sem("squared")
        summed = sem("summed")
        x_root = sem("x_root")
        diag_ready = sem("diag_ready")
        a_high = sem("a_high")
        b_high = sem("b_high")
        merged = sem("merged")
        root = sem("root")
        rstd_ready = sem("rstd_ready")
        w_loaded = [sem(f"w_loaded{i}") for i in range(2)]
        w_high = sem("w_high")
        w_split = sem("w_split")
        unit_done = sem("unit_done")
        unit_free = [sem(f"unit_free{g}") for g in range(2)]
        task_done = [sem(f"task_done{b}") for b in range(2)]
        task_free = [sem(f"task_free{b}") for b in range(2)]
        a_ready = sem("a_ready")
        b_ready = sem("b_ready")
        dve_step = sem("dve_step")
        act_step = sem("act_step")
        silu_done = sem("silu_done")
        q_ready = sem("q_ready")
        masked_ready = sem("masked_ready")
        normed = sem("normed")
        s_loaded = sem("s_loaded")
        s_stored = sem("s_stored")
        p_stored = sem("p_stored")
        spilled = [sem(f"spilled{i}") for i in range(2)]
        att_loaded = sem("att_loaded")
        window = sem("window")
        peak = sem("peak")
        exps = sem("exps")
        rows_stored = [sem(f"rows_stored{i}") for i in range(2)]
        v_stored = sem("v_stored")
        k_stored = [sem(f"k_stored{i}") for i in range(2)]
        qkv_loaded = sem("qkv_loaded")
        cache_loaded = sem("cache_loaded")
        rows_written = sem("rows_written")
        smp_out = sem("smp_out")
        smp_dve = sem("smp_dve")
        smp_act = sem("smp_act")
        parts_loaded = sem("parts_loaded")
        mrg_dve = sem("mrg_dve")
        mrg_act = sem("mrg_act")
        gate_loaded = [sem(f"gate_loaded{i}") for i in range(2)]
        gate_a_loaded = [sem(f"gate_a_loaded{i}") for i in range(2)]
        x_back = [sem(f"x_back{i}") for i in range(2)]
        gain_loaded = sem("gain_loaded")
        y_stored = [sem(f"y_stored{i}") for i in range(2)]

        w_in, w_ret, w_att, w_out, w_gu, w_down = (
            a[name][0].rearrange("(k p) n -> p k n", p=P)
            for name in ("w_in", "w_ret_branch", "w_att_branch", "w_out", "w_gate_up", "w_down"))
        p_kv = (out["p_kv_w128"], out["p_kv_w512"], out["p_kv_w2048"])
        s_kv = (out["s_kv_w128"], out["s_kv_w512"], out["s_kv_w2048"])

        def flat(ap):
            return ap.rearrange("p a b -> p (a b)")

        def pieces(ap):
            return ap.rearrange("p (n t) -> p n t", n=PIECES)

        def unit_out(g):
            return unit_ps[g][:, :, 0:PIECE]

        def columns(ap, g, t, tokens=P):
            if g == 0:
                return ap[:, ds(t * P, tokens)]
            if g == 1:
                start = (t // 4) * 512 + t % 4 if isinstance(t, int) else t
                return ap[:, ds(start, tokens, 4)]
            return ap[:, ds(t, tokens, 8)]

        block = ctx.enter_context(nc.Block())

        @block.sync
        def _(sp):
            sp.dma_start(consts[:], a["c_small"]).then_inc(const_loaded, 16)
            for t in range(2):
                sp.dma_start(x_row[:, t, :], a["x_prompt"][0, t * P:(t + 1) * P, :]).then_inc(x_loaded[t], 16)
            sp.dma_start(gains[:], a["norm_gains"]).then_inc(const_loaded, 16)

            def load(pl, j, kt, src):
                wait(sp, w_split, pl.n(j) - 1)
                sp.dma_start(w_raw[:, j % 2, 0:kt, :], src).then_inc(w_loaded[j % 2], 16)

            cols = (COL_RV, COL_RV + P, COL_RK, COL_RQ)
            for j in range(2):
                load(Place(0), j, KT, w_in[:, :, cols[j]:cols[j] + P])
            for t in range(2, CHUNKS + 1):
                sp.wait_ge(task_done[1], t - 1)
                sp.wait_ge(squared, t - 1)
                if t < CHUNKS:
                    sp.dma_start(x_row[:, t % 2, :], a["x_prompt"][0, t * P:(t + 1) * P, :]).then_inc(x_loaded[t % 2], 16)
                else:
                    sp.dma_start(x_row[0:SAMPLES, 0, :], a["x_sample"][:, 0, :]).then_inc(x_loaded[0], 16)
            for j in range(2, 4):
                load(Place(0), j, KT, w_in[:, :, cols[j]:cols[j] + P])
            for b in range(2):
                sp.wait_ge(task_free[b], CHUNKS + 1)
            sp.dma_start(x_spill.rearrange("k p t -> p k t"), wide[:]).then_inc(x_spilled, 16)
            for b in range(2):
                sp.wait_ge(task_free[b], T_RET // 2)
            sp.dma_start(flat(decay[:]), a["c_decay"]).then_inc(table_loaded, 16)
            sp.dma_start(flat(inner[:]), a["c_inner"]).then_inc(table_loaded, 16)
            with sp.Fori(0, HEADS - 1) as h:
                for j, (c, by) in enumerate(((COL_RV + DV, DV), (COL_RV + DV + P, DV), (COL_RK + DK, DK),
                                             (COL_RQ + DK, DK), (COL_RG, DV), (COL_RG + P, DV))):
                    load(Place(U_HEADS, 6, h), j, KT, w_in[:, :, ds(h * by + c, P)])
            for j in range(6):
                c = COL_ATT + KIND * (j // 2) + P * (j % 2)
                load(Place(U_GROUP0), j, KT, w_in[:, :, c:c + P])
            for j in range(2):
                c = COL_RG + 3 * DV + P * j
                load(Place(U_GATE3), j, KT, w_in[:, :, c:c + P])
            def gate_loads(pl, m):
                for j, c in enumerate((COL_GATE_R, COL_GATE_A)):
                    load(pl, j, KT, w_in[:, :, ds(m * P + c, P)])

            gate_loads(Place(U_GATE0), 0)
            for g in (1, 2):
                with sp.Fori(0, 3) as kind:
                    for j in range(2):
                        load(Place(U_GROUPS + 6 * (g - 1), 2, kind), j, KT,
                             w_in[:, :, ds(kind * KIND + (COL_ATT + 256 * g + P * j), P)])
            with sp.Fori(0, KT - 1) as m:
                gate_loads(Place(U_GATES, 2, m), m + 1)

            def branch_loads(m, x, pl):
                load(pl, x, KT, w_ret[:, :, ds(m * P, P)])

            def gate_load(buffer, m, kind, loaded):
                sp.dma_start(buffer, gate_spill[ds(m * 2 + kind, 1)].rearrange("a p t -> p (a t)")).then_inc(loaded, 16)

            for x in range(2):
                branch_loads(x, x, Place(U_BRANCH))
            for x in range(2):
                sp.wait_ge(spilled[x], 16 * 17)
            sp.wait_ge(window, 18)
            for x in range(2):
                gate_load(gate_r[:, x, :], x, 0, gate_loaded[x])
            with sp.Fori(0, KT // 2 - 1) as i:
                for x in range(2):
                    branch_loads(i * 2 + (2 + x), x, Place(U_BRANCH + 2, 2, i))
                    sp.wait_ge(unit_free[x], i + (U_BRANCH // 2 + 1))
                    gate_load(gate_r[:, x, :], i * 2 + (2 + x), 0, gate_loaded[x])
            for x in range(2):
                load(Place(U_ATT), x, 2, w_att[:, :, x * P:(x + 1) * P])
            sp.wait_ge(unit_done, U_ATT)
            for x in range(2):
                gate_load(gate_a[:, x, :], x, 1, gate_a_loaded[x])
            with sp.Fori(0, KT // 2 - 1) as i:
                for x in range(2):
                    load(Place(U_ATT + 2, 2, i), x, 2, w_att[:, :, ds(i * 2 * P + (2 + x) * P, P)])
                    sp.wait_ge(merged, i * 2 + (1 + x))
                    gate_load(gate_a[:, x, :], i * 2 + (2 + x), 1, gate_a_loaded[x])

            def x_load(j, m):
                sp.dma_start(temp[:, j, :], x_spill[ds(m, 1)].rearrange("a p t -> p (a t)")).then_inc(x_back[j], 16)

            for j in range(2):
                load(Place(U_OUT), j, KT, w_out[:, :, j * P:(j + 1) * P])
            sp.wait_ge(x_spilled, 16)
            sp.wait_ge(unit_done, U_OUT)
            for j in range(2):
                x_load(j, j)
            with sp.Fori(0, KT // 2 - 1) as i:
                for j in range(2):
                    sp.wait_ge(unit_free[j], i + (U_OUT // 2 + 1))
                    x_load(j, i * 2 + (2 + j))
                    load(Place(U_OUT + 2, 2, i), j, KT, w_out[:, :, ds(i * 2 * P + (2 + j) * P, P)])
            for c, nf in enumerate(FF_CHUNKS):
                f0 = sum(FF_CHUNKS[:c])
                with sp.Fori(0, nf) as f:
                    for j in range(2):
                        load(Place(U_FFN_CHUNK[c], 2, f), j, KT, w_gu[:, :, ds(f * P + (j * D_FF + f0 * P), P)])
                with sp.Fori(0, KT // 2) as i:
                    for j in range(2):
                        load(Place(U_FFN_CHUNK[c] + 2 * nf, 2, i), j, nf,
                             w_down[:, f0:f0 + nf, ds(i * 2 * P + j * P, P)])
            sp.wait_ge(unit_done, U_FINAL)
            sp.dma_start(gain_row[:], a["norm_final"].partition_broadcast(P)).then_inc(gain_loaded, 16)
            for t in range(CHUNKS + 1):
                sp.wait_ge(unit_free[t % 2], Place(U_FINAL).half(t) + 1)
                if t < CHUNKS:
                    sp.dma_start(out["y_prompt"][0, t * P:(t + 1) * P, :], y_row[:, t % 2, :]).then_inc(y_stored[t % 2], 16)
                else:
                    sp.dma_start(out["y_sample"][:, 0, :], y_row[0:SAMPLES, 0, :]).then_inc(y_stored[0], 16)
            sp.wait_ge(y_stored[0], 16 * 5)
            sp.wait_ge(y_stored[1], 16 * 4)
            sp.wait_ge(s_stored, 16 * HEADS)
            sp.wait_ge(p_stored, 16 * HEADS)
            sp.wait_ge(v_stored, 16 * GROUPS)
            for x in range(2):
                sp.wait_ge(k_stored[x], 16 * K_STORES[GROUPS][x])
            sp.wait_ge(smp_out, 16 * GROUPS)

        @block.gpsimd
        def _(pool):
            def split(pl, j, kt):
                s = j % 2
                pool.wait_ge(w_loaded[s], pl.half(j) * 16 + 16)
                wait(pool, unit_done, pl.n(j) - 1)
                raw, part = w_raw[:, s, 0:kt, :], w_part[:, s, :, 0:kt, :]
                one = const("ones").unsqueeze(1).to_broadcast([P, kt, P])
                pool.tensor_tensor(part[:, 0], raw, one, ALU.mult).then_inc(w_high, 1)
                pool.wait_ge(w_high, pl.n(j) + 1)
                pool.tensor_tensor(part[:, 1], raw, part[:, 0].bitcast(F32), ALU.subtract).then_inc(w_split, 1)

            pool.wait_ge(const_loaded, 16 * 2)
            for j in range(2):
                split(Place(0), j, KT)
            with pool.Fori(0, (U_ATT - 2) // 2) as i:
                for j in range(2):
                    split(Place(2, 2, i), j, KT)
            with pool.Fori(0, KT // 2) as i:
                for j in range(2):
                    split(Place(U_ATT, 2, i), j, 2)
            with pool.Fori(0, KT // 2) as i:
                for j in range(2):
                    split(Place(U_OUT, 2, i), j, KT)
            for c, nf in enumerate(FF_CHUNKS):
                with pool.Fori(0, nf) as f:
                    for j in range(2):
                        split(Place(U_FFN_CHUNK[c], 2, f), j, KT)
                with pool.Fori(0, KT // 2) as i:
                    for j in range(2):
                        split(Place(U_FFN_CHUNK[c] + 2 * nf, 2, i), j, nf)

        @block.tensor
        def _(pe):
            ident = const("ident")

            def unit(pl, j, kt, hi, lo, ready=None, between=None):
                s = j % 2
                pe.wait_ge(w_split, pl.n(j) + 1)
                wait(pe, unit_free[s], pl.half(j))
                for k in range(kt):
                    if between:
                        between(k)
                    if ready:
                        pe.wait_ge(ready[0], ready[1] + k + 1)
                    for part, (w, x) in enumerate(((0, hi), (0, lo), (1, hi))):
                        for n in range(PIECES):
                            mm = pe.matmul(unit_ps[s][:, n, 0:PIECE], w_part[:, s, w, k, :],
                                           x[:, k, n * PIECE:(n + 1) * PIECE],
                                           start=(k == 0 and part == 0), stop=(k == kt - 1 and part == 2))
                mm.then_inc(unit_done, 1)
                if between:
                    between(kt)

            def begin(pl, j):
                wait(pe, task_free[j % 2], pl.half(j))
                return task_ps[j % 2]

            def end(mm, j):
                mm.then_inc(task_done[j % 2], 1)

            def taken(pl, j):
                pe.wait_ge(task_free[j % 2], pl.half(j) + 1)

            def norm_sum(pl, tiles, source):
                pe.wait_ge(summed, tiles)
                for j in range(4):
                    ps = begin(pl, j)
                    n = TOKENS // 4
                    end(pe.matmul(ps[:, 0:n], const("ones"), source[:, j * n:(j + 1) * n], start=True, stop=True), j)

            pe.wait_ge(const_loaded, 16 * 2)
            for t in range(CHUNKS + 1):
                rows = P if t < CHUNKS else SAMPLES
                pe.wait_ge(x_loaded[t % 2], 16 * (t // 2 + 1))
                for b in range(2):
                    ps = begin(Place(0), 2 * t + b)
                    for q in range(4):
                        c = (4 * b + q) * P
                        mm = pe.transpose(ps[:, q * P:q * P + rows], x_row[0:rows, t % 2, c:c + P], ident[0:rows, 0:rows])
                    end(mm, b)
            def x_norm(j):
                if j == 0:
                    pe.wait_ge(diag_ready, 1)
                ps = begin(Place(T_NORM1), j)
                for q, t in enumerate(X_NORM[j]):
                    n = P if t < CHUNKS else SAMPLES
                    mm = pe.matmul(ps[:, q * P:q * P + n], const("ones", n), diag[0:n, t, 0:n], start=True, stop=True)
                end(mm, j)

            unit(Place(0), 0, KT, a_hi, a_lo, ready=(a_ready, 0))
            unit(Place(0), 1, KT, a_hi, a_lo, between=lambda k: x_norm(k - 3) if 3 <= k < 7 else None)
            for j in range(2, 4):
                unit(Place(0), j, KT, a_hi, a_lo)

            def ret_task(pl, up, heads, j):
                ps = begin(pl, j)
                if j == 0:
                    pe.wait_ge(unit_free[0], up.half(0))
                    pe.wait_ge(unit_free[1], up.half(0))
                if j < VS:
                    for q in range(2):
                        n = 2 * j + q
                        for v in range(2):
                            mm = pe.transpose(ps[:, (2 * q + v) * P:(2 * q + v + 1) * P], v_t[:, v, n * P:(n + 1) * P], ident)
                elif j == VS:
                    for v in range(2):
                        mm = pe.transpose(ps[0:SAMPLES, v * P:(v + 1) * P], v_t[:, v, SEQ:TOKENS], ident)
                elif j < KS:
                    for q in range(4):
                        n = 4 * (j - KT_) + q
                        mm = pe.transpose(ps[:, q * P:(q + 1) * P], k_t[:, n * P:(n + 1) * P], ident)
                elif j == KS:
                    mm = pe.transpose(ps[0:SAMPLES, 0:P], k_t[:, SEQ:TOKENS], ident)
                elif j < UP:
                    for q in range(4):
                        c = slice((4 * (j - SC) + q) * P, (4 * (j - SC) + q + 1) * P)
                        mm = pe.matmul(ps[:, q * P:(q + 1) * P], k_t[:, c], q_t[:, c], start=True, stop=True)
                elif j < OUT_:
                    for q in range(2):
                        n = 2 * (j - UP) + q
                        mm = pe.matmul(ps[:, q * DV:(q + 1) * DV], k_tok[:, n, :], v_tok[:, n, :], start=True, stop=True)
                elif j < OUTER:
                    if j == OUT_:
                        pe.wait_ge(q_ready, heads + 1)
                    for q in range(2):
                        n = 2 * (j - OUT_) + q
                        mm = pe.matmul(ps[:, q * DV:(q + 1) * DV], scores_t[:, n, :], v_tok[:, n, :], start=True, stop=n == 0)
                        if n:
                            mm = pe.matmul(ps[:, q * DV:(q + 1) * DV], q_t[:, n * P:(n + 1) * P], states[:, n - 1, :],
                                           start=False, stop=True)
                elif j < OS:
                    if j == OUTER:
                        pe.wait_ge(masked_ready, heads + 1)
                    for q in range(2):
                        mm = pe.matmul(ps[:, q * DV:(q + 1) * DV], s_kmask[:, 2 * (j - OUTER) + q, :], s_vtok[:],
                                       start=True, stop=True)
                elif j == OS:
                    taken(pl, OUTER + 3)
                    for n in range(SAMPLES):
                        mm = pe.matmul(ps[0:SAMPLES, 0:DV], s_qmask[:, n, :], s_state[:, n, :],
                                       start=(n == 0), stop=(n == SAMPLES - 1))
                elif j < TS:
                    if j == TURN:
                        pe.wait_ge(normed, heads * 2 + 2)
                    for v in range(2):
                        for q in range(2):
                            mm = pe.transpose(ps[:, (2 * v + q) * P:(2 * v + q + 1) * P],
                                              o_tok[:, 2 * (j - TURN) + q, v * P:(v + 1) * P], ident)
                else:
                    for v in range(2):
                        mm = pe.matmul(ps[:, v * SAMPLES:(v + 1) * SAMPLES], s_otok[:, v * P:(v + 1) * P],
                                       ident[0:SAMPLES, 0:SAMPLES], start=True, stop=True)
                end(mm, j)

            def ret_stage(pl, up, heads):
                for j in range(6):
                    unit(up, j, KT, a_hi, a_lo,
                         between=lambda k: ret_task(pl, up, heads, RET_AT[j, k]) if (j, k) in RET_AT else None)

            with pe.Fori(0, HEADS - 1) as h:
                ret_stage(Place(T_RET, RET_TASKS, h), Place(U_HEADS, 6, h), h)
            ret_stage(Place(T_RET + RET_TASKS * (HEADS - 1)), Place(U_GROUP0), HEADS - 1)

            def prep_task(pl, g, j):
                if j == 0:
                    pe.wait_ge(att_loaded, 16 * 2 * (g + 1))
                ps = begin(pl, j)
                kind, t0 = (2, 2 * j) if j < 4 else (1, 2 * (j - 4) + (0 if g == 2 else 4))
                for q in range(2):
                    for pair in range(2):
                        mm = pe.transpose(ps[:, (2 * q + pair) * P:(2 * q + pair + 1) * P],
                                          columns(att_in[:, kind, pair, :], g, t0 + q), ident)
                end(mm, j)

            def tile_scores(pl, e, nth, buf, prev, tiles):
                ps = begin(pl, e)
                pe.wait_ge(window, nth + 1)
                keys = 2 * P if prev else P
                half = slice(64 * e, 64 * e + 64)
                for t in range(tiles):
                    for pair in range(2):
                        at = (2 * t + pair) * keys
                        mm = pe.matmul(ps[:, at:at + keys], q_win[half, buf, pair, t, :],
                                       k_win[half, buf, pair, t * P:t * P + keys], start=True, stop=True)
                end(mm, e)

            def tile_turn(pl, e, nth, buf, prev, tiles):
                ps = begin(pl, 2 + e)
                pe.wait_ge(exps, nth * 2 + (e + 1))
                for x in range(2 * tiles * (2 if prev else 1)):
                    mm = pe.transpose(ps[:, x * P:(x + 1) * P], probs[:, buf, e, x * P:(x + 1) * P], ident)
                end(mm, 2 + e)

            def tile_values(pl, e, buf, prev, tiles, v_tiles):
                ps = begin(pl, 4 + e)
                for t in range(tiles):
                    for pair in range(2):
                        at, col = (2 * t + pair) * HD, (2 * pair + e) * HD
                        blocks = ((2 * pair, v_tiles[0]), (2 * pair + 1, v_tiles[1])) if prev else ((2 * t + pair, v_tiles[t]),)
                        for x, (blk, tile) in enumerate(blocks):
                            v = flat(att_v[:, ds(tile, 1), col:col + HD])
                            mm = pe.matmul(ps[:, at:at + HD], probs_t[:, buf, e, blk, :], v,
                                           start=(x == 0), stop=(x == len(blocks) - 1))
                end(mm, 4 + e)

            def tile_task(j, pl, nth, buf, prev, tiles, v_tiles):
                if j < 2:
                    tile_scores(pl, j, nth, buf, prev, tiles)
                elif j < 4:
                    tile_turn(pl, j - 2, nth, buf, prev, tiles)
                else:
                    tile_values(pl, j - 4, buf, prev, tiles, v_tiles)

            def beside(*args):
                def between(k):
                    for j in range(TILE_TASKS):
                        if TILE_AT[j] == k:
                            tile_task(j, *args)
                return between

            def preparing(pl, g):
                return lambda k: prep_task(pl, g, k - (9 - PREP[g])) if k >= 9 - PREP[g] else None

            unit(Place(U_GATE3), 0, KT, a_hi, a_lo)
            unit(Place(U_GATE3), 1, KT, a_hi, a_lo, between=preparing(Place(T_PREP0), 0))
            unit(Place(U_GATE0), 0, KT, a_hi, a_lo, between=beside(Place(T_TILE0), 0, 0, False, 1, (0,)))
            unit(Place(U_GATE0), 1, KT, a_hi, a_lo)
            with pe.Fori(0, 3) as i:
                for x in range(2):
                    up = Place(U_GROUPS + 2 * x, 4, i)
                    unit(up, 0, KT, a_hi, a_lo,
                         between=beside(Place(T_TILES0 + 6 * x, 12, i), i * 2 + (1 + x), (1 + x) % 2, True, 1,
                                        (i * 2 + x, i * 2 + (x + 1))))
                    unit(up, 1, KT, a_hi, a_lo)
            up = Place(U_GATES)
            unit(up, 0, KT, a_hi, a_lo, between=beside(Place(T_TILES0 + 36), 7, 1, True, 1, (6, 7)))
            unit(up, 1, KT, a_hi, a_lo, between=preparing(Place(T_PREP1), 1))
            for x in range(2):
                unit(Place(U_GATES + 2), x, KT, a_hi, a_lo,
                     between=beside(Place(T_FREE1 + 6 * x), 8 + x, x, False, 2, (2 * x, 2 * x + 1)))
            with pe.Fori(0, 2) as i:
                for x in range(2):
                    unit(Place(U_GATES + 4, 2, i), x, KT, a_hi, a_lo,
                         between=beside(Place(T_PREV1 + 6 * x, 12, i), i * 2 + (10 + x), x, True, 1,
                                        (i * 2 + x, i * 2 + (4 + x))))
            unit(Place(U_GATES + 8), 0, KT, a_hi, a_lo)
            unit(Place(U_GATES + 8), 1, KT, a_hi, a_lo, between=preparing(Place(T_PREP2), 2))
            with pe.Fori(0, 2) as i:
                for x in range(2):
                    unit(Place(U_GATES + 10, 2, i), x, KT, a_hi, a_lo,
                         between=beside(Place(T_FREE2 + 6 * x, 12, i), i * 2 + (14 + x), x, False, 2,
                                        (i * 4 + 2 * x, i * 4 + (2 * x + 1))))

            def sample_task(j):
                pl = Place(T_SAMPLE)
                if j == 0:
                    pe.wait_ge(qkv_loaded, 16)
                ps = begin(pl, j)
                if j < 6:
                    for q in range(4 - 2 * (j % 2)):
                        f = 4 * (j % 2) + q
                        mm = pe.transpose(ps[0:SAMPLES, q * P:(q + 1) * P],
                                          s_qkv_t[:, 6 * (f // 2) + 2 * (j // 2) + f % 2, :], ident)
                elif j == 6:
                    pe.wait_ge(smp_dve, 1)
                    pe.transpose(ps[0:32, 0:P], s_score[:, 0, :], ident)
                    mm = pe.transpose(ps[0:32, P:P + ROWS_B], s_score[0:ROWS_B, 1, :], ident[0:ROWS_B, 0:ROWS_B])
                elif j == 7:
                    pe.wait_ge(smp_dve, 2)
                    pe.transpose(ps[:, 0:32], s_prob[:, 0:P], ident[0:32, 0:32])
                    mm = pe.transpose(ps[0:ROWS_B, 32:64], s_prob[:, P:P + ROWS_B], ident[0:32, 0:32])
                else:
                    pair = j - 8
                    if pair == 0:
                        taken(pl, 7)
                    for n in range(SAMPLES):
                        c, f = 4 * n + 2 * pair, slice(pair * P, (pair + 1) * P)
                        pe.matmul(ps[:, 2 * n:2 * n + 2], kv_a[:, n, 1, f], s_ptok[:, 0, c:c + 2], start=True, stop=False)
                        mm = pe.matmul(ps[:, 2 * n:2 * n + 2], kv_b[:, n, 1, f], s_ptok[0:ROWS_B, 1, c:c + 2],
                                       start=False, stop=True)
                end(mm, j)

            def merge_task(j):
                if j == 0:
                    pe.wait_ge(mrg_dve, 2)
                ps = begin(Place(T_MERGE), j)
                for pair in range(2):
                    for q in range(2):
                        mm = pe.transpose(ps[:, (2 * pair + q) * P:(2 * pair + q + 1) * P],
                                          ao_tok[:, 2 * j + q, pair * P:(pair + 1) * P], ident)
                end(mm, j)

            def late_tasks(m):
                def between(k):
                    for j in range(T_NORM2 - T_SAMPLE):
                        if LATE_AT[j] == (m, k):
                            sample_task(j) if j < T_MERGE - T_SAMPLE else merge_task(j - (T_MERGE - T_SAMPLE))
                return between

            for m in range(KT):
                unit(Place(U_BRANCH), m, KT, a_hi, a_lo, ready=(a_ready, KT) if m == 0 else None, between=late_tasks(m))
            for b in range(2):
                pe.wait_ge(task_free[b], T_NORM2 // 2)
            with pe.Fori(0, KT // 2) as i:
                for j in range(2):
                    unit(Place(U_ATT, 2, i), j, 2, ao_hi, ao_lo)
            with pe.Fori(0, KT // 2) as i:
                for j in range(2):
                    unit(Place(U_OUT, 2, i), j, KT, b_hi, b_lo, ready=(b_ready, 0))
            norm_sum(Place(T_NORM2), KT + 1, temp[:, 3])
            for c, nf in enumerate(FF_CHUNKS):
                with pe.Fori(0, nf) as f:
                    for j in range(2):
                        unit(Place(U_FFN_CHUNK[c], 2, f), j, KT, a_hi, a_lo, ready=(a_ready, 2 * KT))
                with pe.Fori(0, KT // 2) as i:
                    for j in range(2):
                        unit(Place(U_FFN_CHUNK[c] + 2 * nf, 2, i), j, nf, b_hi, b_lo,
                             ready=(b_ready, KT + sum(FF_CHUNKS[:c])))
            for g in range(2):
                pe.wait_ge(unit_free[g], U_FINAL // 2)
            for t in range(CHUNKS + 1):
                n, g = P if t < CHUNKS else SAMPLES, t % 2
                pe.wait_ge(unit_free[g], Place(U_FINAL).half(t))
                for k in range(KT):
                    mm = pe.transpose(unit_ps[g][0:n, k // 4, (k % 4) * P:(k % 4 + 1) * P], wide[:, k, t * P:t * P + n], ident)
                mm.then_inc(unit_done, 1)

        @block.scalar
        def _(act):
            def full(pl, j):
                act.wait_ge(task_done[j % 2], pl.half(j) + 1)
                return task_ps[j % 2]

            def empty(ins, j):
                ins.then_inc(task_free[j % 2], 1)

            def norm_root(pl):
                n = TOKENS // 4
                for j in range(4):
                    ps = full(pl, j)
                    empty(act.activation(rstd[:, j * n:(j + 1) * n], ps[:, 0:n], ACT.Sqrt, scale=1.0 / D,
                                         bias=const("eps")[:, 0:1]), j)

            def turned(t):
                n = P if t < CHUNKS else SAMPLES
                empty(act.activation(wide[:, 4:8, t * P:t * P + n],
                                     full(Place(0), 2 * t + 1)[:].rearrange("p (q t) -> p q t", q=4)[:, :, 0:n], ACT.Copy), 1)

            for t in range(CHUNKS + 1):
                n = P if t < CHUNKS else SAMPLES
                act.wait_ge(x_loaded[t % 2], 16 * (t // 2 + 1))
                wait(act, squared, t)
                act.activation(x_square[0:n, :], x_row[0:n, t % 2, :], ACT.Square, accum_out=x_factor[0:n, t:t + 1])\
                   .then_inc(squared, 1)
                turned(t)
            for b in range(2):
                act.wait_ge(task_free[b], CHUNKS + 1)
            for k in range(KT):
                act.activation(a_hi[:, k, :], wide[:, k, :], ACT.Copy, scale=gains[:, 0, k:k + 1]).then_inc(a_high, 1)
            act.wait_ge(squared, CHUNKS + 1)
            for n, c in ((P, slice(0, CHUNKS)), (SAMPLES, slice(CHUNKS, CHUNKS + 1))):
                act.activation(x_factor[0:n, c], x_factor[0:n, c], ACT.Sqrt, scale=1.0 / D,
                               bias=const("eps", n)[:, 0:1]).then_inc(x_root, 1)
            for j, tiles in enumerate(X_NORM):
                n = min(len(tiles) * P, TOKENS - tiles[0] * P)
                c = tiles[0] * P
                empty(act.activation(rstd[:, c:c + n], full(Place(T_NORM1), j)[:, 0:n], ACT.Copy), j)

            def load_states(h):
                act.dma_start(s_state[:], a["state_ret"][0][:, ds(h, 1)].rearrange("n a d v -> d (n a) v")).then_inc(s_loaded, 16)

            for b in range(2):
                act.wait_ge(task_free[b], T_RET // 2)
            load_states(0)

            def ret_slot(pl, h, j):
                for x in {0: range(VT, KT_), 1: (KS,), 2: range(OUT_, OUTER), 3: (OS,)}.get(j, ()):
                    ps = full(pl, x)
                    if x < VS:
                        ins = act.activation(v_tok[:, 2 * x:2 * x + 2, :], ps[:].rearrange("p (q d) -> p q d", q=2), ACT.Copy)
                    elif x == VS:
                        ins = act.activation(s_vtok[:], ps[0:SAMPLES, 0:DV], ACT.Copy)
                    elif x == KS:
                        ins = act.activation(s_ktok[:], ps[0:SAMPLES, 0:DK], ACT.Copy)
                    elif x < OUTER:
                        n = 2 * (x - OUT_)
                        ins = act.activation(o_tok[:, n:n + 2, :], ps[:].rearrange("p (q d) -> p q d", q=2), ACT.Copy)
                    else:
                        ins = act.activation(s_otok[:], ps[0:SAMPLES, 0:DV], ACT.Copy)
                    empty(ins, x)
                if j == 2:
                    act.wait_ge(task_free[1], pl.half(UP + 3) + 1)
                    act.dma_start(out["p_ret"][0, 0][ds(h, 1)].rearrange("a d v -> d (a v)"), states[:, CHUNKS - 1, :])\
                       .then_inc(p_stored, 16)
                if j == 3:
                    act.wait_ge(task_free[0], pl.half(OUTER + 2) + 1)
                    act.wait_ge(task_free[1], pl.half(OUTER + 3) + 1)
                    act.dma_start(out["s_ret"][0][:, ds(h, 1)].rearrange("n a d v -> d (n a) v"), s_state[:]).then_inc(s_stored, 16)
                    act.wait_ge(normed, h * 2 + 1)
                    act.activation(spread[:, 0:CHUNKS], flat(moments[:, 0:CHUNKS, 1:2]), ACT.Sqrt, bias=const("eps")[:, 1:2])
                    act.activation(spread[0:SAMPLES, CHUNKS:CHUNKS + 1], moments[0:SAMPLES, CHUNKS, 1:2], ACT.Sqrt,
                                   bias=const("eps", SAMPLES)[:, 1:2]).then_inc(root, 1)

            def in_place(pl, j, func):
                act.wait_ge(unit_free[j % 2], pl.half(j) + 1)
                act.activation(stage[:, j % 2, :], stage[:, j % 2, :], func).then_inc(silu_done, 1)

            with act.Fori(0, HEADS - 1) as h:
                pl = Place(T_RET, RET_TASKS, h)
                up = Place(U_HEADS, 6, h)
                for j in range(6):
                    ret_slot(pl, h, j)
                    if j >= 4:
                        in_place(up, j, ACT.Silu)
                act.wait_ge(s_stored, h * 16 + 16)
                load_states(h + 1)

            def spill(pl, j, dst):
                act.wait_ge(unit_free[j % 2], pl.half(j) + 1)
                act.dma_start(dst, stage[:, j % 2, :]).then_inc(spilled[j % 2], 16)

            for j in range(6):
                ret_slot(Place(T_RET + RET_TASKS * (HEADS - 1)), HEADS - 1, j)
                spill(Place(U_GROUP0), j, att_spill[j])

            def load_group(g):
                for x in range(2):
                    act.wait_ge(spilled[x], 16 * (3 * (g + 1) + (g > 0)))
                act.dma_start(att_in[:].rearrange("p a b t -> p (a b) t"),
                              att_spill[6 * g:6 * g + 6, :, 0:SEQ].rearrange("a p t -> p a t")).then_inc(att_loaded, 16)
                n = 1024 if g < 2 else 512
                act.dma_start(bias[:, 0:n], a[f"c_bias{g}"]).then_inc(att_loaded, 16)

            for b in range(2):
                act.wait_ge(task_free[b], T_ATT // 2)
            act.wait_ge(s_stored, 16 * HEADS)
            act.wait_ge(p_stored, 16 * HEADS)
            load_group(0)

            def kv_store(g, kind, t0, n, src, stored):
                rows = p_kv[g][0, 0][:, kind - 1].rearrange("r h d -> r (h d)")
                if g == 0:
                    dst, src = rows, src[:, n - 1, :]
                elif g == 1:
                    dst = rows.rearrange("(p t) d -> p t d", t=4)[:, t0 - 4:t0 - 4 + n, :]
                else:
                    dst = rows.rearrange("(p t) d -> p t d", t=8)[:, t0:t0 + n, :]
                act.dma_start(dst, src).then_inc(stored, 16)

            def prep(pl, g):
                wait(act, v_stored, 16 * g)
                for j in range(PREP[g]):
                    ps = full(pl, j)[:].rearrange("p (q d) -> p q d", q=2)
                    if j < 4:
                        empty(act.activation(att_v[:, 2 * j:2 * j + 2, :], ps, ACT.Copy), j)
                        continue
                    wait(act, k_stored[j % 2], 16 * (K_STORES[g][j % 2] + (j - 4) // 2))
                    empty(act.activation(att_kout[:, j % 2], ps, ACT.Copy), j)
                    if j == 4:
                        for b in range(2):
                            act.wait_ge(task_free[b], pl.half(2 + b) + 1)
                        t0 = (7, 4, 0)[g]
                        kv_store(g, 2, t0, 8 - t0, att_v[:, t0:8, :], v_stored)
                    if g or j == 5:
                        act.wait_ge(task_free[j % 2], pl.half(j) + 1)
                        kv_store(g, 1, 2 * (j - 4) + (0 if g == 2 else 4), 2, att_kout[:, j % 2], k_stored[j % 2])

            def windows(g, t, buf, prev, tiles):
                for pair in range(2):
                    queries, keys = att_in[:, 0, pair, :], att_in[:, 1, pair, :]
                    if prev:
                        act.activation(k_win[:, buf, pair, :], columns(keys, g, t - 1 if g == 0 else t - 4, 2 * P), ACT.Copy)
                    for x in range(tiles):
                        if not prev:
                            act.activation(k_win[:, buf, pair, x * P:(x + 1) * P], columns(keys, g, t + x), ACT.Copy)
                        ins = act.activation(q_win[:, buf, pair, x, :], columns(queries, g, t + x), ACT.Copy, scale=HD ** -0.5)
                ins.then_inc(window, 1)

            def tile(pl, nth, buf, prev, tiles, dst, following):
                keys = 2 * P if prev else P
                for e in range(2):
                    act.wait_ge(peak, nth * 2 + (e + 1))
                    for x in range(tiles):
                        for pair in range(2):
                            s = probs[:, buf, e, (2 * x + pair) * keys:(2 * x + pair + 1) * keys]
                            o = o_ext[:, buf, x, 2 * pair + e, :]
                            ins = act.activation(s, s, ACT.Exp, bias=o[:, HD + 1:HD + 2], accum_out=o[:, HD:HD + 1])
                    ins.then_inc(exps, 1)
                if following:
                    following()
                for e in range(2):
                    ps = full(pl, 4 + e)[:, 0:tiles * 2 * HD].rearrange("p (x d) -> p x d", d=HD)
                    o = o_ext[:, buf, 0:tiles].rearrange("p x h d -> p (x h) d")[:, e::2, 0:HD]
                    empty(act.activation(o, ps, ACT.Copy), 4 + e)
                for e in range(2):
                    act.wait_ge(task_free[e], pl.half(4 + e) + 1)
                act.wait_ge(exps, nth * 2 + 2)
                act.dma_start(dst, o_ext[:, buf, 0:tiles].rearrange("p x h d -> p x (h d)")).then_inc(rows_stored[buf], 16)

            def rows0(t):
                return att_rows[0].rearrange("(t p) d -> p t d", p=P)[:, ds(t, 1)]

            def rows1(half, t, n):
                return att_rows[1].rearrange("(f p t) d -> p f t d", f=2, t=4)[:, half, ds(t, n)]

            def rows2(t):
                return att_rows[2].rearrange("(p t) d -> p t d", t=8)[:, ds(t, 2)]

            def gate(pl, j, m):
                in_place(pl, j, ACT.Sigmoid)
                act.wait_ge(silu_done, m * 2 + (2 * HEADS + j + 1))
                act.dma_start(gate_spill[ds(m * 2 + j, 1)].rearrange("a p t -> p (a t)"), stage[:, j, :]).then_inc(spilled[j], 16)

            def start_group(pl, g, tiles):
                act.wait_ge(att_loaded, 16 * 2 * (g + 1))
                windows(g, 0, 0, False, tiles)
                prep(pl, g)

            def next_group(g, nth):
                act.wait_ge(window, nth)
                act.wait_ge(peak, 2 * nth)
                load_group(g)

            in_place(Place(U_GATE3), 0, ACT.Silu)
            start_group(Place(T_PREP0), 0, 1)
            in_place(Place(U_GATE3), 1, ACT.Silu)
            tile(Place(T_TILE0), 0, 0, False, 1, rows0(0), lambda: windows(0, 1, 1, True, 1))
            for j in range(2):
                gate(Place(U_GATE0), j, 0)
            with act.Fori(0, 3) as i:
                for x in range(2):
                    tile(Place(T_TILES0 + 6 * x, 12, i), i * 2 + (1 + x), (1 + x) % 2, True, 1, rows0(i * 2 + (1 + x)),
                         lambda: windows(0, i * 2 + (2 + x), x, True, 1))
                    for j in range(2):
                        spill(Place(U_GROUPS + 2 * x, 4, i), j,
                              att_spill[ds(i * 4 + (6 + 2 * x + j), 1)].rearrange("a p t -> p (a t)"))
            tile(Place(T_TILES0 + 36), 7, 1, True, 1, rows0(7), lambda: next_group(1, 8))
            gate(Place(U_GATES), 0, 1)
            start_group(Place(T_PREP1), 1, 2)
            gate(Place(U_GATES), 1, 1)
            for x in range(2):
                tile(Place(T_FREE1 + 6 * x), 8 + x, x, False, 2, rows1(0, 2 * x, 2),
                     lambda: windows(1, 4, 0, True, 1) if x else windows(1, 2, 1, False, 2))
                gate(Place(U_GATES + 2), x, 2)
            for n in range(4):
                tile(Place(T_PREV1 + 6 * n), 10 + n, n % 2, True, 1, rows1(1, n, 1),
                     lambda: windows(1, 5 + n, (n + 1) % 2, True, 1) if n < 3 else next_group(2, 14))
                gate(Place(U_GATES + 4 + 2 * (n // 2)), n % 2, 3 + n // 2)
            gate(Place(U_GATES + 8), 0, 5)
            start_group(Place(T_PREP2), 2, 2)
            gate(Place(U_GATES + 8), 1, 5)
            for n in range(4):
                tile(Place(T_FREE2 + 6 * n), 14 + n, n % 2, False, 2, rows2(2 * n),
                     (lambda: windows(2, 2 * n + 2, (n + 1) % 2, False, 2)) if n < 3 else None)
                gate(Place(U_GATES + 10 + 2 * (n // 2)), n % 2, 6 + n // 2)

            act.wait_ge(unit_done, U_BRANCH)
            for k in range(KT):
                act.activation(a_hi[:, k, :], wide[:, k, :], ACT.Copy).then_inc(a_high, 1)

            act.wait_ge(v_stored, 16 * GROUPS)
            for x in range(2):
                act.wait_ge(k_stored[x], 16 * K_STORES[GROUPS][x])
            for x in range(2):
                act.wait_ge(spilled[x], 16 * 17)
                act.wait_ge(rows_stored[x], 16 * 9)
            act.dma_start(s_qkv_t[:], att_spill[:, :, SEQ:TOKENS].rearrange("a p t -> p a t")).then_inc(qkv_loaded, 16)
            pl = Place(T_SAMPLE)
            for j in range(6):
                ps = full(pl, j)
                c, n = (0, 512) if j % 2 == 0 else (512, 256)
                empty(act.activation(s_qkv[:, j // 2, c:c + n], ps[0:SAMPLES, 0:n], ACT.Copy), j)
            for b in range(2):
                act.wait_ge(task_free[b], pl.half(4 + b) + 1)
            act.dma_start(sample_rows.rearrange("a n c -> n a c"), s_qkv[:]).then_inc(rows_written, 16)
            for g in range(GROUPS):
                act.dma_start(s_kv[g][0, :, 0].rearrange("n c h d -> n c (h d)"),
                              s_qkv[:, 1:3, g * 256:(g + 1) * 256]).then_inc(smp_out, 16)
            act.wait_ge(rows_written, 16)
            act.wait_ge(smp_out, 16 * GROUPS)
            r2 = ROWS_B1 + ROWS_B2
            act.dma_start(kv_a[:], a["cache_kv_w128"][0].rearrange("n r c h d -> r n c (h d)")).then_inc(cache_loaded, 16)
            for name, by, r0, r1 in (("cache_kv_w512", 4, 0, ROWS_B1), ("cache_kv_w2048", 16, ROWS_B1, ROWS_B1 + ROWS_B2)):
                act.dma_start(kv_b[r0:r1], a[name][0].rearrange("n (r s) c h d -> r s n c (h d)", s=by)[:, 0]).then_inc(cache_loaded, 16)
            act.dma_start(q_a[:], sample_rows[0, :, 0:256].partition_broadcast(P)).then_inc(cache_loaded, 16)
            act.dma_start(q_b[0:ROWS_B1], sample_rows[0, :, 256:512].partition_broadcast(ROWS_B1)).then_inc(cache_loaded, 16)
            act.dma_start(q_b[ROWS_B1:r2], sample_rows[0, :, 512:768].partition_broadcast(ROWS_B2)).then_inc(cache_loaded, 16)
            by_group = sample_rows.rearrange("a n (g c) -> a g n c", g=GROUPS)
            act.dma_start(q_b[r2:ROWS_B], by_group[0]).then_inc(cache_loaded, 16)
            for c in range(2):
                act.dma_start(kv_b[r2:ROWS_B, :, c, :], by_group[1 + c]).then_inc(cache_loaded, 16)
            act.wait_ge(smp_act, 1)
            act.activation(s_prob[:], s_prob[:], ACT.Exp, bias=s_small[:, 0:1], accum_out=s_small[:, 1:2]).then_inc(root, 1)

            for b in range(2):
                act.wait_ge(task_free[b], T_MERGE // 2)
            for g in range(GROUPS):
                act.dma_start(parts[:, g].rearrange("p (t h) d -> p t (h d)", h=AH),
                              att_rows[g].rearrange("(t p) d -> p t d", p=P)).then_inc(parts_loaded, 16)
            act.wait_ge(mrg_dve, 1)
            act.activation(mrg[:, 0:3, :], mrg[:, 0:3, :], ACT.Exp).then_inc(mrg_act, 1)

            for m in range(KT):
                act.wait_ge(merged, m + 1)
                act.activation(b_hi[:, m, :], wide[:, m, :], ACT.Copy).then_inc(b_high, 1)
            for m in range(KT):
                act.wait_ge(unit_free[m % 2], Place(U_OUT).half(m) + 1)
                act.wait_ge(summed, m + 1)
                act.activation(temp[:, 2, :], wide[:, m, :], ACT.Square).then_inc(squared, 1)
            norm_root(Place(T_NORM2))
            for c, nf in enumerate(FF_CHUNKS):
                with act.Fori(0, nf) as f:
                    act.wait_ge(unit_free[0], Place(U_FFN_CHUNK[c], 2, f).half(0) + 1)
                    act.activation(temp[:, 0, :], temp[:, 0, :], ACT.Silu).then_inc(silu_done, 1)
            for t in range(CHUNKS + 1):
                n, g = P if t < CHUNKS else SAMPLES, t % 2
                act.wait_ge(unit_done, U_FINAL + t + 1)
                if t:
                    act.wait_ge(act_step, 2 * t)
                act.activation(y_square[0:n, :].rearrange("p (a b) -> p a b", a=2), unit_ps[g][0:n, 0:2, :], ACT.Square,
                               accum_out=fin[0:n, g, 0:1]).then_inc(act_step, 1)
                act.wait_ge(act_step, 2 * t + 1)
                act.activation(fin[0:n, g, 0:1], fin[0:n, g, 0:1], ACT.Sqrt, scale=1.0 / D, bias=const("eps", n)[:, 0:1])\
                   .then_inc(act_step, 1)

        @block.vector
        def _(dve):
            step = Steps(dve, dve_step)

            def full(pl, j):
                dve.wait_ge(task_done[j % 2], pl.half(j) + 1)
                return task_ps[j % 2]

            def empty(ins, j):
                ins.then_inc(task_free[j % 2], 1)

            def take(pl, j):
                dve.wait_ge(unit_done, pl.n(j) + 1)
                return unit_out(j % 2)

            def scaled(pl, j, dst, by=None):
                ps = take(pl, j)
                if by is None:
                    ins = dve.tensor_tensor(pieces(dst), ps, pieces(rstd[:]), ALU.mult)
                else:
                    ins = dve.scalar_tensor_tensor(out=pieces(dst), in0=ps, scalar=by, in1=pieces(rstd[:]),
                                                   op0=ALU.mult, op1=ALU.mult)
                ins.then_inc(unit_free[j % 2], 1)

            def norm_factor(tasks):
                for b in range(2):
                    dve.wait_ge(task_free[b], tasks // 2)
                dve.reciprocal(rstd[:], rstd[:]).then_inc(rstd_ready, 1)

            for t in range(CHUNKS + 1):
                n = P if t < CHUNKS else SAMPLES
                empty(dve.tensor_copy(wide[:, 0:4, t * P:t * P + n],
                                      full(Place(0), 2 * t)[:].rearrange("p (q t) -> p q t", q=4)[:, :, 0:n]), 0)
            dve.wait_ge(const_loaded, 16 * 2)
            for b in range(2):
                dve.wait_ge(task_free[b], CHUNKS + 1)
            for k in range(KT):
                dve.wait_ge(a_high, k + 1)
                dve.scalar_tensor_tensor(out=a_lo[:, k, :], in0=wide[:, k, :], scalar=gains[:, 0, k:k + 1],
                                         in1=a_hi[:, k, :].bitcast(F32), op0=ALU.mult, op1=ALU.subtract).then_inc(a_ready, 1)
            dve.wait_ge(x_root, 2)
            step(dve.reciprocal(x_factor[:, 0:CHUNKS], x_factor[:, 0:CHUNKS]))
            step(dve.reciprocal(x_factor[0:SAMPLES, CHUNKS:CHUNKS + 1], x_factor[0:SAMPLES, CHUNKS:CHUNKS + 1]))
            step.settle()
            step(dve.tensor_scalar(diag[0:SAMPLES, CHUNKS, 0:SAMPLES], const("ident", SAMPLES)[:, 0:SAMPLES],
                                   x_factor[0:SAMPLES, CHUNKS:CHUNKS + 1], None, ALU.mult))
            dve.tensor_tensor(diag[:, 0:CHUNKS, :], const("ident").unsqueeze(1).to_broadcast([P, CHUNKS, P]),
                              x_factor[:, 0:CHUNKS].unsqueeze(2).to_broadcast([P, CHUNKS, P]), ALU.mult).then_inc(diag_ready, 1)
            for b in range(2):
                dve.wait_ge(task_free[b], T_RET // 2)
            scaled(Place(0), 0, v_t[:, 0, :])
            scaled(Place(0), 1, v_t[:, 1, :])
            scaled(Place(0), 2, k_t[:])
            scaled(Place(0), 3, q_t[:], DK ** -0.5)
            dve.wait_ge(table_loaded, 16 * 2)
            dve.wait_ge(x_spilled, 16)

            def ret_slot(pl, h, j):
                if j < 2:
                    empty(dve.tensor_scalar(k_tok[:, 4 * j:4 * j + 4, :],
                                            full(pl, KT_ + j)[:].rearrange("p (q d) -> p q d", q=4),
                                            const("tail")[:, ds(h, 1)], None, ALU.mult), KT_ + j)
                if j == 1:
                    dve.wait_ge(task_free[KS % 2], pl.half(KS) + 1)
                    eye = const("eye8").rearrange("p (a b) -> p a b", a=SAMPLES)
                    dve.tensor_tensor(s_kmask[:], s_ktok[:].unsqueeze(1).to_broadcast([SAMPLES, SAMPLES, DK]),
                                      masks8().to_broadcast([SAMPLES, SAMPLES, DK]), ALU.mult)
                    dve.tensor_tensor(s_qmask[:], q_t[:, SEQ:TOKENS].unsqueeze(2).to_broadcast([P, SAMPLES, SAMPLES]),
                                      eye, ALU.mult).then_inc(masked_ready, 1)
                    for x in range(2):
                        ps = full(pl, SC + x)[:].rearrange("p (q t) -> p q t", q=4)
                        empty(dve.tensor_tensor(scores_t[:, 4 * x:4 * x + 4, :], ps,
                                                decay[:, ds(h, 1), :].to_broadcast([P, 4, P]), ALU.mult), SC + x)
                    q = q_t[:, 0:SEQ].rearrange("p (n t) -> p n t", t=P)
                    dve.tensor_tensor(q, q, inner[:, ds(h, 1), :].to_broadcast([P, CHUNKS, P]), ALU.mult).then_inc(q_ready, 1)
                if j in (1, 2):
                    for x in (range(UP, UP + 3) if j == 1 else (UP + 3,)):
                        ps = full(pl, x)
                        for q in range(2):
                            n = 2 * (x - UP) + q
                            u = ps[:, q * DV:(q + 1) * DV]
                            if n == 0:
                                ins = dve.tensor_copy(states[:, 0, :], u)
                            else:
                                ins = dve.scalar_tensor_tensor(out=states[:, n, :], in0=states[:, n - 1, :],
                                                               scalar=const("gamma_c")[:, ds(h, 1)], in1=u,
                                                               op0=ALU.mult, op1=ALU.add)
                            if q == 0:
                                step(ins)
                                step.settle()
                            else:
                                empty(ins, x)
                                dve.wait_ge(task_free[x % 2], pl.half(x) + 1)
                if j in (2, 3):
                    for x in (range(OUTER, OUTER + 3) if j == 2 else (OUTER + 3,)):
                        if x == OUTER:
                            dve.wait_ge(s_loaded, h * 16 + 16)
                        s = s_state[:, 2 * (x - OUTER):2 * (x - OUTER) + 2, :]
                        ps = full(pl, x)[:].rearrange("p (q d) -> p q d", q=2)
                        empty(dve.scalar_tensor_tensor(out=s, in0=s, scalar=const("gamma")[:, ds(h, 1)], in1=ps,
                                                       op0=ALU.mult, op1=ALU.add), x)
                if j == 3:
                    for x in (OUT_ + 2, OUT_ + 3, OS):
                        dve.wait_ge(task_free[x % 2], pl.half(x) + 1)
                    rows = [(o_tok[:, n, :], P) for n in range(CHUNKS)] + [(s_otok[:], SAMPLES)]
                    for n, (o, r) in enumerate(rows):
                        step(dve.bn_stats(stats[0:r, n, :], o))
                    step.settle()
                    dve.memset(spread[:], 1.0)
                    for n, (o, r) in enumerate(rows):
                        ins = dve.bn_aggr(moments[0:r, n, :], stats[0:r, n, :])
                        if n < CHUNKS:
                            step(ins)
                    ins.then_inc(normed, 1)
                    dve.wait_ge(root, h + 1)
                    step(dve.reciprocal(spread[:, 0:CHUNKS], spread[:, 0:CHUNKS]))
                    step(dve.reciprocal(spread[0:SAMPLES, CHUNKS:CHUNKS + 1], spread[0:SAMPLES, CHUNKS:CHUNKS + 1]))
                    step.settle()
                    dve.wait_ge(normed, h * 2 + 1)
                    for n, (o, r) in enumerate(rows):
                        ins = dve.tensor_scalar(o, o, moments[0:r, n, 0:1], spread[0:r, n:n + 1], ALU.subtract, ALU.mult)
                    ins.then_inc(normed, 1)
                if j == 4:
                    dve.wait_ge(p_stored, h * 16 + 16)
                    for x in range(4):
                        ps = full(pl, TURN + x)[:].rearrange("p (v t) -> p v t", v=2)
                        empty(dve.tensor_copy(wide[:, ds(h * 2, 2), 2 * P * x:2 * P * (x + 1)], ps), TURN + x)
                    ps = full(pl, TS)[:, 0:2 * SAMPLES].rearrange("p (v t) -> p v t", v=2)
                    empty(dve.tensor_copy(wide[:, ds(h * 2, 2), SEQ:TOKENS], ps), TS)

            def masks8():
                return const("ident", SAMPLES)[:, 0:SAMPLES].unsqueeze(2)

            def gated(pl, j, h, v, done):
                scaled(pl, j, stage[:, j % 2, :])
                dve.wait_ge(silu_done, done)
                for b in range(2):
                    dve.wait_ge(task_free[b], h * (RET_TASKS // 2) + (T_RET + RET_TASKS) // 2)
                t = flat(wide[:, ds(h * 2 + v, 1), :])
                step(dve.tensor_tensor(t, t, stage[:, j % 2, :], ALU.mult))

            with dve.Fori(0, HEADS - 1) as h:
                step.enter(h, STEPS_HEAD)
                up = Place(U_HEADS, 6, h)
                for j in range(6):
                    ret_slot(Place(T_RET, RET_TASKS, h), h, j)
                    if j < 2:
                        scaled(up, j, v_t[:, j, :])
                    elif j == 2:
                        scaled(up, j, k_t[:])
                    elif j == 3:
                        scaled(up, j, q_t[:], DK ** -0.5)
                    else:
                        gated(up, j, h, j - 4, h * 2 + (j - 3))
                step.leave(HEADS - 1)

            def staged(pl, j, before):
                wait(dve, spilled[j % 2], before)
                scaled(pl, j, stage[:, j % 2, :])

            for j in range(6):
                ret_slot(Place(T_RET + RET_TASKS * (HEADS - 1)), HEADS - 1, j)
                staged(Place(U_GROUP0), j, 16 * (j // 2))
            for j in range(2):
                dve.wait_ge(spilled[j], 16 * 3)
                gated(Place(U_GATE3), j, HEADS - 1, j, 2 * (HEADS - 1) + j + 1)

            def tile(pl, g, buf, prev, tiles, stored):
                wait(dve, rows_stored[buf], stored)
                keys = 2 * P if prev else P
                n = 2 * tiles
                for e in range(2):
                    ps = full(pl, e)[:, 0:n * keys]
                    s = probs[:, buf, e, 0:n * keys]
                    o = o_ext[:, buf, 0:tiles].rearrange("p x h d -> p (x h) d")[:, e::2, HD + 1:HD + 2]
                    if g == 2:
                        b = bias[:, 0:512].rearrange("p (e a k) -> p e a k", e=2, a=2)[:, e]
                    else:
                        b = bias[:].rearrange("p (e a k) -> p e a k", e=2, a=2)[:, e, :, 2 * P - keys:2 * P]
                    if tiles == 2:
                        b = b.unsqueeze(1).to_broadcast([P, 2, 2, P])
                        ps, sx = (y.rearrange("p (t a k) -> p t a k", t=2, a=2) for y in (ps, s))
                    else:
                        ps, sx = (y.rearrange("p (a k) -> p a k", a=2) for y in (ps, s))
                    empty(dve.tensor_tensor(sx, ps, b, ALU.add), e)
                    dve.wait_ge(task_free[e], pl.half(e) + 1)
                    dve.tensor_reduce(o, s.rearrange("p (x k) -> p x k", k=keys), AX_X, ALU.max, negate=True).then_inc(peak, 1)
                for e in range(2):
                    ps = full(pl, 2 + e)[:, 0:n * keys]
                    empty(dve.tensor_copy(probs_t[:, buf, e].rearrange("p x t -> p (x t)")[:, 0:n * keys], ps), 2 + e)

            dve.wait_ge(att_loaded, 16 * 2)
            tile(Place(T_TILE0), 0, 0, False, 1, 0)
            for j in range(2):
                staged(Place(U_GATE0), j, 16 * 3)
            with dve.Fori(0, 3) as i:
                for x in range(2):
                    tile(Place(T_TILES0 + 6 * x, 12, i), 0, (1 + x) % 2, True, 1, i * 16 + 16 if x else 0)
                    for j in range(2):
                        staged(Place(U_GROUPS + 2 * x, 4, i), j, i * 32 + 16 * (4 + x))
                dve.wait_ge(rows_stored[1], i * 16 + 16)
            tile(Place(T_TILES0 + 36), 0, 1, True, 1, 16 * 3)
            for j in range(2):
                staged(Place(U_GATES), j, 16 * 10)
            dve.wait_ge(att_loaded, 16 * 4)
            for x in range(2):
                tile(Place(T_FREE1 + 6 * x), 1, x, False, 2, 16 * 4)
                staged(Place(U_GATES + 2), x, 16 * 11)
            with dve.Fori(0, 2) as i:
                for x in range(2):
                    tile(Place(T_PREV1 + 6 * x, 12, i), 1, x, True, 1, i * 16 + 16 * 5)
                    staged(Place(U_GATES + 4, 2, i), x, i * 16 + 16 * 12)
            for j in range(2):
                staged(Place(U_GATES + 8), j, 16 * 14)
            dve.wait_ge(att_loaded, 16 * 6)
            with dve.Fori(0, 2) as i:
                for x in range(2):
                    tile(Place(T_FREE2 + 6 * x, 12, i), 2, x, False, 2, i * 16 + 16 * 7)
                    staged(Place(U_GATES + 10, 2, i), x, i * 16 + 16 * 15)

            for k in range(KT):
                dve.wait_ge(a_high, KT + k + 1)
                dve.tensor_tensor(a_lo[:, k, :], wide[:, k, :], a_hi[:, k, :].bitcast(F32), ALU.subtract).then_inc(a_ready, 1)

            def sample_products(x):
                if x == 0:
                    dve.wait_ge(cache_loaded, 16 * 9)
                q, kv, r = ((q_a, kv_a, P), (q_b, kv_b, ROWS_B))[x]
                step(dve.tensor_tensor(q[:], q[:], kv[:, :, 0, :], ALU.mult))
                step.settle()
                ins = dve.tensor_reduce(s_score[0:r, x, :], q[:].rearrange("p n (h d) -> p (n h) d", d=HD), AX_X, ALU.add)
                step(ins) if x == 0 else ins.then_inc(smp_dve, 1)

            def sample_scores():
                pl = Place(T_SAMPLE)
                ps = full(pl, 6)
                step(dve.scalar_tensor_tensor(out=s_prob[:, 0:P], in0=ps[0:32, 0:P], scalar=HD ** -0.5, in1=const("bias_sa", 32),
                                              op0=ALU.mult, op1=ALU.add))
                empty(dve.scalar_tensor_tensor(out=s_prob[:, P:P + ROWS_B], in0=ps[0:32, P:P + ROWS_B], scalar=HD ** -0.5,
                                               in1=const("bias_sb", 32), op0=ALU.mult, op1=ALU.add), 6)
                dve.wait_ge(task_free[0], pl.half(6) + 1)
                dve.tensor_reduce(s_small[:, 0:1], s_prob[:], AX_X, ALU.max, negate=True).then_inc(smp_act, 1)
                dve.wait_ge(root, HEADS + 1)
                step(dve.reciprocal(s_small[:, 2:3], s_small[:, 1:2]))
                step.settle()
                dve.tensor_scalar(s_prob[:], s_prob[:], s_small[:, 2:3], None, ALU.mult).then_inc(smp_dve, 1)

            def sample_outputs():
                pl = Place(T_SAMPLE)
                ps = full(pl, 7)
                step(dve.tensor_copy(s_ptok[:, 0, :], ps[:, 0:32]))
                empty(dve.tensor_copy(s_ptok[0:ROWS_B, 1, :], ps[0:ROWS_B, 32:64]), 7)
                for pair in range(2):
                    ps = full(pl, 8 + pair)[:, 0:2 * SAMPLES].rearrange("p (n e) -> p e n", e=2)
                    for e in range(2):
                        half = slice(64 * e, 64 * e + 64)
                        step(dve.tensor_copy(ao_hi[half, pair, SEQ:TOKENS], ps[half, e, :]))
                    step.settle()
                    for e in range(2):
                        half = slice(64 * e, 64 * e + 64)
                        ins = dve.tensor_tensor(ao_lo[half, pair, SEQ:TOKENS], ps[half, e, :],
                                                ao_hi[half, pair, SEQ:TOKENS].bitcast(F32), ALU.subtract)
                        if e == 0:
                            step(ins)
                    empty(ins, 8 + pair)


            def merge_weights():
                dve.wait_ge(parts_loaded, 16 * GROUPS)
                low = mrg[:, 6, :].unsqueeze(2)
                minus = [parts[:, g, :, HD + 1:HD + 2] for g in range(GROUPS)]
                total = [parts[:, g, :, HD:HD + 1] for g in range(GROUPS)]
                step(dve.tensor_tensor(low, minus[0], minus[1], ALU.min))
                step.settle()
                step(dve.tensor_tensor(low, low, minus[2], ALU.min))
                step.settle()
                for g in range(GROUPS):
                    ins = dve.tensor_tensor(mrg[:, g, :].unsqueeze(2), low, minus[g], ALU.subtract)
                    if g < GROUPS - 1:
                        step(ins)
                ins.then_inc(mrg_dve, 1)
                dve.wait_ge(mrg_act, 1)
                for g in range(GROUPS):
                    step(dve.tensor_tensor(mrg[:, 3 + g, :].unsqueeze(2), mrg[:, g, :].unsqueeze(2), total[g], ALU.mult))
                step.settle()
                for g in (1, 2):
                    step(dve.tensor_tensor(mrg[:, 3, :], mrg[:, 3, :], mrg[:, 3 + g, :], ALU.add))
                    step.settle()
                step(dve.reciprocal(mrg[:, 7, :], mrg[:, 3, :]))
                step.settle()
                for g in range(GROUPS):
                    step(dve.tensor_tensor(mrg[:, g, :], mrg[:, g, :], mrg[:, 7, :], ALU.mult))
                step.settle()

            def merge_group(g):
                ao = ao_tok[:].rearrange("p t (h d) -> p (t h) d", d=HD)
                by = mrg[:, g, :].unsqueeze(2).to_broadcast([P, CHUNKS * AH, HD])
                step(dve.tensor_tensor(prod[:] if g else ao, parts[:, g, :, 0:HD], by, ALU.mult))
                step.settle()
                if g:
                    ins = dve.tensor_tensor(ao, ao, prod[:], ALU.add)
                    if g == 1:
                        step(ins)
                        step.settle()
                    else:
                        ins.then_inc(mrg_dve, 1)

            def merge_turned():
                for j in range(4):
                    ps = full(Place(T_MERGE), j)[:].rearrange("p (a t) -> p a t", a=2)
                    c = slice(2 * P * j, 2 * P * (j + 1))
                    step(dve.tensor_copy(ao_hi[:, :, c], ps))
                    step.settle()
                    empty(dve.tensor_tensor(ao_lo[:, :, c], ps, ao_hi[:, :, c].bitcast(F32), ALU.subtract), j)

            for m in range(KT):
                x = m % 2
                dve.wait_ge(gate_loaded[x], 16 * (m // 2 + 1))
                dve.tensor_tensor(pieces(wide[:, m, :]), take(Place(U_BRANCH), m), pieces(gate_r[:, x, :]), ALU.mult)\
                   .then_inc(unit_free[x], 1)
                if m == 1:
                    sample_products(0)
                elif m == 2:
                    sample_products(1)
                    sample_scores()
                elif m == 3:
                    sample_outputs()
                elif m == 5:
                    merge_weights()
                    merge_group(0)
                elif m == 6:
                    merge_group(1)
                    merge_group(2)
                    merge_turned()

            def merge_branches(pl, x, m, nth):
                ga, w = gate_a[:, x, :], flat(wide[:, ds(m, 1), :])
                dve.wait_ge(gate_a_loaded[x], nth)
                dve.tensor_tensor(pieces(ga), take(pl, x), pieces(ga), ALU.mult).then_inc(unit_free[x], 1)
                dve.wait_ge(unit_free[x], pl.half(x) + 1)
                dve.tensor_tensor(w, w, ga, ALU.add).then_inc(merged, 1)

            def merged_low(m):
                dve.wait_ge(b_high, m + 1)
                hi, lo, w = (flat(y[:, ds(m, 1), :]) for y in (b_hi, b_lo, wide))
                dve.tensor_tensor(lo, w, hi.bitcast(F32), ALU.subtract).then_inc(b_ready, 1)

            merge_branches(Place(U_ATT), 0, 0, 16)
            with dve.Fori(0, KT // 2 - 1) as i:
                for x in range(2):
                    merge_branches(Place(U_ATT + 2 * x, 2, i), 1 - x, i * 2 + (1 + x), i * 16 + 16 * (1 + x))
                    merged_low(i * 2 + x)
            merge_branches(Place(U_ATT + 6), 1, KT - 1, 16 * 4)
            for m in range(KT - 2, KT):
                merged_low(m)

            dve.wait_ge(unit_done, U_OUT)
            dve.memset(temp[:, 3, :], 0.0).then_inc(summed, 1)
            with dve.Fori(0, KT // 2) as i:
                step.enter(i, STEPS_OUT)
                for j in range(2):
                    m = i * 2 + j
                    ps = take(Place(U_OUT, 2, i), j)
                    dve.wait_ge(x_back[j], i * 16 + 16)
                    x2 = flat(wide[:, ds(m, 1), :])
                    hi, lo = flat(a_hi[:, ds(m, 1), :]), flat(a_lo[:, ds(m, 1), :])
                    g = gains[:, 1, ds(m, 1)]
                    dve.tensor_tensor(pieces(x2), ps, pieces(temp[:, j, :]), ALU.add).then_inc(unit_free[j], 1)
                    dve.wait_ge(unit_free[j], Place(U_OUT, 2, i).half(j) + 1)
                    step(dve.tensor_scalar(hi, x2, g, None, ALU.mult))
                    step.settle()
                    dve.scalar_tensor_tensor(out=lo, in0=x2, scalar=g, in1=hi.bitcast(F32), op0=ALU.mult, op1=ALU.subtract)\
                       .then_inc(a_ready, 1)
                    dve.wait_ge(squared, m + (CHUNKS + 2))
                    dve.wait_ge(summed, m + 1)
                    dve.tensor_tensor(temp[:, 3, :], temp[:, 3, :], temp[:, 2, :], ALU.add).then_inc(summed, 1)
                step.leave(KT // 2)
            norm_factor(T_END)
            dve.wait_ge(rstd_ready, 1)

            for c, nf in enumerate(FF_CHUNKS):
                f0 = sum(FF_CHUNKS[:c])
                with dve.Fori(0, nf) as f:
                    step.enter(f, STEPS_FFN)
                    pl = Place(U_FFN_CHUNK[c], 2, f)
                    for j in range(2):
                        scaled(pl, j, temp[:, j, :])
                    dve.wait_ge(unit_free[1], pl.half(1) + 1)
                    dve.wait_ge(silu_done, f + (2 * HEADS + 2 * KT + f0 + 1))
                    step(dve.tensor_tensor(temp[:, 2, :], temp[:, 0, :], temp[:, 1, :], ALU.mult))
                    step.settle()
                    hi, lo = flat(b_hi[:, ds(f, 1), :]), flat(b_lo[:, ds(f, 1), :])
                    step(dve.tensor_copy(hi, temp[:, 2, :]))
                    step.settle()
                    dve.tensor_tensor(lo, temp[:, 2, :], hi.bitcast(F32), ALU.subtract).then_inc(b_ready, 1)
                    step.leave(nf)
                with dve.Fori(0, KT // 2) as i:
                    for j in range(2):
                        ps = take(Place(U_FFN_CHUNK[c] + 2 * nf, 2, i), j)
                        x = pieces(flat(wide[:, ds(i * 2 + j, 1), :]))
                        dve.tensor_tensor(x, ps, x, ALU.add).then_inc(unit_free[j], 1)

            dve.wait_ge(gain_loaded, 16)
            for t in range(CHUNKS + 1):
                n, g = P if t < CHUNKS else SAMPLES, t % 2
                dve.wait_ge(act_step, 2 * t + 2)
                wait(dve, y_stored[g], 16 * (t // 2))
                step(dve.reciprocal(fin[0:n, g, 1:2], fin[0:n, g, 0:1]))
                step.settle()
                ps = unit_ps[g][0:n, 0:2, :]
                dve.scalar_tensor_tensor(out=y_row[0:n, g, :].rearrange("p (a b) -> p a b", a=2), in0=ps,
                                         scalar=fin[0:n, g, 1:2], in1=gain_row[0:n, :].rearrange("p (a b) -> p a b", a=2),
                                         op0=ALU.mult, op1=ALU.mult).then_inc(unit_free[g], 1)


_INS = ["x_prompt", "x_sample", "state_ret", "cache_kv_w128", "cache_kv_w512", "cache_kv_w2048", "w_in",
        "w_ret_branch", "w_att_branch", "w_out", "w_gate_up", "w_down", "norm_final"]
_OUTS = [("y_prompt", (1, SEQ, D)), ("y_sample", (SAMPLES, 1, D)), ("p_ret", (1, 1, HEADS, DK, DV)),
         ("p_kv_w128", (1, 1, KEPT[0], 2, AH, HD)), ("p_kv_w512", (1, 1, KEPT[1], 2, AH, HD)),
         ("p_kv_w2048", (1, 1, KEPT[2], 2, AH, HD)), ("s_ret", (1, SAMPLES, HEADS, DK, DV)),
         ("s_kv_w128", (1, SAMPLES, 1, 2, AH, HD)), ("s_kv_w512", (1, SAMPLES, 1, 2, AH, HD)),
         ("s_kv_w2048", (1, SAMPLES, 1, 2, AH, HD))]


def kernel(**inputs):
    import concourse.bacc as bacc
    from concourse.bass_utils import run_bass_kernel_spmd

    nc = bacc.Bacc("TRN2", target_bir_lowering=False, num_devices=1)
    arrays, ins = {}, {}
    for name in _INS:
        arrays[f"in_{name}"] = np.ascontiguousarray(inputs[name])
    arrays["in_norm_gains"] = np.ascontiguousarray(
        np.stack([np.asarray(inputs[n])[0].reshape(KT, P).T for n in ("norm_mix", "norm_ffn")], 1))
    for name, table in tables().items():
        arrays[f"in_{name}"] = table
    for key, x in arrays.items():
        ins[key[3:]] = nc.dram_tensor(key, x.shape, F32, kind="ExternalInput").ap()
    outs = {name: nc.dram_tensor(f"out_{name}", shape, F32, kind="ExternalOutput").ap() for name, shape in _OUTS}
    build(nc, ins, outs)
    r = run_bass_kernel_spmd(nc, [arrays], core_ids=[0])
    return tuple(r.results[0][f"out_{name}"] for name, _ in _OUTS)
```

```python
from contextlib import ExitStack

import numpy as np
import concourse.bass as bass
from concourse import mybir

F32 = mybir.dt.float32
F32R = mybir.dt.float32r
ALU = mybir.AluOpType
ACT = mybir.ActivationFunctionType
AX_X = mybir.AxisListType.X
ds = bass.ds

P = 128
D = 1024
SEQ = 1024
SAMPLES = 8
TOKENS = SEQ + SAMPLES
PIECES = 3
PIECE = TOKENS // PIECES
KT = D // P
HEADS, DK, DV = 4, 128, 256
CHUNKS = SEQ // P
GROUPS = 3
DILATION = (1, 4, 16)
KEPT = (128, 512, 1024)
AH, HD = 4, 64
PAST = (128, 256, 256)
D_FF = 2816
D_IN = 7424
COL_RQ, COL_RK, COL_RV, COL_RG = 0, 512, 1024, 2048
COL_ATT, COL_GATE_R, COL_GATE_A = 3072, 5376, 6400
KIND = 768
RMS_EPS, GN_EPS = 1e-6, 1e-5
MASKED = -1e30
ROWS_B1, ROWS_B2 = 64, 16
ROWS_B = ROWS_B1 + ROWS_B2 + GROUPS
S_ROWS = 64 + SAMPLES
OUT_ROW = AH * (HD + 2)

U_HEAD0 = 0
U_HEADS = 4
U_GROUP0 = U_HEADS + 6 * (HEADS - 1)
U_GATE3 = U_GROUP0 + 6
U_GATE0 = U_GATE3 + 2
U_GROUPS = U_GATE0 + 2
U_GATES = U_GROUPS + 12
U_BRANCH = U_GATES + 14
U_ATT = U_BRANCH + 8
U_OUT = U_ATT + 8
U_FFN = U_OUT + 8
FF_CHUNKS = (8, 7, 7)
T_NORM1 = 18
T_RET = T_NORM1 + 4
RET_TASKS = 28
T_ATT = T_RET + HEADS * RET_TASKS
PREP = (6, 6, 8)
TILE_TASKS = 6
T_PREP0 = T_ATT
T_TILE0 = T_PREP0 + PREP[0]
T_TILES0 = T_TILE0 + TILE_TASKS
T_PREP1 = T_TILES0 + 7 * TILE_TASKS
T_FREE1 = T_PREP1 + PREP[1]
T_PREV1 = T_FREE1 + 2 * TILE_TASKS
T_PREP2 = T_PREV1 + 4 * TILE_TASKS
T_FREE2 = T_PREP2 + PREP[2]
T_SAMPLE = T_FREE2 + 4 * TILE_TASKS
T_MERGE = T_SAMPLE + 10
T_NORM2 = T_MERGE + 4
T_END = T_NORM2 + 4
U_FFN_CHUNK = [U_FFN + sum(2 * n + 8 for n in FF_CHUNKS[:c]) for c in range(len(FF_CHUNKS) + 1)]
U_FINAL = U_FFN_CHUNK[-1]

VT, VS, KT_, KS, SC, UP, OUT_, OUTER, OS, TURN, TS = 0, 4, 5, 7, 8, 10, 14, 18, 22, 23, 27
RET_AT = {(0, 2 + j): j for j in range(6)}
RET_AT.update({(1, 0): 6, (1, 1): 7, (1, 2): 8, (1, 3): 9, (1, 5): 10, (1, 6): 11, (1, 7): 12, (2, 0): 13})
RET_AT.update({(2, 1 + j): 14 + j for j in range(7)})
RET_AT.update({(3, 0): 21, (3, 3): 22, (4, 2): 23, (4, 3): 24, (4, 4): 25, (4, 5): 26, (4, 6): 27})
TILE_AT = (1, 1, 5, 6, 8, 8)
STEPS_HEAD, STEPS_OUT, STEPS_FFN = 29, 2, 2
X_ROWS = 4
X_NORM = ((0, 1, 2), (3, 4, 5), (6, 7), (8,))
LATE_AT = ((0, 1), (0, 2), (0, 4), (0, 5), (0, 6), (0, 7), (3, 5), (4, 0), (4, 3), (4, 4), (7, 1), (7, 2), (7, 3), (7, 4))
ATT_SLOT = 4
POOL_LOW = 6
K_STORES = ((0, 0, 0, 0), (0, 1, 0, 0), (1, 2, 0, 0), (2, 3, 1, 1))

CONSTS = {}
_at = 0
for _name, _n in (("ident", P), ("ones", P), ("eye8", 64), ("tail", HEADS), ("gamma_c", HEADS),
                  ("gamma", HEADS), ("eps", 2), ("bias_sa", P), ("bias_sb", ROWS_B)):
    CONSTS[_name] = (_at, _n)
    _at += _n
N_CONST = _at


def tables():
    f = np.float32
    log_gamma = np.log1p(-np.exp2(f(-5.0) - np.arange(HEADS, dtype=f))).astype(f)
    idx = np.arange(P, dtype=f)
    diff = idx[None, :] - idx[:, None]
    decay = np.where(diff[:, None, :] >= 0,
                     np.exp(np.maximum(diff, 0)[:, None, :] * log_gamma[None, :, None]), 0).astype(f)
    inner = np.exp((idx + 1)[None, :] * log_gamma[:, None]).astype(f)
    inner = np.broadcast_to(inner[None], (P, HEADS, P))
    slopes = np.exp2(f(-8.0) * (np.arange(GROUPS * AH, dtype=f) + 1) / f(GROUPS * AH)).astype(f)
    slopes = slopes.reshape(GROUPS, AH)
    parts = {
        "ident": np.eye(P), "ones": np.ones((P, P)),
        "eye8": np.broadcast_to(np.eye(8).reshape(1, 64), (P, 64)),
        "tail": np.exp((P - 1 - idx)[:, None] * log_gamma[None]),
        "gamma_c": np.broadcast_to(np.exp(P * log_gamma)[None], (P, HEADS)),
        "gamma": np.broadcast_to(np.exp(log_gamma)[None], (P, HEADS)),
        "eps": np.broadcast_to(np.array([[RMS_EPS, GN_EPS]]), (P, 2)),
    }
    sa, sb = np.zeros((P, P)), np.zeros((P, ROWS_B))
    for n in range(SAMPLES):
        for h in range(AH):
            row = n * AH + h
            sa[row] = -slopes[0, h] * (P - np.arange(P))
            sb[row, :ROWS_B1] = -slopes[1, h] * (PAST[1] - 4 * np.arange(ROWS_B1))
            sb[row, ROWS_B1:ROWS_B1 + ROWS_B2] = -slopes[2, h] * (PAST[2] - 16 * np.arange(ROWS_B2))
    parts["bias_sa"], parts["bias_sb"] = sa, sb
    small = np.zeros((P, N_CONST), f)
    for name, (at, n) in CONSTS.items():
        small[:, at:at + n] = parts[name]
    qi, kj = np.arange(P)[:, None], np.arange(2 * P)[None]
    dist = qi + P - kj
    near = [np.where((dist >= 0) & (dist <= P), -slopes[g][:, None, None] * (dist * DILATION[g]), MASKED)
            for g in (0, 1)]
    a, b = np.arange(P) // 2, np.arange(P) % 2
    d2 = a[:, None] - a[None]
    near.append(np.where((d2 >= 0) & (b[:, None] == b[None]), -slopes[2][:, None, None] * (d2 * 16), MASKED))
    bias = [x.reshape(2, 2, P, -1).transpose(2, 1, 0, 3).astype(f) for x in near]
    return {"c_small": small, "c_decay": decay.reshape(P, -1), "c_inner": np.ascontiguousarray(inner).reshape(P, -1),
            "c_bias0": bias[0].reshape(P, -1), "c_bias1": bias[1].reshape(P, -1), "c_bias2": bias[2].reshape(P, -1)}


class Place:

    def __init__(self, first, per=0, turn=None):
        assert first % 2 == 0 and per % 2 == 0
        self.first, self.per, self.turn = first, per, turn

    def n(self, j):
        at = self.first + j
        return at if self.turn is None else self.turn * self.per + at

    def half(self, j):
        at = (self.first + j) // 2
        return at if self.turn is None else self.turn * (self.per // 2) + at


class Steps:

    def __init__(self, eng, sem):
        self.eng, self.sem, self.count, self.shift = eng, sem, 0, None

    def __call__(self, instruction):
        instruction.then_inc(self.sem, 1)
        self.count += 1

    def settle(self):
        self.eng.wait_ge(self.sem, self.count if self.shift is None else self.shift + self.count)

    def enter(self, turn, per):
        self.saved = (self.count, self.shift, per)
        self.shift = turn * per if self.shift is None else self.shift + turn * per

    def leave(self, turns):
        count, self.shift, per = self.saved
        assert self.count - count == per, (self.count - count, per)
        self.count = count + per * turns


def wait(eng, sem, value):
    if not isinstance(value, int) or value > 0:
        eng.wait_ge(sem, value)


def build(nc, a, out):
    ctx = ExitStack()
    with ctx:
        def sb(name, shape, dt=F32, stack=ctx):
            return stack.enter_context(nc.sbuf_tensor(name, shape, dt))

        def scratch(name, shape):
            return nc.dram_tensor(name, shape, F32, kind="Internal").ap()

        def sem(name):
            return ctx.enter_context(nc.semaphore(name))

        a_hi = sb("a_hi", [P, KT, TOKENS], F32R)
        with ExitStack() as s:
            gate_a = sb("gate_a", [P, 2, TOKENS], stack=s)
        a_lo = sb("a_lo", [P, KT, TOKENS], F32R)
        wide = sb("wide", [P, KT, TOKENS])
        w_raw = sb("w_raw", [P, 2, KT, P])
        w_part = sb("w_part", [P, 2, 2, KT, P], F32R)
        rstd = sb("rstd", [P, TOKENS])
        consts = sb("consts", [P, N_CONST])
        gains = sb("gains", [P, 2, KT])

        def const(name, rows=P):
            at, n = CONSTS[name]
            return consts[0:rows, at:at + n]

        with ExitStack() as s:
            x_row = sb("x_row", [P, X_ROWS, D], stack=s)
            x_square = sb("x_square", [P, D], stack=s)
            x_factor = sb("x_factor", [P, CHUNKS + 1], stack=s)
            diag = sb("diag", [P, CHUNKS + 1, P], stack=s)
        with ExitStack() as s:
            stage = sb("stage", [P, 2, TOKENS], stack=s)
            with ExitStack() as r:
                decay = sb("decay", [P, HEADS, P], stack=r)
                inner = sb("inner", [P, HEADS, P], stack=r)
                q_t = sb("q_t", [P, TOKENS], stack=r)
                k_t = sb("k_t", [P, TOKENS], stack=r)
                v_t = sb("v_t", [P, 2, TOKENS], stack=r)
                k_tok = sb("k_tok", [P, CHUNKS, DK], stack=r)
                v_tok = sb("v_tok", [P, CHUNKS, DV], stack=r)
                scores_t = sb("scores_t", [P, CHUNKS, P], stack=r)
                states = sb("states", [P, CHUNKS, DV], stack=r)
                o_tok = sb("o_tok", [P, CHUNKS, DV], stack=r)
                stats = sb("stats", [P, CHUNKS + 1, 6], stack=r)
                moments = sb("moments", [P, CHUNKS + 1, 2], stack=r)
                spread = sb("spread", [P, CHUNKS + 1], stack=r)
                s_state = sb("s_state", [P, SAMPLES, DV], stack=r)
                s_kparts = sb("s_kparts", [S_ROWS, SAMPLES, DK], F32R, stack=r)
                s_vparts = sb("s_vparts", [S_ROWS, DV], F32R, stack=r)
                s_ktok = sb("s_ktok", [SAMPLES, DK], stack=r)
                s_khigh = sb("s_khigh", [SAMPLES, DK], F32R, stack=r)
                s_klow = sb("s_klow", [SAMPLES, DK], stack=r)
                s_vtok = sb("s_vtok", [SAMPLES, DV], stack=r)
                s_qmask = sb("s_qmask", [P, SAMPLES, SAMPLES], stack=r)
                s_otok = sb("s_otok", [SAMPLES, DV], stack=r)
            with ExitStack() as r:
                att_in = sb("att_in", [P, 3, 2, SEQ], stack=r)
                att_v = sb("att_v", [P, CHUNKS, 4 * HD], stack=r)
                att_kout = sb("att_kout", [P, 4, 2, 4 * HD], stack=r)
                bias = sb("bias", [P, 1024], stack=r)
                q_win = sb("q_win", [P, 2, 2, 2, P], stack=r)
                k_win = sb("k_win", [P, 2, 2, 2 * P], stack=r)
                probs = sb("probs", [P, 2, 2, 4 * P], stack=r)
                probs_t = sb("probs_t", [P, 2, 2, 4, P], stack=r)
                o_ext = sb("o_ext", [P, 2, 2, AH, HD + 2], stack=r)
        with ExitStack() as s:
            ao_hi = sb("ao_hi", [P, 2, TOKENS], F32R, stack=s)
            ao_lo = sb("ao_lo", [P, 2, TOKENS], F32R, stack=s)
            with ExitStack() as r:
                gate_r = sb("gate_r", [P, 2, TOKENS], stack=r)
                with ExitStack() as q:
                    s_qkv_t = sb("s_qkv_t", [P, 18, SAMPLES], stack=q)
                    with ExitStack() as z:
                        s_qkv = sb("s_qkv", [SAMPLES, 3, KIND], stack=z)
                    with ExitStack() as z:
                        q_a = sb("q_a", [P, SAMPLES, 4 * HD], stack=z)
                        q_b = sb("q_b", [ROWS_B, SAMPLES, 4 * HD], stack=z)
                        kv_a = sb("kv_a", [P, SAMPLES, 2, 4 * HD], stack=z)
                        kv_b = sb("kv_b", [ROWS_B, SAMPLES, 2, 4 * HD], stack=z)
                        s_score = sb("s_score", [P, 2, 32], stack=z)
                        s_prob = sb("s_prob", [32, P + ROWS_B], stack=z)
                        s_ptok = sb("s_ptok", [P, 2, SAMPLES, 32], stack=z)
                        s_out = sb("s_out", [32, 4 * HD], stack=z)
                        s_small = sb("s_small", [32, 4], stack=z)
                with ExitStack() as q:
                    parts = sb("parts", [P, GROUPS, CHUNKS * AH, HD + 2], stack=q)
                    ao_tok = sb("ao_tok", [P, CHUNKS, 4 * HD], stack=q)
                    prod = sb("prod", [P, CHUNKS * AH, HD], stack=q)
                    mrg = sb("mrg", [P, 8, CHUNKS * AH], stack=q)
            with ExitStack() as r:
                b_hi = sb("b_hi", [P, KT, TOKENS], F32R, stack=r)
                b_lo = sb("b_lo", [P, KT, TOKENS], F32R, stack=r)
        with ExitStack() as s:
            temp = sb("temp", [P, 4, TOKENS], stack=s)
            y_row = sb("y_row", [P, 3, D], stack=s)
            gain_row = sb("gain_row", [P, D], stack=s)
            fin = sb("fin", [P, 3, 2], stack=s)
            y_square = sb("y_square", [P, D], stack=s)

        unit_ps = [ctx.enter_context(nc.psum_tensor(f"unit_ps{g}", [P, PIECES, 512], F32)) for g in range(2)]
        task_banks = ctx.enter_context(nc.psum_tensor("task_banks", [P, 2, 512], F32))
        task_ps = [task_banks[:, b, :] for b in range(2)]
        y_ps = [unit_ps[0][:, 0:2, :], unit_ps[1][:, 0:2, :], task_banks[:]]

        x_spill = scratch("x_spill", [KT, P, TOKENS])
        att_spill = scratch("att_spill", [18, P, TOKENS])
        gate_spill = scratch("gate_spill", [2 * KT, P, TOKENS])
        att_rows = scratch("att_rows", [GROUPS, SEQ, OUT_ROW])
        sample_rows = scratch("sample_rows", [3, SAMPLES, KIND])

        const_loaded = sem("const_loaded")
        gains_loaded = sem("gains_loaded")
        table_loaded = sem("table_loaded")
        x_loaded = [sem(f"x_loaded{i}") for i in range(X_ROWS)]
        x_spilled = sem("x_spilled")
        squared = sem("squared")
        summed = sem("summed")
        x_root = sem("x_root")
        diag_ready = sem("diag_ready")
        a_high = sem("a_high")
        b_high = sem("b_high")
        merged = sem("merged")
        root = sem("root")
        rstd_ready = sem("rstd_ready")
        w_loaded = [sem(f"w_loaded{i}") for i in range(2)]
        w_high = sem("w_high")
        w_split = sem("w_split")
        unit_done = sem("unit_done")
        unit_free = [sem(f"unit_free{g}") for g in range(2)]
        task_done = [sem(f"task_done{b}") for b in range(2)]
        task_free = [sem(f"task_free{b}") for b in range(2)]
        a_ready = sem("a_ready")
        b_ready = sem("b_ready")
        dve_step = sem("dve_step")
        act_step = sem("act_step")
        silu_done = sem("silu_done")
        q_ready = sem("q_ready")
        masked_ready = sem("masked_ready")
        normed = sem("normed")
        s_loaded = sem("s_loaded")
        s_stored = sem("s_stored")
        p_stored = sem("p_stored")
        spilled = [sem(f"spilled{i}") for i in range(2)]
        att_loaded = sem("att_loaded")
        window = sem("window")
        peak = sem("peak")
        exps = sem("exps")
        rows_stored = [sem(f"rows_stored{i}") for i in range(2)]
        v_stored = sem("v_stored")
        k_stored = [sem(f"k_stored{i}") for i in range(4)]
        qkv_loaded = sem("qkv_loaded")
        cache_loaded = sem("cache_loaded")
        rows_written = sem("rows_written")
        smp_out = sem("smp_out")
        smp_dve = sem("smp_dve")
        smp_act = sem("smp_act")
        parts_loaded = sem("parts_loaded")
        mrg_dve = sem("mrg_dve")
        mrg_act = sem("mrg_act")
        gate_loaded = [sem(f"gate_loaded{i}") for i in range(2)]
        gate_a_loaded = [sem(f"gate_a_loaded{i}") for i in range(2)]
        x_back = [sem(f"x_back{i}") for i in range(2)]
        gain_loaded = sem("gain_loaded")
        y_turned = sem("y_turned")
        y_ready = sem("y_ready")
        y_stored = [sem(f"y_stored{i}") for i in range(3)]

        w_in, w_ret, w_att, w_out, w_gu, w_down = (
            a[name][0].rearrange("(k p) n -> p k n", p=P)
            for name in ("w_in", "w_ret_branch", "w_att_branch", "w_out", "w_gate_up", "w_down"))
        p_kv = (out["p_kv_w128"], out["p_kv_w512"], out["p_kv_w2048"])
        s_kv = (out["s_kv_w128"], out["s_kv_w512"], out["s_kv_w2048"])

        def flat(ap):
            return ap.rearrange("p a b -> p (a b)")

        def pieces(ap):
            return ap.rearrange("p (n t) -> p n t", n=PIECES)

        def unit_out(g):
            return unit_ps[g][:, :, 0:PIECE]

        def columns(ap, g, t, tokens=P):
            if g == 0:
                return ap[:, ds(t * P, tokens)]
            if g == 1:
                start = (t // 4) * 512 + t % 4 if isinstance(t, int) else t
                return ap[:, ds(start, tokens, 4)]
            return ap[:, ds(t, tokens, 8)]

        block = ctx.enter_context(nc.Block())

        @block.sync
        def _(sp):
            def load(pl, j, kt, src):
                wait(sp, w_split, pl.n(j) - 1)
                sp.dma_start(w_raw[:, j % 2, 0:kt, :], src).then_inc(w_loaded[j % 2], 16)

            cols = (COL_RV, COL_RV + P, COL_RK, COL_RQ)
            for t in range(CHUNKS + 1):
                r = t % X_ROWS
                if t >= X_ROWS:
                    sp.wait_ge(task_done[1], t - X_ROWS + 1)
                    sp.wait_ge(squared, t - X_ROWS + 1)
                if t < CHUNKS:
                    sp.dma_start(x_row[:, r, :], a["x_prompt"][0, t * P:(t + 1) * P, :]).then_inc(x_loaded[r], 16)
                else:
                    sp.dma_start(x_row[0:SAMPLES, r, :], a["x_sample"][:, 0, :]).then_inc(x_loaded[r], 16)
                if t == X_ROWS:
                    load(Place(0), 0, KT, w_in[:, :, cols[0]:cols[0] + P])
            for j in range(1, 4):
                load(Place(0), j, KT, w_in[:, :, cols[j]:cols[j] + P])
            for b in range(2):
                sp.wait_ge(task_free[b], CHUNKS + 1)
            sp.dma_start(x_spill.rearrange("k p t -> p k t"), wide[:]).then_inc(x_spilled, 16)
            for b in range(2):
                sp.wait_ge(task_free[b], T_RET // 2)
            sp.dma_start(flat(decay[:]), a["c_decay"]).then_inc(table_loaded, 16)
            sp.dma_start(flat(inner[:]), a["c_inner"]).then_inc(table_loaded, 16)
            with sp.Fori(0, HEADS - 1) as h:
                for j, (c, by) in enumerate(((COL_RV + DV, DV), (COL_RV + DV + P, DV), (COL_RK + DK, DK),
                                             (COL_RQ + DK, DK), (COL_RG, DV), (COL_RG + P, DV))):
                    load(Place(U_HEADS, 6, h), j, KT, w_in[:, :, ds(h * by + c, P)])
            for j in range(6):
                c = COL_ATT + KIND * (j // 2) + P * (j % 2)
                load(Place(U_GROUP0), j, KT, w_in[:, :, c:c + P])
            for j in range(2):
                c = COL_RG + 3 * DV + P * j
                load(Place(U_GATE3), j, KT, w_in[:, :, c:c + P])
            def gate_loads(pl, m):
                for j, c in enumerate((COL_GATE_R, COL_GATE_A)):
                    load(pl, j, KT, w_in[:, :, ds(m * P + c, P)])

            gate_loads(Place(U_GATE0), 0)
            for g in (1, 2):
                with sp.Fori(0, 3) as kind:
                    for j in range(2):
                        load(Place(U_GROUPS + 6 * (g - 1), 2, kind), j, KT,
                             w_in[:, :, ds(kind * KIND + (COL_ATT + 256 * g + P * j), P)])
            with sp.Fori(0, KT - 1) as m:
                gate_loads(Place(U_GATES, 2, m), m + 1)

            def gate_load(buffer, m, kind, loaded):
                sp.dma_start(buffer, gate_spill[ds(m * 2 + kind, 1)].rearrange("a p t -> p (a t)")).then_inc(loaded, 16)

            for m in range(2):
                load(Place(U_BRANCH), m, KT, w_ret[:, :, m * P:(m + 1) * P])
            sp.wait_ge(spilled[0], 16 * 17)
            sp.wait_ge(window, 18)
            for x in range(2):
                gate_load(gate_r[:, x, :], x, 0, gate_loaded[x])
            for m in range(2, KT):
                load(Place(U_BRANCH), m, KT, w_ret[:, :, m * P:(m + 1) * P])
                if m > 2:
                    sp.wait_ge(unit_free[(m - 1) % 2], Place(U_BRANCH).half(m - 1))
                    gate_load(gate_r[:, (m - 1) % 2, :], m - 1, 0, gate_loaded[(m - 1) % 2])
            sp.wait_ge(unit_free[1], Place(U_BRANCH).half(KT - 1))
            gate_load(gate_r[:, 1, :], KT - 1, 0, gate_loaded[1])
            for s in range(2):
                sp.wait_ge(w_split, U_ATT - 1 + s)
                for m in range(ATT_SLOT * s, ATT_SLOT * (s + 1)):
                    at = 2 * (m % ATT_SLOT)
                    sp.dma_start(w_raw[:, s, at:at + 2, :], w_att[:, :, m * P:(m + 1) * P]).then_inc(w_loaded[s], 16)
            sp.wait_ge(w_split, U_ATT + ATT_SLOT)
            sp.dma_start(w_raw[:, 0], w_out[:, :, 0:P]).then_inc(w_loaded[0], 16)
            sp.wait_ge(spilled[1], 16 * 17)
            sp.wait_ge(unit_done, U_ATT)
            for x in range(2):
                gate_load(gate_a[:, x, :], x, 1, gate_a_loaded[x])
            with sp.Fori(0, KT // 2 - 1) as i:
                for x in range(2):
                    sp.wait_ge(merged, i * 2 + (1 + x))
                    gate_load(gate_a[:, x, :], i * 2 + (2 + x), 1, gate_a_loaded[x])

            def x_load(j, m):
                sp.dma_start(temp[:, j, :], x_spill[ds(m, 1)].rearrange("a p t -> p (a t)")).then_inc(x_back[j], 16)

            load(Place(U_OUT), 1, KT, w_out[:, :, P:2 * P])
            sp.wait_ge(x_spilled, 16)
            sp.wait_ge(unit_done, U_OUT)
            for j in range(2):
                x_load(j, j)
            with sp.Fori(0, KT // 2 - 1) as i:
                for j in range(2):
                    load(Place(U_OUT + 2, 2, i), j, KT, w_out[:, :, ds(i * 2 * P + (2 + j) * P, P)])
                    sp.wait_ge(unit_free[j], i + (U_OUT // 2 + 1))
                    x_load(j, i * 2 + (2 + j))
            for c, nf in enumerate(FF_CHUNKS):
                f0 = sum(FF_CHUNKS[:c])
                with sp.Fori(0, nf) as f:
                    for j in range(2):
                        load(Place(U_FFN_CHUNK[c], 2, f), j, KT, w_gu[:, :, ds(f * P + (j * D_FF + f0 * P), P)])
                with sp.Fori(0, KT // 2) as i:
                    for j in range(2):
                        load(Place(U_FFN_CHUNK[c] + 2 * nf, 2, i), j, nf,
                             w_down[:, f0:f0 + nf, ds(i * 2 * P + j * P, P)])
            sp.wait_ge(unit_done, U_FINAL)
            sp.dma_start(gain_row[:], a["norm_final"].partition_broadcast(P)).then_inc(gain_loaded, 16)
            for t in range(CHUNKS + 1):
                sp.wait_ge(y_ready, t + 1)
                if t < CHUNKS:
                    sp.dma_start(out["y_prompt"][0, t * P:(t + 1) * P, :], y_row[:, t % 3, :]).then_inc(y_stored[t % 3], 16)
                else:
                    sp.dma_start(out["y_sample"][:, 0, :], y_row[0:SAMPLES, t % 3, :]).then_inc(y_stored[t % 3], 16)
            for g in range(3):
                sp.wait_ge(y_stored[g], 16 * 3)
            sp.wait_ge(s_stored, 16 * HEADS)
            sp.wait_ge(p_stored, 16 * HEADS)
            sp.wait_ge(v_stored, 16 * GROUPS)
            for x in range(4):
                sp.wait_ge(k_stored[x], 16 * K_STORES[GROUPS][x])
            sp.wait_ge(smp_out, 16 * GROUPS)

        @block.gpsimd
        def _(pool):
            def split(pl, j, kt, replaced=None):
                s = j % 2
                pool.wait_ge(w_loaded[s], pl.half(j) * 16 + 16)
                wait(pool, unit_done, pl.n(j) - 1 if replaced is None else replaced)
                raw, part = w_raw[:, s, 0:kt, :], w_part[:, s, :, 0:kt, :]
                one = const("ones").unsqueeze(1).to_broadcast([P, kt, P])
                pool.tensor_tensor(part[:, 0], raw, one, ALU.mult).then_inc(w_high, 1)
                pool.wait_ge(w_high, pl.n(j) + 1)
                pool.tensor_tensor(part[:, 1], raw, part[:, 0].bitcast(F32), ALU.subtract).then_inc(w_split, 1)

            pool.wait_ge(const_loaded, 16)
            for j in range(2):
                split(Place(0), j, KT)
            with pool.Fori(0, (U_ATT - 2) // 2) as i:
                for j in range(2):
                    split(Place(2, 2, i), j, KT)
            for s in range(2):
                pool.wait_ge(w_loaded[s], (U_ATT // 2 + ATT_SLOT) * 16)
                pool.wait_ge(unit_done, U_ATT - 1 + s)
                one = const("ones").unsqueeze(1).to_broadcast([P, KT, P])
                raw, part = w_raw[:, s], w_part[:, s]
                pool.tensor_tensor(part[:, 0], raw, one, ALU.mult).then_inc(w_high, ATT_SLOT)
                pool.wait_ge(w_high, U_ATT + ATT_SLOT * (s + 1))
                pool.tensor_tensor(part[:, 1], raw, part[:, 0].bitcast(F32), ALU.subtract).then_inc(w_split, ATT_SLOT)
            for m in range(POOL_LOW):
                if m == ATT_SLOT - 1:
                    split(Place(U_OUT), 0, KT, U_ATT + ATT_SLOT)
                pool.wait_ge(b_high, m + 1)
                pool.tensor_tensor(b_lo[:, m, :], wide[:, m, :], b_hi[:, m, :].bitcast(F32), ALU.subtract).then_inc(b_ready, 1)
            split(Place(U_OUT), 1, KT)
            with pool.Fori(0, KT // 2 - 1) as i:
                for j in range(2):
                    split(Place(U_OUT + 2, 2, i), j, KT)
            for c, nf in enumerate(FF_CHUNKS):
                with pool.Fori(0, nf) as f:
                    for j in range(2):
                        split(Place(U_FFN_CHUNK[c], 2, f), j, KT)
                with pool.Fori(0, KT // 2) as i:
                    for j in range(2):
                        split(Place(U_FFN_CHUNK[c] + 2 * nf, 2, i), j, nf)

        @block.tensor
        def _(pe):
            ident = const("ident")

            def unit(pl, j, kt, hi, lo, ready=None, between=None, at=None):
                s = j % 2
                slot, k0, weights = at or (s, 0, pl.n(j) + 1)
                pe.wait_ge(w_split, weights)
                wait(pe, unit_free[s], pl.half(j))
                for k in range(kt):
                    if between:
                        between(k)
                    if ready:
                        pe.wait_ge(ready[0], ready[1] + k + 1)
                    for part, (w, x) in enumerate(((0, hi), (0, lo), (1, hi))):
                        for n in range(PIECES):
                            mm = pe.matmul(unit_ps[s][:, n, 0:PIECE], w_part[:, slot, w, k0 + k, :],
                                           x[:, k, n * PIECE:(n + 1) * PIECE],
                                           start=(k == 0 and part == 0), stop=(k == kt - 1 and part == 2))
                mm.then_inc(unit_done, 1)
                if between:
                    between(kt)

            def begin(pl, j):
                wait(pe, task_free[j % 2], pl.half(j))
                return task_ps[j % 2]

            def end(mm, j):
                mm.then_inc(task_done[j % 2], 1)

            def taken(pl, j):
                pe.wait_ge(task_free[j % 2], pl.half(j) + 1)

            def norm_sum(j):
                if j == 0:
                    pe.wait_ge(summed, KT + 1)
                ps = begin(Place(T_NORM2), j)
                n = TOKENS // 4
                end(pe.matmul(ps[:, 0:n], const("ones"), temp[:, 3, j * n:(j + 1) * n], start=True, stop=True), j)

            pe.wait_ge(const_loaded, 16)
            for t in range(CHUNKS + 1):
                rows = P if t < CHUNKS else SAMPLES
                pe.wait_ge(x_loaded[t % X_ROWS], 16 * (t // X_ROWS + 1))
                for b in range(2):
                    ps = begin(Place(0), 2 * t + b)
                    for q in range(4):
                        c = (4 * b + q) * P
                        mm = pe.transpose(ps[:, q * P:q * P + rows], x_row[0:rows, t % X_ROWS, c:c + P], ident[0:rows, 0:rows])
                    end(mm, b)
            def x_norm(j):
                if j == 0:
                    pe.wait_ge(diag_ready, 1)
                ps = begin(Place(T_NORM1), j)
                for q, t in enumerate(X_NORM[j]):
                    n = P if t < CHUNKS else SAMPLES
                    mm = pe.matmul(ps[:, q * P:q * P + n], const("ones", n), diag[0:n, t, 0:n], start=True, stop=True)
                end(mm, j)

            unit(Place(0), 0, KT, a_hi, a_lo, ready=(a_ready, 0))
            unit(Place(0), 1, KT, a_hi, a_lo, between=lambda k: x_norm(k) if k < len(X_NORM) else None)
            for j in range(2, 4):
                unit(Place(0), j, KT, a_hi, a_lo)

            def ret_task(pl, up, heads, j):
                ps = begin(pl, j)
                if j == 0:
                    pe.wait_ge(unit_free[0], up.half(0))
                    pe.wait_ge(unit_free[1], up.half(0))
                if j < VS:
                    for q in range(2):
                        n = 2 * j + q
                        for v in range(2):
                            mm = pe.transpose(ps[:, (2 * q + v) * P:(2 * q + v + 1) * P], v_t[:, v, n * P:(n + 1) * P], ident)
                elif j == VS:
                    for v in range(2):
                        mm = pe.transpose(ps[0:SAMPLES, v * P:(v + 1) * P], v_t[:, v, SEQ:TOKENS], ident)
                elif j < KS:
                    for q in range(4):
                        n = 4 * (j - KT_) + q
                        mm = pe.transpose(ps[:, q * P:(q + 1) * P], k_t[:, n * P:(n + 1) * P], ident)
                elif j == KS:
                    mm = pe.transpose(ps[0:SAMPLES, 0:P], k_t[:, SEQ:TOKENS], ident)
                elif j < UP:
                    for q in range(4):
                        c = slice((4 * (j - SC) + q) * P, (4 * (j - SC) + q + 1) * P)
                        mm = pe.matmul(ps[:, q * P:(q + 1) * P], k_t[:, c], q_t[:, c], start=True, stop=True)
                elif j < OUT_:
                    for q in range(2):
                        n = 2 * (j - UP) + q
                        mm = pe.matmul(ps[:, q * DV:(q + 1) * DV], k_tok[:, n, :], v_tok[:, n, :], start=True, stop=True)
                elif j < OUTER:
                    if j == OUT_:
                        pe.wait_ge(q_ready, heads + 1)
                    for q in range(2):
                        n = 2 * (j - OUT_) + q
                        mm = pe.matmul(ps[:, q * DV:(q + 1) * DV], scores_t[:, n, :], v_tok[:, n, :], start=True, stop=n == 0)
                        if n:
                            mm = pe.matmul(ps[:, q * DV:(q + 1) * DV], q_t[:, n * P:(n + 1) * P], states[:, n - 1, :],
                                           start=False, stop=True)
                elif j < OS:
                    if j == OUTER:
                        pe.wait_ge(masked_ready, heads + 1)
                    for q in range(2):
                        mm = pe.matmul(ps[:, q * DV:(q + 1) * DV], s_kparts[:, 2 * (j - OUTER) + q, :], s_vparts[:],
                                       start=True, stop=True)
                elif j == OS:
                    taken(pl, OUTER + 3)
                    for n in range(SAMPLES):
                        mm = pe.matmul(ps[0:SAMPLES, 0:DV], s_qmask[:, n, :], s_state[:, n, :],
                                       start=(n == 0), stop=(n == SAMPLES - 1))
                elif j < TS:
                    if j == TURN:
                        pe.wait_ge(normed, heads * 2 + 2)
                    for v in range(2):
                        for q in range(2):
                            mm = pe.transpose(ps[:, (2 * v + q) * P:(2 * v + q + 1) * P],
                                              o_tok[:, 2 * (j - TURN) + q, v * P:(v + 1) * P], ident)
                else:
                    for v in range(2):
                        mm = pe.matmul(ps[:, v * SAMPLES:(v + 1) * SAMPLES], s_otok[:, v * P:(v + 1) * P],
                                       ident[0:SAMPLES, 0:SAMPLES], start=True, stop=True)
                end(mm, j)

            def ret_stage(pl, up, heads):
                for j in range(6):
                    unit(up, j, KT, a_hi, a_lo,
                         between=lambda k: ret_task(pl, up, heads, RET_AT[j, k]) if (j, k) in RET_AT else None)

            with pe.Fori(0, HEADS - 1) as h:
                ret_stage(Place(T_RET, RET_TASKS, h), Place(U_HEADS, 6, h), h)
            ret_stage(Place(T_RET + RET_TASKS * (HEADS - 1)), Place(U_GROUP0), HEADS - 1)

            def prep_task(pl, g, j):
                if j == 0:
                    pe.wait_ge(att_loaded, 16 * 2 * (g + 1))
                ps = begin(pl, j)
                kind, t0 = (2, 2 * j) if j < 4 else (1, 2 * (j - 4) + (0 if g == 2 else 4))
                for q in range(2):
                    for pair in range(2):
                        mm = pe.transpose(ps[:, (2 * q + pair) * P:(2 * q + pair + 1) * P],
                                          columns(att_in[:, kind, pair, :], g, t0 + q), ident)
                end(mm, j)

            def tile_scores(pl, nth, buf, prev, tiles):
                ps = [begin(pl, e) for e in range(2)]
                pe.wait_ge(window, nth + 1)
                keys = 2 * P if prev else P
                for t in range(tiles):
                    for pair in range(2):
                        at = (2 * t + pair) * keys
                        for e in range(2):
                            half = slice(64 * e, 64 * e + 64)
                            mm = pe.matmul(ps[e][:, at:at + keys], q_win[half, buf, pair, t, :],
                                           k_win[half, buf, pair, t * P:t * P + keys], start=True, stop=True)
                            if (t, pair) == (tiles - 1, 1):
                                end(mm, e)

            def tile_turn(pl, e, nth, buf, prev, tiles):
                ps = begin(pl, 2 + e)
                pe.wait_ge(exps, nth * 2 + (e + 1))
                for x in range(2 * tiles * (2 if prev else 1)):
                    mm = pe.transpose(ps[:, x * P:(x + 1) * P], probs[:, buf, e, x * P:(x + 1) * P], ident)
                end(mm, 2 + e)

            def tile_values(pl, e, buf, prev, tiles, v_tiles):
                ps = begin(pl, 4 + e)
                for t in range(tiles):
                    for pair in range(2):
                        at, col = (2 * t + pair) * HD, (2 * pair + e) * HD
                        blocks = ((2 * pair, v_tiles[0]), (2 * pair + 1, v_tiles[1])) if prev else ((2 * t + pair, v_tiles[t]),)
                        for x, (blk, tile) in enumerate(blocks):
                            v = flat(att_v[:, ds(tile, 1), col:col + HD])
                            mm = pe.matmul(ps[:, at:at + HD], probs_t[:, buf, e, blk, :], v,
                                           start=(x == 0), stop=(x == len(blocks) - 1))
                end(mm, 4 + e)

            def tile_task(j, pl, nth, buf, prev, tiles, v_tiles):
                if j == 0:
                    tile_scores(pl, nth, buf, prev, tiles)
                elif 2 <= j < 4:
                    tile_turn(pl, j - 2, nth, buf, prev, tiles)
                elif j >= 4:
                    tile_values(pl, j - 4, buf, prev, tiles, v_tiles)

            def beside(*args):
                def between(k):
                    for j in range(TILE_TASKS):
                        if TILE_AT[j] == k:
                            tile_task(j, *args)
                return between

            def preparing(pl, g):
                return lambda k: prep_task(pl, g, k - (9 - PREP[g])) if k >= 9 - PREP[g] else None

            unit(Place(U_GATE3), 0, KT, a_hi, a_lo)
            unit(Place(U_GATE3), 1, KT, a_hi, a_lo)
            unit(Place(U_GATE0), 0, KT, a_hi, a_lo, between=preparing(Place(T_PREP0), 0))
            unit(Place(U_GATE0), 1, KT, a_hi, a_lo, between=beside(Place(T_TILE0), 0, 0, False, 1, (0,)))
            with pe.Fori(0, 3) as i:
                for x in range(2):
                    up = Place(U_GROUPS + 2 * x, 4, i)
                    unit(up, 0, KT, a_hi, a_lo,
                         between=beside(Place(T_TILES0 + 6 * x, 12, i), i * 2 + (1 + x), (1 + x) % 2, True, 1,
                                        (i * 2 + x, i * 2 + (x + 1))))
                    unit(up, 1, KT, a_hi, a_lo)
            up = Place(U_GATES)
            unit(up, 0, KT, a_hi, a_lo, between=beside(Place(T_TILES0 + 36), 7, 1, True, 1, (6, 7)))
            unit(up, 1, KT, a_hi, a_lo, between=preparing(Place(T_PREP1), 1))
            for x in range(2):
                unit(Place(U_GATES + 2), x, KT, a_hi, a_lo,
                     between=beside(Place(T_FREE1 + 6 * x), 8 + x, x, False, 2, (2 * x, 2 * x + 1)))
            with pe.Fori(0, 2) as i:
                for x in range(2):
                    unit(Place(U_GATES + 4, 2, i), x, KT, a_hi, a_lo,
                         between=beside(Place(T_PREV1 + 6 * x, 12, i), i * 2 + (10 + x), x, True, 1,
                                        (i * 2 + x, i * 2 + (4 + x))))
            unit(Place(U_GATES + 8), 0, KT, a_hi, a_lo)
            unit(Place(U_GATES + 8), 1, KT, a_hi, a_lo, between=preparing(Place(T_PREP2), 2))
            with pe.Fori(0, 2) as i:
                for x in range(2):
                    unit(Place(U_GATES + 10, 2, i), x, KT, a_hi, a_lo,
                         between=beside(Place(T_FREE2 + 6 * x, 12, i), i * 2 + (14 + x), x, False, 2,
                                        (i * 4 + 2 * x, i * 4 + (2 * x + 1))))

            def sample_task(j):
                pl = Place(T_SAMPLE)
                if j == 0:
                    pe.wait_ge(qkv_loaded, 16)
                ps = begin(pl, j)
                if j < 6:
                    for q in range(4 - 2 * (j % 2)):
                        f = 4 * (j % 2) + q
                        mm = pe.transpose(ps[0:SAMPLES, q * P:(q + 1) * P],
                                          s_qkv_t[:, 6 * (f // 2) + 2 * (j // 2) + f % 2, :], ident)
                elif j == 6:
                    pe.wait_ge(smp_dve, 1)
                    pe.transpose(ps[0:32, 0:P], s_score[:, 0, :], ident)
                    mm = pe.transpose(ps[0:32, P:P + ROWS_B], s_score[0:ROWS_B, 1, :], ident[0:ROWS_B, 0:ROWS_B])
                elif j == 7:
                    pe.wait_ge(smp_dve, 2)
                    pe.transpose(ps[:, 0:32], s_prob[:, 0:P], ident[0:32, 0:32])
                    mm = pe.transpose(ps[0:ROWS_B, 32:64], s_prob[:, P:P + ROWS_B], ident[0:32, 0:32])
                elif j == 8:
                    taken(pl, 7)
                    for n in range(SAMPLES):
                        pe.matmul(ps[0:32, 0:4 * HD], s_ptok[:, 0, n, :], kv_a[:, n, 1, :], start=(n == 0), stop=False)
                        mm = pe.matmul(ps[0:32, 0:4 * HD], s_ptok[0:ROWS_B, 1, n, :], kv_b[:, n, 1, :],
                                       start=False, stop=(n == SAMPLES - 1))
                else:
                    taken(pl, 8)
                    for pair in range(2):
                        mm = pe.transpose(ps[:, 32 * pair:32 * pair + 32], s_out[:, pair * P:(pair + 1) * P], ident[0:32, 0:32])
                end(mm, j)

            def merge_task(j):
                if j == 0:
                    pe.wait_ge(mrg_dve, 2)
                ps = begin(Place(T_MERGE), j)
                for pair in range(2):
                    for q in range(2):
                        mm = pe.transpose(ps[:, (2 * pair + q) * P:(2 * pair + q + 1) * P],
                                          ao_tok[:, 2 * j + q, pair * P:(pair + 1) * P], ident)
                end(mm, j)

            def late_tasks(m):
                def between(k):
                    for j in range(T_NORM2 - T_SAMPLE):
                        if LATE_AT[j] == (m, k):
                            if j < T_MERGE - T_SAMPLE:
                                sample_task(j)
                            else:
                                merge_task(j - (T_MERGE - T_SAMPLE))
                return between

            for m in range(KT):
                unit(Place(U_BRANCH), m, KT, a_hi, a_lo, ready=(a_ready, KT) if m == 0 else None, between=late_tasks(m))
            for b in range(2):
                pe.wait_ge(task_free[b], T_NORM2 // 2)
            for m in range(KT):
                slot = m // ATT_SLOT
                unit(Place(U_ATT), m, 2, ao_hi, ao_lo, at=(slot, 2 * (m % ATT_SLOT), U_ATT + ATT_SLOT * (slot + 1)))
            with pe.Fori(0, KT // 2) as i:
                for j in range(2):
                    unit(Place(U_OUT, 2, i), j, KT, b_hi, b_lo, ready=(b_ready, 0))
            for c, nf in enumerate(FF_CHUNKS):
                peeled = 1 if c == 0 else 0
                if peeled:
                    unit(Place(U_FFN), 0, KT, a_hi, a_lo, ready=(a_ready, 2 * KT),
                         between=lambda k: norm_sum(k - 4) if 4 <= k < 8 else None)
                    unit(Place(U_FFN), 1, KT, a_hi, a_lo)
                with pe.Fori(0, nf - peeled) as f:
                    for j in range(2):
                        unit(Place(U_FFN_CHUNK[c] + 2 * peeled, 2, f), j, KT, a_hi, a_lo)
                with pe.Fori(0, KT // 2) as i:
                    for j in range(2):
                        unit(Place(U_FFN_CHUNK[c] + 2 * nf, 2, i), j, nf, b_hi, b_lo,
                             ready=(b_ready, KT + sum(FF_CHUNKS[:c])))
            for g in range(2):
                pe.wait_ge(unit_free[g], U_FINAL // 2)
            for t in range(CHUNKS + 1):
                n = P if t < CHUNKS else SAMPLES
                wait(pe, y_ready, t - 2)
                for k in range(KT):
                    mm = pe.transpose(y_ps[t % 3][0:n, k // 4, (k % 4) * P:(k % 4 + 1) * P], wide[:, k, t * P:t * P + n], ident)
                mm.then_inc(y_turned, 1)

        @block.scalar
        def _(act):
            def full(pl, j):
                act.wait_ge(task_done[j % 2], pl.half(j) + 1)
                return task_ps[j % 2]

            def empty(ins, j):
                ins.then_inc(task_free[j % 2], 1)

            def norm_root(pl):
                n = TOKENS // 4
                for j in range(4):
                    ps = full(pl, j)
                    empty(act.activation(rstd[:, j * n:(j + 1) * n], ps[:, 0:n], ACT.Sqrt, scale=1.0 / D,
                                         bias=const("eps")[:, 0:1]), j)

            act.dma_start(consts[:], a["c_small"]).then_inc(const_loaded, 16)
            act.dma_start(gains[:], a["norm_gains"]).then_inc(gains_loaded, 16)

            def turned(t):
                n = P if t < CHUNKS else SAMPLES
                empty(act.activation(wide[:, 4:8, t * P:t * P + n],
                                     full(Place(0), 2 * t + 1)[:].rearrange("p (q t) -> p q t", q=4)[:, :, 0:n], ACT.Copy), 1)

            for t in range(CHUNKS + 1):
                n = P if t < CHUNKS else SAMPLES
                act.wait_ge(x_loaded[t % X_ROWS], 16 * (t // X_ROWS + 1))
                wait(act, squared, t)
                act.activation(x_square[0:n, :], x_row[0:n, t % X_ROWS, :], ACT.Square, accum_out=x_factor[0:n, t:t + 1])\
                   .then_inc(squared, 1)
                turned(t)
            for b in range(2):
                act.wait_ge(task_free[b], CHUNKS + 1)
            act.wait_ge(gains_loaded, 16)
            for k in range(KT):
                act.activation(a_hi[:, k, :], wide[:, k, :], ACT.Copy, scale=gains[:, 0, k:k + 1]).then_inc(a_high, 1)
            act.wait_ge(squared, CHUNKS + 1)
            for n, c in ((P, slice(0, CHUNKS)), (SAMPLES, slice(CHUNKS, CHUNKS + 1))):
                act.activation(x_factor[0:n, c], x_factor[0:n, c], ACT.Sqrt, scale=1.0 / D,
                               bias=const("eps", n)[:, 0:1]).then_inc(x_root, 1)
            for j, tiles in enumerate(X_NORM):
                n = min(len(tiles) * P, TOKENS - tiles[0] * P)
                c = tiles[0] * P
                empty(act.activation(rstd[:, c:c + n], full(Place(T_NORM1), j)[:, 0:n], ACT.Copy), j)

            def load_states(h):
                act.dma_start(s_state[:], a["state_ret"][0][:, ds(h, 1)].rearrange("n a d v -> d (n a) v")).then_inc(s_loaded, 16)

            for b in range(2):
                act.wait_ge(task_free[b], T_RET // 2)
            load_states(0)

            def ret_slot(pl, h, j):
                for x in {0: range(VT, KT_), 1: (KS,), 2: range(OUT_, OUTER), 3: (OS,)}.get(j, ()):
                    ps = full(pl, x)
                    if x < VS:
                        ins = act.activation(v_tok[:, 2 * x:2 * x + 2, :], ps[:].rearrange("p (q d) -> p q d", q=2), ACT.Copy)
                    elif x == VS:
                        ins = act.activation(s_vtok[:], ps[0:SAMPLES, 0:DV], ACT.Copy)
                    elif x == KS:
                        ins = act.activation(s_ktok[:], ps[0:SAMPLES, 0:DK], ACT.Copy)
                    elif x < OUTER:
                        n = 2 * (x - OUT_)
                        ins = act.activation(o_tok[:, n:n + 2, :], ps[:].rearrange("p (q d) -> p q d", q=2), ACT.Copy)
                    else:
                        ins = act.activation(s_otok[:], ps[0:SAMPLES, 0:DV], ACT.Copy)
                    empty(ins, x)
                if j == 2:
                    act.wait_ge(task_free[1], pl.half(UP + 3) + 1)
                    act.dma_start(out["p_ret"][0, 0][ds(h, 1)].rearrange("a d v -> d (a v)"), states[:, CHUNKS - 1, :])\
                       .then_inc(p_stored, 16)
                if j == 3:
                    act.wait_ge(task_free[0], pl.half(OUTER + 2) + 1)
                    act.wait_ge(task_free[1], pl.half(OUTER + 3) + 1)
                    act.dma_start(out["s_ret"][0][:, ds(h, 1)].rearrange("n a d v -> d (n a) v"), s_state[:]).then_inc(s_stored, 16)
                    act.wait_ge(normed, h * 2 + 1)
                    act.activation(spread[:, 0:CHUNKS], flat(moments[:, 0:CHUNKS, 1:2]), ACT.Sqrt, bias=const("eps")[:, 1:2])
                    act.activation(spread[0:SAMPLES, CHUNKS:CHUNKS + 1], moments[0:SAMPLES, CHUNKS, 1:2], ACT.Sqrt,
                                   bias=const("eps", SAMPLES)[:, 1:2]).then_inc(root, 1)

            def in_place(pl, j, func):
                act.wait_ge(unit_free[j % 2], pl.half(j) + 1)
                act.activation(stage[:, j % 2, :], stage[:, j % 2, :], func).then_inc(silu_done, 1)

            with act.Fori(0, HEADS - 1) as h:
                pl = Place(T_RET, RET_TASKS, h)
                up = Place(U_HEADS, 6, h)
                for j in range(6):
                    ret_slot(pl, h, j)
                    if j >= 4:
                        in_place(up, j, ACT.Silu)
                act.wait_ge(s_stored, h * 16 + 16)
                load_states(h + 1)

            def spill(pl, j, dst):
                act.wait_ge(unit_free[j % 2], pl.half(j) + 1)
                act.dma_start(dst, stage[:, j % 2, :]).then_inc(spilled[j % 2], 16)

            for j in range(6):
                ret_slot(Place(T_RET + RET_TASKS * (HEADS - 1)), HEADS - 1, j)
                spill(Place(U_GROUP0), j, att_spill[j])

            def load_group(g):
                for x in range(2):
                    act.wait_ge(spilled[x], 16 * (3 * (g + 1) + (g > 0)))
                act.dma_start(att_in[:].rearrange("p a b t -> p (a b) t"),
                              att_spill[6 * g:6 * g + 6, :, 0:SEQ].rearrange("a p t -> p a t")).then_inc(att_loaded, 16)
                n = 1024 if g < 2 else 512
                act.dma_start(bias[:, 0:n], a[f"c_bias{g}"]).then_inc(att_loaded, 16)

            for b in range(2):
                act.wait_ge(task_free[b], T_ATT // 2)
            act.wait_ge(s_stored, 16 * HEADS)
            act.wait_ge(p_stored, 16 * HEADS)
            load_group(0)

            def kv_store(g, kind, t0, n, src, stored):
                rows = p_kv[g][0, 0][:, kind - 1].rearrange("r h d -> r (h d)")
                if g == 0:
                    dst, src = rows, src[:, n - 1, :]
                elif g == 1:
                    dst = rows.rearrange("(p t) d -> p t d", t=4)[:, t0 - 4:t0 - 4 + n, :]
                else:
                    dst = rows.rearrange("(p t) d -> p t d", t=8)[:, t0:t0 + n, :]
                act.dma_start(dst, src).then_inc(stored, 16)

            def prep(pl, g):
                wait(act, v_stored, 16 * g)
                for j in range(PREP[g]):
                    ps = full(pl, j)[:].rearrange("p (q d) -> p q d", q=2)
                    if j < 4:
                        empty(act.activation(att_v[:, 2 * j:2 * j + 2, :], ps, ACT.Copy), j)
                        continue
                    wait(act, k_stored[j - 4], 16 * K_STORES[g][j - 4])
                    empty(act.activation(att_kout[:, j - 4], ps, ACT.Copy), j)
                    if j == 4:
                        for b in range(2):
                            act.wait_ge(task_free[b], pl.half(2 + b) + 1)
                        t0 = (7, 4, 0)[g]
                        kv_store(g, 2, t0, 8 - t0, att_v[:, t0:8, :], v_stored)
                    if g or j == 5:
                        act.wait_ge(task_free[j % 2], pl.half(j) + 1)
                        kv_store(g, 1, 2 * (j - 4) + (0 if g == 2 else 4), 2, att_kout[:, j - 4], k_stored[j - 4])

            def windows(g, t, buf, prev, tiles):
                for pair in range(2):
                    queries, keys = att_in[:, 0, pair, :], att_in[:, 1, pair, :]
                    if prev:
                        act.activation(k_win[:, buf, pair, :], columns(keys, g, t - 1 if g == 0 else t - 4, 2 * P), ACT.Copy)
                    for x in range(tiles):
                        if not prev:
                            act.activation(k_win[:, buf, pair, x * P:(x + 1) * P], columns(keys, g, t + x), ACT.Copy)
                        ins = act.activation(q_win[:, buf, pair, x, :], columns(queries, g, t + x), ACT.Copy, scale=HD ** -0.5)
                ins.then_inc(window, 1)

            def tile(pl, nth, buf, prev, tiles, dst, following):
                keys = 2 * P if prev else P
                for e in range(2):
                    act.wait_ge(peak, nth * 2 + (e + 1))
                    for x in range(tiles):
                        for pair in range(2):
                            s = probs[:, buf, e, (2 * x + pair) * keys:(2 * x + pair + 1) * keys]
                            o = o_ext[:, buf, x, 2 * pair + e, :]
                            ins = act.activation(s, s, ACT.Exp, bias=o[:, HD + 1:HD + 2], accum_out=o[:, HD:HD + 1])
                    ins.then_inc(exps, 1)
                if following:
                    following()
                for e in range(2):
                    ps = full(pl, 4 + e)[:, 0:tiles * 2 * HD].rearrange("p (x d) -> p x d", d=HD)
                    o = o_ext[:, buf, 0:tiles].rearrange("p x h d -> p (x h) d")[:, e::2, 0:HD]
                    empty(act.activation(o, ps, ACT.Copy), 4 + e)
                for e in range(2):
                    act.wait_ge(task_free[e], pl.half(4 + e) + 1)
                act.wait_ge(exps, nth * 2 + 2)
                act.dma_start(dst, o_ext[:, buf, 0:tiles].rearrange("p x h d -> p x (h d)")).then_inc(rows_stored[buf], 16)

            def rows0(t):
                return att_rows[0].rearrange("(t p) d -> p t d", p=P)[:, ds(t, 1)]

            def rows1(half, t, n):
                return att_rows[1].rearrange("(f p t) d -> p f t d", f=2, t=4)[:, half, ds(t, n)]

            def rows2(t):
                return att_rows[2].rearrange("(p t) d -> p t d", t=8)[:, ds(t, 2)]

            def gate(pl, j, m):
                in_place(pl, j, ACT.Sigmoid)
                act.wait_ge(silu_done, m * 2 + (2 * HEADS + j + 1))
                act.dma_start(gate_spill[ds(m * 2 + j, 1)].rearrange("a p t -> p (a t)"), stage[:, j, :]).then_inc(spilled[j], 16)

            def start_group(pl, g, tiles):
                act.wait_ge(att_loaded, 16 * 2 * (g + 1))
                windows(g, 0, 0, False, tiles)
                prep(pl, g)

            def next_group(g, nth):
                act.wait_ge(window, nth)
                act.wait_ge(peak, 2 * nth)
                load_group(g)

            for j in range(2):
                in_place(Place(U_GATE3), j, ACT.Silu)
            start_group(Place(T_PREP0), 0, 1)
            gate(Place(U_GATE0), 0, 0)
            tile(Place(T_TILE0), 0, 0, False, 1, rows0(0), lambda: windows(0, 1, 1, True, 1))
            gate(Place(U_GATE0), 1, 0)
            with act.Fori(0, 3) as i:
                for x in range(2):
                    tile(Place(T_TILES0 + 6 * x, 12, i), i * 2 + (1 + x), (1 + x) % 2, True, 1, rows0(i * 2 + (1 + x)),
                         lambda: windows(0, i * 2 + (2 + x), x, True, 1))
                    for j in range(2):
                        spill(Place(U_GROUPS + 2 * x, 4, i), j,
                              att_spill[ds(i * 4 + (6 + 2 * x + j), 1)].rearrange("a p t -> p (a t)"))
            tile(Place(T_TILES0 + 36), 7, 1, True, 1, rows0(7), lambda: next_group(1, 8))
            gate(Place(U_GATES), 0, 1)
            start_group(Place(T_PREP1), 1, 2)
            gate(Place(U_GATES), 1, 1)
            for x in range(2):
                tile(Place(T_FREE1 + 6 * x), 8 + x, x, False, 2, rows1(0, 2 * x, 2),
                     lambda: windows(1, 4, 0, True, 1) if x else windows(1, 2, 1, False, 2))
                gate(Place(U_GATES + 2), x, 2)
            for n in range(4):
                tile(Place(T_PREV1 + 6 * n), 10 + n, n % 2, True, 1, rows1(1, n, 1),
                     lambda: windows(1, 5 + n, (n + 1) % 2, True, 1) if n < 3 else next_group(2, 14))
                gate(Place(U_GATES + 4 + 2 * (n // 2)), n % 2, 3 + n // 2)
            gate(Place(U_GATES + 8), 0, 5)
            start_group(Place(T_PREP2), 2, 2)
            gate(Place(U_GATES + 8), 1, 5)

            def high_part(k):
                act.activation(a_hi[:, k, :], wide[:, k, :], ACT.Copy).then_inc(a_high, 1)

            def next_stage():
                act.wait_ge(window, 18)
                act.dma_start(s_qkv_t[:], att_spill[:, :, SEQ:TOKENS].rearrange("a p t -> p a t")).then_inc(qkv_loaded, 16)
                act.wait_ge(unit_done, U_BRANCH)
                for k in range(2):
                    high_part(k)

            for n in range(4):
                tile(Place(T_FREE2 + 6 * n), 14 + n, n % 2, False, 2, rows2(2 * n),
                     (lambda: windows(2, 2 * n + 2, (n + 1) % 2, False, 2)) if n < 3 else next_stage)
                if n < 3:
                    gate(Place(U_GATES + 10 + 2 * (n // 2)), n % 2, 6 + n // 2)

            pl = Place(T_SAMPLE)

            def sample_rows_out(j):
                ps = full(pl, j)
                c, n = (0, 512) if j % 2 == 0 else (512, 256)
                empty(act.activation(s_qkv[:, j // 2, c:c + n], ps[0:SAMPLES, 0:n], ACT.Copy), j)

            for k in range(2, KT):
                high_part(k)
                if k == 3:
                    act.wait_ge(v_stored, 16 * GROUPS)
                    for x in range(4):
                        act.wait_ge(k_stored[x], 16 * K_STORES[GROUPS][x])
                    act.dma_start(kv_a[:], a["cache_kv_w128"][0].rearrange("n r c h d -> r n c (h d)")).then_inc(cache_loaded, 16)
                    for name, by, r0, r1 in (("cache_kv_w512", 4, 0, ROWS_B1),
                                             ("cache_kv_w2048", 16, ROWS_B1, ROWS_B1 + ROWS_B2)):
                        rows = a[name][0].rearrange("n (r s) c h d -> r s n c (h d)", s=by)[:, 0]
                        act.dma_start(kv_b[r0:r1], rows).then_inc(cache_loaded, 16)
                if k >= 3:
                    sample_rows_out(k - 3)
            sample_rows_out(5)
            for b in range(2):
                act.wait_ge(task_free[b], pl.half(4 + b) + 1)
            act.dma_start(sample_rows.rearrange("a n c -> n a c"), s_qkv[:]).then_inc(rows_written, 16)
            for g in range(GROUPS):
                act.dma_start(s_kv[g][0, :, 0].rearrange("n c h d -> n c (h d)"),
                              s_qkv[:, 1:3, g * 256:(g + 1) * 256]).then_inc(smp_out, 16)
            gate(Place(U_GATES + 12), 1, 7)
            act.wait_ge(rows_written, 16)
            act.wait_ge(smp_out, 16 * GROUPS)
            r2 = ROWS_B1 + ROWS_B2
            act.dma_start(q_a[:], sample_rows[0, :, 0:256].partition_broadcast(P)).then_inc(cache_loaded, 16)
            act.dma_start(q_b[0:ROWS_B1], sample_rows[0, :, 256:512].partition_broadcast(ROWS_B1)).then_inc(cache_loaded, 16)
            act.dma_start(q_b[ROWS_B1:r2], sample_rows[0, :, 512:768].partition_broadcast(ROWS_B2)).then_inc(cache_loaded, 16)
            by_group = sample_rows.rearrange("a n (g c) -> a g n c", g=GROUPS)
            act.dma_start(q_b[r2:ROWS_B], by_group[0]).then_inc(cache_loaded, 16)
            for c in range(2):
                act.dma_start(kv_b[r2:ROWS_B, :, c, :], by_group[1 + c]).then_inc(cache_loaded, 16)
            act.wait_ge(smp_act, 1)
            act.activation(s_prob[:], s_prob[:], ACT.Exp, bias=s_small[:, 0:1], accum_out=s_small[:, 1:2]).then_inc(root, 1)

            for b in range(2):
                act.wait_ge(task_free[b], T_MERGE // 2)
            for x in range(2):
                act.wait_ge(rows_stored[x], 16 * 9)
            for g in range(GROUPS):
                act.dma_start(parts[:, g].rearrange("p (t h) d -> p t (h d)", h=AH),
                              att_rows[g].rearrange("(t p) d -> p t d", p=P)).then_inc(parts_loaded, 16)
            act.wait_ge(mrg_dve, 1)
            act.activation(mrg[:, 0:3, :], mrg[:, 0:3, :], ACT.Exp).then_inc(mrg_act, 1)

            for m in range(KT):
                act.wait_ge(merged, m + 1)
                act.activation(b_hi[:, m, :], wide[:, m, :], ACT.Copy).then_inc(b_high, 1)
            for m in range(KT):
                act.wait_ge(unit_free[m % 2], Place(U_OUT).half(m) + 1)
                act.wait_ge(summed, m + 1)
                act.activation(temp[:, 2, :], wide[:, m, :], ACT.Square).then_inc(squared, 1)
            norm_root(Place(T_NORM2))
            for c, nf in enumerate(FF_CHUNKS):
                with act.Fori(0, nf) as f:
                    act.wait_ge(unit_free[0], Place(U_FFN_CHUNK[c], 2, f).half(0) + 1)
                    act.activation(temp[:, 0, :], temp[:, 0, :], ACT.Silu).then_inc(silu_done, 1)
            for t in range(CHUNKS + 1):
                n, g = P if t < CHUNKS else SAMPLES, t % 3
                act.wait_ge(y_turned, t + 1)
                if t:
                    act.wait_ge(act_step, 2 * t)
                act.activation(y_square[0:n, :].rearrange("p (a b) -> p a b", a=2), y_ps[g][0:n], ACT.Square,
                               accum_out=fin[0:n, g, 0:1]).then_inc(act_step, 1)
                act.wait_ge(act_step, 2 * t + 1)
                act.activation(fin[0:n, g, 0:1], fin[0:n, g, 0:1], ACT.Sqrt, scale=1.0 / D, bias=const("eps", n)[:, 0:1])\
                   .then_inc(act_step, 1)

        @block.vector
        def _(dve):
            step = Steps(dve, dve_step)

            def full(pl, j):
                dve.wait_ge(task_done[j % 2], pl.half(j) + 1)
                return task_ps[j % 2]

            def empty(ins, j):
                ins.then_inc(task_free[j % 2], 1)

            def take(pl, j):
                dve.wait_ge(unit_done, pl.n(j) + 1)
                return unit_out(j % 2)

            def scaled(pl, j, dst, by=None):
                ps = take(pl, j)
                if by is None:
                    ins = dve.tensor_tensor(pieces(dst), ps, pieces(rstd[:]), ALU.mult)
                else:
                    ins = dve.scalar_tensor_tensor(out=pieces(dst), in0=ps, scalar=by, in1=pieces(rstd[:]),
                                                   op0=ALU.mult, op1=ALU.mult)
                ins.then_inc(unit_free[j % 2], 1)

            def norm_factor(tasks):
                for b in range(2):
                    dve.wait_ge(task_free[b], tasks // 2)
                dve.reciprocal(rstd[:], rstd[:]).then_inc(rstd_ready, 1)

            for t in range(CHUNKS + 1):
                n = P if t < CHUNKS else SAMPLES
                empty(dve.tensor_copy(wide[:, 0:4, t * P:t * P + n],
                                      full(Place(0), 2 * t)[:].rearrange("p (q t) -> p q t", q=4)[:, :, 0:n]), 0)
            dve.wait_ge(const_loaded, 16)
            dve.wait_ge(gains_loaded, 16)
            for b in range(2):
                dve.wait_ge(task_free[b], CHUNKS + 1)
            for k in range(KT):
                dve.wait_ge(a_high, k + 1)
                dve.scalar_tensor_tensor(out=a_lo[:, k, :], in0=wide[:, k, :], scalar=gains[:, 0, k:k + 1],
                                         in1=a_hi[:, k, :].bitcast(F32), op0=ALU.mult, op1=ALU.subtract).then_inc(a_ready, 1)
            dve.wait_ge(x_root, 2)
            step(dve.reciprocal(x_factor[:, 0:CHUNKS], x_factor[:, 0:CHUNKS]))
            step(dve.reciprocal(x_factor[0:SAMPLES, CHUNKS:CHUNKS + 1], x_factor[0:SAMPLES, CHUNKS:CHUNKS + 1]))
            step.settle()
            step(dve.tensor_scalar(diag[0:SAMPLES, CHUNKS, 0:SAMPLES], const("ident", SAMPLES)[:, 0:SAMPLES],
                                   x_factor[0:SAMPLES, CHUNKS:CHUNKS + 1], None, ALU.mult))
            dve.tensor_tensor(diag[:, 0:CHUNKS, :], const("ident").unsqueeze(1).to_broadcast([P, CHUNKS, P]),
                              x_factor[:, 0:CHUNKS].unsqueeze(2).to_broadcast([P, CHUNKS, P]), ALU.mult).then_inc(diag_ready, 1)
            for b in range(2):
                dve.wait_ge(task_free[b], T_RET // 2)
            scaled(Place(0), 0, v_t[:, 0, :])
            scaled(Place(0), 1, v_t[:, 1, :])
            step(dve.memset(s_kparts[:].bitcast(F32), 0.0))
            step(dve.memset(s_vparts[:].bitcast(F32), 0.0))
            step.settle()
            scaled(Place(0), 2, k_t[:])
            scaled(Place(0), 3, q_t[:], DK ** -0.5)
            dve.wait_ge(table_loaded, 16 * 2)
            dve.wait_ge(x_spilled, 16)

            def ret_slot(pl, h, j):
                if j < 2:
                    empty(dve.tensor_scalar(k_tok[:, 4 * j:4 * j + 4, :],
                                            full(pl, KT_ + j)[:].rearrange("p (q d) -> p q d", q=4),
                                            const("tail")[:, ds(h, 1)], None, ALU.mult), KT_ + j)
                if j == 1:
                    dve.wait_ge(task_free[KS % 2], pl.half(KS) + 1)
                    eye = const("eye8").rearrange("p (a b) -> p a b", a=SAMPLES)
                    step(dve.tensor_copy(s_khigh[:], s_ktok[:]))
                    for row in (0, 32):
                        step(dve.tensor_copy(s_vparts[row:row + SAMPLES, :], s_vtok[:]))
                    step.settle()
                    step(dve.tensor_tensor(s_klow[:], s_ktok[:], s_khigh[:].bitcast(F32), ALU.subtract))
                    dve.tensor_tensor(s_vparts[64:64 + SAMPLES, :], s_vtok[:], s_vparts[0:SAMPLES, :].bitcast(F32), ALU.subtract)
                    step.settle()
                    for row, part in ((0, s_khigh[:].bitcast(F32)), (32, s_klow[:]), (64, s_khigh[:].bitcast(F32))):
                        dve.tensor_tensor(s_kparts[row:row + SAMPLES], part.unsqueeze(1).to_broadcast([SAMPLES, SAMPLES, DK]),
                                          masks8().to_broadcast([SAMPLES, SAMPLES, DK]), ALU.mult)
                    dve.tensor_tensor(s_qmask[:], q_t[:, SEQ:TOKENS].unsqueeze(2).to_broadcast([P, SAMPLES, SAMPLES]),
                                      eye, ALU.mult).then_inc(masked_ready, 1)
                    for x in range(2):
                        ps = full(pl, SC + x)[:].rearrange("p (q t) -> p q t", q=4)
                        empty(dve.tensor_tensor(scores_t[:, 4 * x:4 * x + 4, :], ps,
                                                decay[:, ds(h, 1), :].to_broadcast([P, 4, P]), ALU.mult), SC + x)
                    q = q_t[:, 0:SEQ].rearrange("p (n t) -> p n t", t=P)
                    dve.tensor_tensor(q, q, inner[:, ds(h, 1), :].to_broadcast([P, CHUNKS, P]), ALU.mult).then_inc(q_ready, 1)
                if j in (1, 2):
                    for x in (range(UP, UP + 3) if j == 1 else (UP + 3,)):
                        ps = full(pl, x)
                        for q in range(2):
                            n = 2 * (x - UP) + q
                            u = ps[:, q * DV:(q + 1) * DV]
                            if n == 0:
                                ins = dve.tensor_copy(states[:, 0, :], u)
                            else:
                                ins = dve.scalar_tensor_tensor(out=states[:, n, :], in0=states[:, n - 1, :],
                                                               scalar=const("gamma_c")[:, ds(h, 1)], in1=u,
                                                               op0=ALU.mult, op1=ALU.add)
                            if q == 0:
                                step(ins)
                                step.settle()
                            else:
                                empty(ins, x)
                                dve.wait_ge(task_free[x % 2], pl.half(x) + 1)
                if j in (2, 3):
                    for x in (range(OUTER, OUTER + 3) if j == 2 else (OUTER + 3,)):
                        if x == OUTER:
                            dve.wait_ge(s_loaded, h * 16 + 16)
                        s = s_state[:, 2 * (x - OUTER):2 * (x - OUTER) + 2, :]
                        ps = full(pl, x)[:].rearrange("p (q d) -> p q d", q=2)
                        empty(dve.scalar_tensor_tensor(out=s, in0=s, scalar=const("gamma")[:, ds(h, 1)], in1=ps,
                                                       op0=ALU.mult, op1=ALU.add), x)
                if j == 3:
                    for x in (OUT_ + 2, OUT_ + 3, OS):
                        dve.wait_ge(task_free[x % 2], pl.half(x) + 1)
                    rows = [(o_tok[:, n, :], P) for n in range(CHUNKS)] + [(s_otok[:], SAMPLES)]
                    for n, (o, r) in enumerate(rows):
                        step(dve.bn_stats(stats[0:r, n, :], o))
                    step.settle()
                    dve.memset(spread[:], 1.0)
                    for n, (o, r) in enumerate(rows):
                        ins = dve.bn_aggr(moments[0:r, n, :], stats[0:r, n, :])
                        if n < CHUNKS:
                            step(ins)
                    ins.then_inc(normed, 1)
                    dve.wait_ge(root, h + 1)
                    step(dve.reciprocal(spread[:, 0:CHUNKS], spread[:, 0:CHUNKS]))
                    step(dve.reciprocal(spread[0:SAMPLES, CHUNKS:CHUNKS + 1], spread[0:SAMPLES, CHUNKS:CHUNKS + 1]))
                    step.settle()
                    dve.wait_ge(normed, h * 2 + 1)
                    for n, (o, r) in enumerate(rows):
                        ins = dve.tensor_scalar(o, o, moments[0:r, n, 0:1], spread[0:r, n:n + 1], ALU.subtract, ALU.mult)
                    ins.then_inc(normed, 1)
                if j == 4:
                    dve.wait_ge(p_stored, h * 16 + 16)
                    for x in range(4):
                        ps = full(pl, TURN + x)[:].rearrange("p (v t) -> p v t", v=2)
                        empty(dve.tensor_copy(wide[:, ds(h * 2, 2), 2 * P * x:2 * P * (x + 1)], ps), TURN + x)
                    ps = full(pl, TS)[:, 0:2 * SAMPLES].rearrange("p (v t) -> p v t", v=2)
                    empty(dve.tensor_copy(wide[:, ds(h * 2, 2), SEQ:TOKENS], ps), TS)

            def masks8():
                return const("ident", SAMPLES)[:, 0:SAMPLES].unsqueeze(2)

            def gated(pl, j, h, v, done):
                scaled(pl, j, stage[:, j % 2, :])
                dve.wait_ge(silu_done, done)
                for b in range(2):
                    dve.wait_ge(task_free[b], h * (RET_TASKS // 2) + (T_RET + RET_TASKS) // 2)
                t = flat(wide[:, ds(h * 2 + v, 1), :])
                step(dve.tensor_tensor(t, t, stage[:, j % 2, :], ALU.mult))

            with dve.Fori(0, HEADS - 1) as h:
                step.enter(h, STEPS_HEAD)
                up = Place(U_HEADS, 6, h)
                for j in range(6):
                    ret_slot(Place(T_RET, RET_TASKS, h), h, j)
                    if j < 2:
                        scaled(up, j, v_t[:, j, :])
                    elif j == 2:
                        scaled(up, j, k_t[:])
                    elif j == 3:
                        scaled(up, j, q_t[:], DK ** -0.5)
                    else:
                        gated(up, j, h, j - 4, h * 2 + (j - 3))
                step.leave(HEADS - 1)

            def staged(pl, j, before):
                wait(dve, spilled[j % 2], before)
                scaled(pl, j, stage[:, j % 2, :])

            for j in range(6):
                ret_slot(Place(T_RET + RET_TASKS * (HEADS - 1)), HEADS - 1, j)
                staged(Place(U_GROUP0), j, 16 * (j // 2))
            for j in range(2):
                dve.wait_ge(spilled[j], 16 * 3)
                gated(Place(U_GATE3), j, HEADS - 1, j, 2 * (HEADS - 1) + j + 1)

            def tile(pl, g, buf, prev, tiles, stored):
                wait(dve, rows_stored[buf], stored)
                keys = 2 * P if prev else P
                n = 2 * tiles
                for e in range(2):
                    ps = full(pl, e)[:, 0:n * keys]
                    s = probs[:, buf, e, 0:n * keys]
                    o = o_ext[:, buf, 0:tiles].rearrange("p x h d -> p (x h) d")[:, e::2, HD + 1:HD + 2]
                    if g == 2:
                        b = bias[:, 0:512].rearrange("p (e a k) -> p e a k", e=2, a=2)[:, e]
                    else:
                        b = bias[:].rearrange("p (e a k) -> p e a k", e=2, a=2)[:, e, :, 2 * P - keys:2 * P]
                    if tiles == 2:
                        b = b.unsqueeze(1).to_broadcast([P, 2, 2, P])
                        ps, sx = (y.rearrange("p (t a k) -> p t a k", t=2, a=2) for y in (ps, s))
                    else:
                        ps, sx = (y.rearrange("p (a k) -> p a k", a=2) for y in (ps, s))
                    empty(dve.tensor_tensor(sx, ps, b, ALU.add), e)
                    dve.wait_ge(task_free[e], pl.half(e) + 1)
                    dve.tensor_reduce(o, s.rearrange("p (x k) -> p x k", k=keys), AX_X, ALU.max, negate=True).then_inc(peak, 1)
                for e in range(2):
                    ps = full(pl, 2 + e)[:, 0:n * keys]
                    empty(dve.tensor_copy(probs_t[:, buf, e].rearrange("p x t -> p (x t)")[:, 0:n * keys], ps), 2 + e)

            dve.wait_ge(att_loaded, 16 * 2)
            staged(Place(U_GATE0), 0, 16 * 3)
            tile(Place(T_TILE0), 0, 0, False, 1, 0)
            staged(Place(U_GATE0), 1, 16 * 3)
            with dve.Fori(0, 3) as i:
                for x in range(2):
                    tile(Place(T_TILES0 + 6 * x, 12, i), 0, (1 + x) % 2, True, 1, i * 16 + 16 if x else 0)
                    for j in range(2):
                        staged(Place(U_GROUPS + 2 * x, 4, i), j, i * 32 + 16 * (4 + x))
                dve.wait_ge(rows_stored[1], i * 16 + 16)
            tile(Place(T_TILES0 + 36), 0, 1, True, 1, 16 * 3)
            for j in range(2):
                staged(Place(U_GATES), j, 16 * 10)
            dve.wait_ge(att_loaded, 16 * 4)
            for x in range(2):
                tile(Place(T_FREE1 + 6 * x), 1, x, False, 2, 16 * 4)
                staged(Place(U_GATES + 2), x, 16 * 11)
            with dve.Fori(0, 2) as i:
                for x in range(2):
                    tile(Place(T_PREV1 + 6 * x, 12, i), 1, x, True, 1, i * 16 + 16 * 5)
                    staged(Place(U_GATES + 4, 2, i), x, i * 16 + 16 * 12)
            for j in range(2):
                staged(Place(U_GATES + 8), j, 16 * 14)
            dve.wait_ge(att_loaded, 16 * 6)
            with dve.Fori(0, 2) as i:
                for x in range(2):
                    tile(Place(T_FREE2 + 6 * x, 12, i), 2, x, False, 2, i * 16 + 16 * 7)
                    staged(Place(U_GATES + 10, 2, i), x, i * 16 + 16 * 15)

            for k in range(KT):
                dve.wait_ge(a_high, KT + k + 1)
                dve.tensor_tensor(a_lo[:, k, :], wide[:, k, :], a_hi[:, k, :].bitcast(F32), ALU.subtract).then_inc(a_ready, 1)

            def sample_products(x):
                if x == 0:
                    dve.wait_ge(cache_loaded, 16 * 9)
                q, kv, r = ((q_a, kv_a, P), (q_b, kv_b, ROWS_B))[x]
                step(dve.tensor_tensor(q[:], q[:], kv[:, :, 0, :], ALU.mult))
                step.settle()
                ins = dve.tensor_reduce(s_score[0:r, x, :], q[:].rearrange("p n (h d) -> p (n h) d", d=HD), AX_X, ALU.add)
                if x == 0:
                    step(ins)
                else:
                    ins.then_inc(smp_dve, 1)

            def sample_scores():
                pl = Place(T_SAMPLE)
                ps = full(pl, 6)
                step(dve.scalar_tensor_tensor(out=s_prob[:, 0:P], in0=ps[0:32, 0:P], scalar=HD ** -0.5, in1=const("bias_sa", 32),
                                              op0=ALU.mult, op1=ALU.add))
                empty(dve.scalar_tensor_tensor(out=s_prob[:, P:P + ROWS_B], in0=ps[0:32, P:P + ROWS_B], scalar=HD ** -0.5,
                                               in1=const("bias_sb", 32), op0=ALU.mult, op1=ALU.add), 6)
                dve.wait_ge(task_free[0], pl.half(6) + 1)
                dve.tensor_reduce(s_small[:, 0:1], s_prob[:], AX_X, ALU.max, negate=True).then_inc(smp_act, 1)
                dve.wait_ge(root, HEADS + 1)
                step(dve.reciprocal(s_small[:, 2:3], s_small[:, 1:2]))
                step.settle()
                dve.tensor_scalar(s_prob[:], s_prob[:], s_small[:, 2:3], None, ALU.mult).then_inc(smp_dve, 1)

            def sample_outputs():
                pl = Place(T_SAMPLE)
                for x in range(2):
                    dve.wait_ge(rows_stored[x], 16 * 9)
                ps = full(pl, 7)
                for x, r in enumerate((P, ROWS_B)):
                    own = const("eye8", r).rearrange("p (a b) -> p a b", a=SAMPLES).unsqueeze(3)
                    p = ps[0:r, 32 * x:32 * x + 32].rearrange("p (b c) -> p b c", c=AH).unsqueeze(1)
                    ins = dve.tensor_tensor(s_ptok[0:r, x].rearrange("p a (b c) -> p a b c", c=AH),
                                            p.to_broadcast([r, SAMPLES, SAMPLES, AH]),
                                            own.to_broadcast([r, SAMPLES, SAMPLES, AH]), ALU.mult)
                    if x == 0:
                        step(ins)
                empty(ins, 7)
                empty(dve.tensor_copy(s_out[:], full(pl, 8)[0:32, 0:4 * HD]), 8)
                ps = full(pl, 9)[:, 0:64].rearrange("p (a n h) -> p a n h", a=2, h=AH)
                for part in range(2):
                    for pair in range(2):
                        for e in range(2):
                            half = slice(64 * e, 64 * e + 64)
                            src, hi = ps[half, pair, :, 2 * pair + e], ao_hi[half, pair, SEQ:TOKENS]
                            if part == 0:
                                ins = dve.tensor_copy(hi, src)
                            else:
                                ins = dve.tensor_tensor(ao_lo[half, pair, SEQ:TOKENS], src, hi.bitcast(F32), ALU.subtract)
                            if (part, pair, e) != (1, 1, 1):
                                step(ins)
                    step.settle()
                empty(ins, 9)

            def merge_weights():
                dve.wait_ge(parts_loaded, 16 * GROUPS)
                low = mrg[:, 6, :].unsqueeze(2)
                minus = [parts[:, g, :, HD + 1:HD + 2] for g in range(GROUPS)]
                total = [parts[:, g, :, HD:HD + 1] for g in range(GROUPS)]
                step(dve.tensor_tensor(low, minus[0], minus[1], ALU.min))
                step.settle()
                step(dve.tensor_tensor(low, low, minus[2], ALU.min))
                step.settle()
                for g in range(GROUPS):
                    ins = dve.tensor_tensor(mrg[:, g, :].unsqueeze(2), low, minus[g], ALU.subtract)
                    if g < GROUPS - 1:
                        step(ins)
                ins.then_inc(mrg_dve, 1)
                dve.wait_ge(mrg_act, 1)
                for g in range(GROUPS):
                    step(dve.tensor_tensor(mrg[:, 3 + g, :].unsqueeze(2), mrg[:, g, :].unsqueeze(2), total[g], ALU.mult))
                step.settle()
                for g in (1, 2):
                    step(dve.tensor_tensor(mrg[:, 3, :], mrg[:, 3, :], mrg[:, 3 + g, :], ALU.add))
                    step.settle()
                step(dve.reciprocal(mrg[:, 7, :], mrg[:, 3, :]))
                step.settle()
                for g in range(GROUPS):
                    step(dve.tensor_tensor(mrg[:, g, :], mrg[:, g, :], mrg[:, 7, :], ALU.mult))
                step.settle()

            def merge_group(g):
                ao = ao_tok[:].rearrange("p t (h d) -> p (t h) d", d=HD)
                by = mrg[:, g, :].unsqueeze(2).to_broadcast([P, CHUNKS * AH, HD])
                step(dve.tensor_tensor(prod[:] if g else ao, parts[:, g, :, 0:HD], by, ALU.mult))
                step.settle()
                if g:
                    ins = dve.tensor_tensor(ao, ao, prod[:], ALU.add)
                    if g == 1:
                        step(ins)
                        step.settle()
                    else:
                        ins.then_inc(mrg_dve, 1)

            def merge_turned():
                for j in range(4):
                    ps = full(Place(T_MERGE), j)[:].rearrange("p (a t) -> p a t", a=2)
                    c = slice(2 * P * j, 2 * P * (j + 1))
                    step(dve.tensor_copy(ao_hi[:, :, c], ps))
                    step.settle()
                    empty(dve.tensor_tensor(ao_lo[:, :, c], ps, ao_hi[:, :, c].bitcast(F32), ALU.subtract), j)

            for m in range(KT):
                x = m % 2
                dve.wait_ge(gate_loaded[x], 16 * (m // 2 + 1))
                dve.tensor_tensor(pieces(wide[:, m, :]), take(Place(U_BRANCH), m), pieces(gate_r[:, x, :]), ALU.mult)\
                   .then_inc(unit_free[x], 1)
                if m == 1:
                    sample_products(0)
                    sample_products(1)
                elif m == 2:
                    sample_scores()
                    sample_outputs()
                elif m == 4:
                    merge_weights()
                    merge_group(0)
                elif m == 5:
                    merge_group(1)
                    merge_group(2)
                elif m == 6:
                    merge_turned()

            def merge_branches(pl, x, m, nth):
                ga, w = gate_a[:, x, :], flat(wide[:, ds(m, 1), :])
                dve.wait_ge(gate_a_loaded[x], nth)
                dve.tensor_tensor(pieces(ga), take(pl, x), pieces(ga), ALU.mult).then_inc(unit_free[x], 1)
                dve.wait_ge(unit_free[x], pl.half(x) + 1)
                dve.tensor_tensor(w, w, ga, ALU.add).then_inc(merged, 1)

            with dve.Fori(0, KT // 2) as i:
                for x in range(2):
                    merge_branches(Place(U_ATT, 2, i), x, i * 2 + x, i * 16 + 16)
            dve.wait_ge(b_ready, POOL_LOW)
            for m in range(POOL_LOW, KT):
                dve.wait_ge(b_high, m + 1)
                dve.tensor_tensor(b_lo[:, m, :], wide[:, m, :], b_hi[:, m, :].bitcast(F32), ALU.subtract).then_inc(b_ready, 1)

            dve.wait_ge(unit_done, U_OUT)
            dve.memset(temp[:, 3, :], 0.0).then_inc(summed, 1)
            with dve.Fori(0, KT // 2) as i:
                step.enter(i, STEPS_OUT)
                for j in range(2):
                    m = i * 2 + j
                    ps = take(Place(U_OUT, 2, i), j)
                    dve.wait_ge(x_back[j], i * 16 + 16)
                    x2 = flat(wide[:, ds(m, 1), :])
                    hi, lo = flat(a_hi[:, ds(m, 1), :]), flat(a_lo[:, ds(m, 1), :])
                    g = gains[:, 1, ds(m, 1)]
                    dve.tensor_tensor(pieces(x2), ps, pieces(temp[:, j, :]), ALU.add).then_inc(unit_free[j], 1)
                    dve.wait_ge(unit_free[j], Place(U_OUT, 2, i).half(j) + 1)
                    step(dve.tensor_scalar(hi, x2, g, None, ALU.mult))
                    step.settle()
                    dve.scalar_tensor_tensor(out=lo, in0=x2, scalar=g, in1=hi.bitcast(F32), op0=ALU.mult, op1=ALU.subtract)\
                       .then_inc(a_ready, 1)
                    dve.wait_ge(squared, m + (CHUNKS + 2))
                    dve.wait_ge(summed, m + 1)
                    dve.tensor_tensor(temp[:, 3, :], temp[:, 3, :], temp[:, 2, :], ALU.add).then_inc(summed, 1)
                step.leave(KT // 2)
            norm_factor(T_END)
            dve.wait_ge(rstd_ready, 1)

            for c, nf in enumerate(FF_CHUNKS):
                f0 = sum(FF_CHUNKS[:c])
                with dve.Fori(0, nf) as f:
                    step.enter(f, STEPS_FFN)
                    pl = Place(U_FFN_CHUNK[c], 2, f)
                    for j in range(2):
                        scaled(pl, j, temp[:, j, :])
                    dve.wait_ge(unit_free[1], pl.half(1) + 1)
                    dve.wait_ge(silu_done, f + (2 * HEADS + 2 * KT + f0 + 1))
                    step(dve.tensor_tensor(temp[:, 2, :], temp[:, 0, :], temp[:, 1, :], ALU.mult))
                    step.settle()
                    hi, lo = flat(b_hi[:, ds(f, 1), :]), flat(b_lo[:, ds(f, 1), :])
                    step(dve.tensor_copy(hi, temp[:, 2, :]))
                    step.settle()
                    dve.tensor_tensor(lo, temp[:, 2, :], hi.bitcast(F32), ALU.subtract).then_inc(b_ready, 1)
                    step.leave(nf)
                with dve.Fori(0, KT // 2) as i:
                    for j in range(2):
                        ps = take(Place(U_FFN_CHUNK[c] + 2 * nf, 2, i), j)
                        x = pieces(flat(wide[:, ds(i * 2 + j, 1), :]))
                        dve.tensor_tensor(x, ps, x, ALU.add).then_inc(unit_free[j], 1)

            dve.wait_ge(gain_loaded, 16)
            for t in range(CHUNKS + 1):
                n, g = P if t < CHUNKS else SAMPLES, t % 3
                dve.wait_ge(act_step, 2 * t + 2)
                wait(dve, y_stored[g], 16 * (t // 3))
                step(dve.reciprocal(fin[0:n, g, 1:2], fin[0:n, g, 0:1]))
                step.settle()
                ps = y_ps[g][0:n]
                dve.scalar_tensor_tensor(out=y_row[0:n, g, :].rearrange("p (a b) -> p a b", a=2), in0=ps,
                                         scalar=fin[0:n, g, 1:2], in1=gain_row[0:n, :].rearrange("p (a b) -> p a b", a=2),
                                         op0=ALU.mult, op1=ALU.mult).then_inc(y_ready, 1)


_INS = ["x_prompt", "x_sample", "state_ret", "cache_kv_w128", "cache_kv_w512", "cache_kv_w2048", "w_in",
        "w_ret_branch", "w_att_branch", "w_out", "w_gate_up", "w_down", "norm_final"]
_OUTS = [("y_prompt", (1, SEQ, D)), ("y_sample", (SAMPLES, 1, D)), ("p_ret", (1, 1, HEADS, DK, DV)),
         ("p_kv_w128", (1, 1, KEPT[0], 2, AH, HD)), ("p_kv_w512", (1, 1, KEPT[1], 2, AH, HD)),
         ("p_kv_w2048", (1, 1, KEPT[2], 2, AH, HD)), ("s_ret", (1, SAMPLES, HEADS, DK, DV)),
         ("s_kv_w128", (1, SAMPLES, 1, 2, AH, HD)), ("s_kv_w512", (1, SAMPLES, 1, 2, AH, HD)),
         ("s_kv_w2048", (1, SAMPLES, 1, 2, AH, HD))]


def kernel(**inputs):
    import concourse.bacc as bacc
    from concourse.bass_utils import run_bass_kernel_spmd

    nc = bacc.Bacc("TRN2", target_bir_lowering=False, num_devices=1)
    arrays, ins = {}, {}
    for name in _INS:
        arrays[f"in_{name}"] = np.ascontiguousarray(inputs[name])
    arrays["in_norm_gains"] = np.ascontiguousarray(
        np.stack([np.asarray(inputs[n])[0].reshape(KT, P).T for n in ("norm_mix", "norm_ffn")], 1))
    for name, table in tables().items():
        arrays[f"in_{name}"] = table
    for key, x in arrays.items():
        ins[key[3:]] = nc.dram_tensor(key, x.shape, F32, kind="ExternalInput").ap()
    outs = {name: nc.dram_tensor(f"out_{name}", shape, F32, kind="ExternalOutput").ap() for name, shape in _OUTS}
    build(nc, ins, outs)
    r = run_bass_kernel_spmd(nc, [arrays], core_ids=[0])
    return tuple(r.results[0][f"out_{name}"] for name, _ in _OUTS)
```
